# Optimizing a Trainium2 kernel written in Bass

```python
import math
import jax, jax.numpy as jnp
from jax import lax
import numpy as np

D_MODEL = 1024
BATCH = 1
SEQ = 1024
DEPTH = 1

DA_HEADS = 8
DA_HD = 64
DA_QK = DA_HEADS * 2 * DA_HD
DA_V = DA_HEADS * 2 * DA_HD
Q_BLOCK = 128
NUM_BUCKETS = 32
MAX_DISTANCE = 128
RW_HD = 64
RW_HEADS = D_MODEL // RW_HD
RW_W = RW_HEADS * RW_HD
DECAY_LORA = max(32, int(round(1.8 * D_MODEL ** 0.5 / 32)) * 32)
AAA_LORA = max(32, int(round(1.8 * D_MODEL ** 0.5 / 32)) * 32)
GATE_LORA = max(32, int(round(0.6 * D_MODEL ** 0.8 / 32)) * 32)
RW_LNX_EPS = 64e-5
RW_SHIFT_COLS = 3 * RW_W + DECAY_LORA + AAA_LORA + GATE_LORA
IN_SPLITS = (DA_QK, DA_QK, DA_V, RW_SHIFT_COLS, 2 * D_MODEL)
IN_COLS = sum(IN_SPLITS)
MEM_TOKENS = 256
CA_HEADS = 4
CA_HD = D_MODEL // CA_HEADS
D_FF = -(-8 * D_MODEL // (3 * 256)) * 256
DN_ALPHA = (2.0 * DEPTH) ** 0.25
DN_BETA = (8.0 * DEPTH) ** -0.25
LN_EPS = 1e-5

kernel_name = "hybrid_diffattn_rwkv7_gated_deepnorm"

def _split_cols(p, sizes):
    outs, off = [], 0
    for s in sizes:
        outs.append(p[..., off:off + s])
        off += s
    return outs

def _layer_norm(x, g, b, eps=LN_EPS):
    xf = x.astype(jnp.float32)
    mu = jnp.mean(xf, axis=-1, keepdims=True)
    var = jnp.mean(jnp.square(xf - mu), axis=-1, keepdims=True)
    return ((xf - mu) * lax.rsqrt(var + eps) * g + b).astype(x.dtype)

def _rms_norm(x, g, eps=LN_EPS):
    xf = x.astype(jnp.float32)
    ms = jnp.mean(jnp.square(xf), axis=-1, keepdims=True)
    return (xf * lax.rsqrt(ms + eps) * g).astype(x.dtype)

def _token_shift(p):
    return jnp.pad(p, ((0, 0), (1, 0), (0, 0)))[:, :-1]

def _t5_bucket(rel):
    n = jnp.maximum(rel, 0)
    max_exact = NUM_BUCKETS // 2
    nf = jnp.maximum(n, 1).astype(jnp.float32)
    large = max_exact + (jnp.log(nf / max_exact) / math.log(MAX_DISTANCE / max_exact)
                         * (NUM_BUCKETS - max_exact)).astype(jnp.int32)
    large = jnp.minimum(large, NUM_BUCKETS - 1)
    return jnp.where(n < max_exact, n, large)

def _diff_attention(q, k, v, lam, bias_table):
    S = q.shape[1]
    scale = DA_HD ** -0.5
    outs = []
    for i in range(S // Q_BLOCK):
        q0, kend = i * Q_BLOCK, (i + 1) * Q_BLOCK
        qb, kb, vb = q[:, q0:kend], k[:, :kend], v[:, :kend]
        rel = jnp.arange(q0, kend)[:, None] - jnp.arange(kend)[None, :]
        bias = jnp.transpose(bias_table[_t5_bucket(rel)], (2, 0, 1)).astype(jnp.float32)
        logits = jnp.einsum('bqhcd,bkhcd->bhcqk', qb, kb).astype(jnp.float32) * scale
        logits = logits + bias[None, :, None]
        logits = jnp.where((rel >= 0)[None, None, None], logits, -jnp.inf)
        p = jax.nn.softmax(logits, axis=-1)
        attn = (p[:, :, 0] - lam * p[:, :, 1]).astype(v.dtype)
        outs.append(jnp.einsum('bhqk,bkhd->bqhd', attn, vb))
    return jnp.concatenate(outs, axis=1)

def _rwkv7_recurrence(r, decay, k, v, a_vec, b_vec):
    Bn, _, H, N = r.shape

    def step(state, inp):
        r_t, w_t, k_t, v_t, a_t, b_t = inp
        sa = jnp.einsum('bhvk,bhk->bhv', state, a_t)
        state = (state * w_t[:, :, None, :] + sa[..., None] * b_t[:, :, None, :]
                 + v_t[..., None] * k_t[:, :, None, :])
        return state, jnp.einsum('bhvk,bhk->bhv', state, r_t)

    xs = tuple(jnp.moveaxis(t, 1, 0) for t in (r, decay, k, v, a_vec, b_vec))
    state0 = jnp.zeros((Bn, H, N, N), jnp.float32)
    _, ys = lax.scan(step, state0, xs)
    return jnp.moveaxis(ys, 0, 1)

def setup_inputs(seed: int = 0) -> dict:
    key = jax.random.key(seed)
    ks = iter(jax.random.split(key, 48))
    D = D_MODEL

    def nrm(shape, scale):
        return jax.random.normal(next(ks), shape, jnp.float32) * scale

    def gain(shape):
        return 1.0 + nrm(shape, 0.02)

    return {
        'x': nrm((BATCH, SEQ, D), 1.0),
        'mem': nrm((BATCH, MEM_TOKENS, D), 1.0),
        'rel_bias': nrm((NUM_BUCKETS, DA_HEADS), 0.5),
        'w_in': nrm((DEPTH, D, IN_COLS), D ** -0.5),
        'shift_mu': jax.random.uniform(next(ks), (DEPTH, RW_SHIFT_COLS), jnp.float32),
        'lambda_q1': nrm((DEPTH, DA_HD), 0.1),
        'lambda_k1': nrm((DEPTH, DA_HD), 0.1),
        'lambda_q2': nrm((DEPTH, DA_HD), 0.1),
        'lambda_k2': nrm((DEPTH, DA_HD), 0.1),
        'da_subln_g': gain((DEPTH, 2 * DA_HD)),
        'w_da_proj': nrm((DEPTH, DA_V, D), DA_V ** -0.5),
        'rw_w0': jax.random.uniform(next(ks), (DEPTH, RW_W), jnp.float32, -6.0, -1.0),
        'rw_w2': nrm((DEPTH, DECAY_LORA, RW_W), 0.1 * DECAY_LORA ** -0.5),
        'rw_a0': nrm((DEPTH, RW_W), 0.1),
        'rw_a2': nrm((DEPTH, AAA_LORA, RW_W), AAA_LORA ** -0.5),
        'rw_g2': nrm((DEPTH, GATE_LORA, RW_W), GATE_LORA ** -0.5),
        'rw_k_k': 0.85 + nrm((DEPTH, RW_W), 0.05),
        'rw_k_a': 1.0 + nrm((DEPTH, RW_W), 0.05),
        'rw_r_k': nrm((DEPTH, RW_HEADS, RW_HD), 0.1),
        'rw_lnx_g': gain((DEPTH, RW_W)),
        'rw_lnx_b': nrm((DEPTH, RW_W), 0.02),
        'w_rw_proj': nrm((DEPTH, RW_W, D), RW_W ** -0.5),
        'w_mix_out': nrm((DEPTH, D, D), DN_BETA * D ** -0.5),
        'ln1_g': gain((DEPTH, D)),
        'ln1_b': nrm((DEPTH, D), 0.02),
        'mem_ln_g': gain((DEPTH, D)),
        'mem_ln_b': nrm((DEPTH, D), 0.02),
        'w_cq': nrm((DEPTH, D, D), D ** -0.5),
        'w_ckv': nrm((DEPTH, D, 2 * D), D ** -0.5),
        'w_co': nrm((DEPTH, D, D), DN_BETA * D ** -0.5),
        'ln2_g': gain((DEPTH, D)),
        'ln2_b': nrm((DEPTH, D), 0.02),
        'w_ffn_in': nrm((DEPTH, D, 2 * D_FF), D ** -0.5),
        'w_ffn_out': nrm((DEPTH, D_FF, D), DN_BETA * D_FF ** -0.5),
        'ln3_g': gain((DEPTH, D)),
        'ln3_b': nrm((DEPTH, D), 0.02),
    }

def reference(x, mem, rel_bias, w_in, shift_mu, lambda_q1, lambda_k1, lambda_q2, lambda_k2,
              da_subln_g, w_da_proj, rw_w0, rw_w2, rw_a0, rw_a2, rw_g2, rw_k_k, rw_k_a, rw_r_k,
              rw_lnx_g, rw_lnx_b, w_rw_proj, w_mix_out, ln1_g, ln1_b, mem_ln_g, mem_ln_b,
              w_cq, w_ckv, w_co, ln2_g, ln2_b, w_ffn_in, w_ffn_out, ln3_g, ln3_b):
    f32 = jnp.float32
    B, S, D = x.shape
    M = mem.shape[1]

    def heads(t):
        return t.reshape(B, S, RW_HEADS, RW_HD)

    for l in range(DEPTH):
        proj = x @ w_in[l]
        da_q, da_k, da_v, rw_cols, gate_cols = _split_cols(proj, IN_SPLITS)

        lam_init = 0.8 - 0.6 * math.exp(-0.3 * l)
        lam = (jnp.exp(jnp.sum(lambda_q1[l].astype(f32) * lambda_k1[l].astype(f32)))
               - jnp.exp(jnp.sum(lambda_q2[l].astype(f32) * lambda_k2[l].astype(f32))) + lam_init)
        o = _diff_attention(da_q.reshape(B, S, DA_HEADS, 2, DA_HD),
                            da_k.reshape(B, S, DA_HEADS, 2, DA_HD),
                            da_v.reshape(B, S, DA_HEADS, 2 * DA_HD), lam, rel_bias)
        o = _rms_norm(o, da_subln_g[l]) * (1.0 - lam_init)
        y_da = o.reshape(B, S, DA_V) @ w_da_proj[l]

        rw_cols = rw_cols + shift_mu[l] * (_token_shift(rw_cols) - rw_cols)
        rw_r, rw_k, rw_v, rw_wd, rw_ad, rw_gd = _split_cols(
            rw_cols, (RW_W, RW_W, RW_W, DECAY_LORA, AAA_LORA, GATE_LORA))
        w_log = -jax.nn.softplus(-(rw_w0[l] + jnp.tanh(rw_wd) @ rw_w2[l]).astype(f32)) - 0.5
        decay = jnp.exp(-jnp.exp(w_log))
        a_ic = jax.nn.sigmoid((rw_a0[l] + rw_ad @ rw_a2[l]).astype(f32))
        g_out = jax.nn.sigmoid(rw_gd) @ rw_g2[l]
        kf = rw_k.astype(f32)
        kk = heads(kf * rw_k_k[l])
        kk = kk / jnp.maximum(jnp.sqrt(jnp.sum(jnp.square(kk), axis=-1, keepdims=True)), 1e-12)
        a_h = heads(a_ic)
        k_h = heads(kf * (1.0 + (a_ic - 1.0) * rw_k_a[l]))
        r_h = heads(rw_r.astype(f32))
        v_h = heads(rw_v.astype(f32))
        y = _rwkv7_recurrence(r_h, heads(decay), k_h, v_h, -kk, kk * a_h)
        mu = jnp.mean(y, axis=-1, keepdims=True)
        var = jnp.mean(jnp.square(y - mu), axis=-1, keepdims=True)
        y = ((y - mu) * lax.rsqrt(var + RW_LNX_EPS)).reshape(B, S, RW_W) * rw_lnx_g[l] + rw_lnx_b[l]
        bonus = jnp.sum(r_h * k_h * rw_r_k[l], axis=-1, keepdims=True) * v_h
        y = (y + bonus.reshape(B, S, RW_W)).astype(x.dtype)
        y_rw = (y * g_out) @ w_rw_proj[l]

        gate_a, gate_b = _split_cols(gate_cols, (D, D))
        mixed = jax.nn.sigmoid(gate_a) * y_da + jax.nn.sigmoid(gate_b) * y_rw
        x = _layer_norm(DN_ALPHA * x + mixed @ w_mix_out[l], ln1_g[l], ln1_b[l])

        m = _layer_norm(mem, mem_ln_g[l], mem_ln_b[l])
        cq = (x @ w_cq[l]).reshape(B, S, CA_HEADS, CA_HD)
        ck, cv = _split_cols(m @ w_ckv[l], (D, D))
        ck = ck.reshape(B, M, CA_HEADS, CA_HD)
        cv = cv.reshape(B, M, CA_HEADS, CA_HD)
        logits = jnp.einsum('bqhd,bmhd->bhqm', cq, ck).astype(f32) * (CA_HD ** -0.5)
        p = jax.nn.softmax(logits, axis=-1).astype(x.dtype)
        co = jnp.einsum('bhqm,bmhd->bqhd', p, cv).reshape(B, S, D) @ w_co[l]
        x = _layer_norm(DN_ALPHA * x + co, ln2_g[l], ln2_b[l])

        gate, up = _split_cols(x @ w_ffn_in[l], (D_FF, D_FF))
        f = (jax.nn.silu(gate) * up) @ w_ffn_out[l]
        x = _layer_norm(DN_ALPHA * x + f, ln3_g[l], ln3_b[l])
    return x


_drawn_inputs = setup_inputs


def setup_inputs(seed=0):
    import zlib

    import numpy as np

    out = dict(_drawn_inputs(seed))
    spreads = {}
    factors = {'lambda_q1': 8.0,
     'lambda_k1': 2.944,
     'lambda_q2': 4.278,
     'lambda_k2': 6.585,
     'da_subln_g': 8.0,
     'rw_w2': 8.0,
     'rw_a0': 8.0,
     'rw_k_k': 7.736,
     'rw_k_a': 7.048,
     'rw_lnx_g': 8.0,
     'rw_lnx_b': 8.0,
     'ln1_g': 2.791,
     'ln1_b': 2.756,
     'mem_ln_g': 8.0,
     'mem_ln_b': 25.772,
     'ln2_b': 2.787,
     'ln3_g': 8.14,
     'ln3_b': 8.394}
    for name, (base, spread) in spreads.items():
        noise = np.random.default_rng([zlib.crc32(name.encode()), seed]).standard_normal(out[name].shape)
        drawn = base * np.exp(spread * noise) if base else spread * noise
        out[name] = __import__('jax').numpy.asarray(drawn.astype(out[name].dtype))
    for name, factor in factors.items():
        out[name] = (out[name] * factor).astype(out[name].dtype)
    return out
```

```python
import math
from contextlib import ExitStack

import numpy as np

import concourse.bass as bass
from concourse import mybir

P = 128
F32 = mybir.dt.float32
ALU = mybir.AluOpType
ACT = mybir.ActivationFunctionType
AX = mybir.AxisListType.X

D = 1024
S = 1024
KT = D // P
NT = S // P
HALF = S // 2
DA_HEADS, DA_HD = 8, 64
BUCKETS, MAX_DIST = 32, 128
RW_HD = 64
PAIRS = D // P
CHUNK = 64
LORA, GATE_LORA = 64, 160
RW0 = 3 * D
LW0 = RW0 + 3 * D
LG0 = LW0 + 2 * LORA
GATE0 = LG0 + GATE_LORA
MEM = 256
CA_HEADS, CA_HD = 4, 256
FF = 2816
FT = FF // P
ALPHA = 2.0 ** 0.25
LN_EPS = 1e-5
LNX_EPS = 64e-5
LAM_INIT = 0.8 - 0.6 * math.exp(0.0)
DECAY = math.exp(-0.5)
MASKED = -1e30
NORM_SCALE = 2.0 ** 20
NORM_SHIFT = 10 * math.log(2.0)

C_IDENT, C_FLIP, C_HSUM, C_HMEAN, C_MEAN, C_STRICT, C_INCL, C_LEVEL1T = range(8)
LEVELS = (2, 4, 8, 16, 32)
C_LEVEL = 8
N_CONST = C_LEVEL + len(LEVELS)
WIN = 3 * P

PAIR_ROWS = ("mu_r", "mu_k", "mu_v", "w0", "a0", "k_k", "k_a", "r_k", "lnx_g", "lnx_b")
LN_ROWS = ("ln1_g", "ln1_b", "ln2_g", "ln2_b", "ln3_g", "ln3_b", "mem_ln_g", "mem_ln_b")
R_SUBLN, R_MUW, R_MUG, R_MUG2 = 64, 65, 66, 67


def shape_constants():
    i = np.arange(P)[:, None]
    j = np.arange(P)[None, :]
    same_head = i // RW_HD == j // RW_HD
    same_chunk = i // CHUNK == j // CHUNK
    tiles = [i == j, i + j == P - 1, same_head, same_head / RW_HD, np.full((P, P), 1.0 / D),
             same_chunk & (i < j), same_chunk & (i <= j), (i % 2 == 0) & (j == i + 1)]
    for s in LEVELS:
        tiles.append(((i // s) % 2 == 1) & (j // s == i // s - 1))
    const = np.concatenate([np.asarray(t, np.float32) for t in tiles], axis=1)
    rel = 2 * P - 1 - np.arange(WIN)
    n = np.maximum(rel, 0)
    exact = BUCKETS // 2
    nf = np.maximum(n, 1).astype(np.float32)
    large = exact + (np.log(nf / np.float32(exact)) / np.float32(math.log(MAX_DIST / exact))
                     * np.float32(BUCKETS - exact)).astype(np.int32)
    bucket = np.where(n < exact, n, np.minimum(large, BUCKETS - 1))
    pick = (np.arange(BUCKETS)[:, None] == bucket[None, :]).astype(np.float32)
    pick[BUCKETS - 1] -= 1.0
    future = np.where(rel < 0, np.float32(MASKED), np.float32(0.0))[None, :].repeat(DA_HEADS, 0)
    return const, pick, np.ascontiguousarray(future, np.float32)


class Memory:

    def __init__(self, nc, ctx):
        def sb(name, shape):
            return ctx.enter_context(nc.sbuf_tensor(name, shape, F32))

        self.PS = ctx.enter_context(nc.psum_tensor("PS", [P, 8, 512], F32))
        self.xT = sb("xT", [P, KT, S])
        self.big = sb("big", [P, 24, S])
        self.wslot = sb("wslot", [P, 4, KT, P])
        self.const = sb("const_sb", [P, N_CONST * P])
        self.tab1 = sb("tab1", [P, P])
        self.tab2 = sb("tab2", [P, P])
        self.subln = sb("subln", [P, 1])
        self.lam = sb("lam", [P, 1])
        self.neglam = sb("neglam", [P, 1])
        self.eps = sb("eps", [P, 3])
        self.lora = sb("lora", [P, S])
        self.gd1 = sb("gd1", [P, S])
        self.gd2 = sb("gd2", [32, S])
        self.bias = self.big[:, 22:24, :].rearrange("p a (h k) -> p (a h) k", k=2 * P)
        self.memT = self.big[:, 21:23, :].rearrange("p a n -> p (a n)").rearrange("p (k n) -> p k n", n=MEM)
        self.scratch = nc.dram_tensor("bias_rows", [DA_HEADS, WIN], F32, kind="Internal").ap()

    def c(self, n, count=1):
        return self.const[:, n * P:(n + count) * P]


def semaphores(nc, ctx, prefix=""):
    taken = []

    def sem(name):
        taken.append(nc.alloc_semaphore(name=prefix + name))
        return taken[-1]

    def clear():
        nc.clear_and_free_semaphores(taken)
        nc.all_engine_barrier()

    ctx.callback(clear)
    return sem


def tile_cols(w):
    return w.rearrange("(k p) n -> p k n", p=P)


def setup_phase(nc, m, d):
    xT, lora, gd1, gd2 = m.xT, m.lora, m.gd1, m.gd2
    PS, const = m.PS, m.const
    with ExitStack() as ctx:
        def sb(name, shape):
            return ctx.enter_context(nc.sbuf_tensor(name, shape, F32))

        sem = semaphores(nc, ctx)

        xin = sb("xin", [P, 2, D])
        rows1 = sb("rows1", [P, P])
        rows2 = sb("rows2", [P, P])
        wl = [sb("wl0", [P, KT, P]), sb("wl1", [P, KT, P]), sb("wl2", [P, KT, 32])]
        raw = sb("raw_lora", [P, 1 + S])
        lamv = sb("lamv", [P, 4, DA_HD])
        lprod = sb("lprod", [P, 2, DA_HD])
        lsum = sb("lsum", [P, 2])
        lexp = sb("lexp", [P, 2])
        rel = sb("rel", [BUCKETS, DA_HEADS])
        pick = sb("pick_sb", [BUCKETS, WIN])
        future = sb("future_sb", [DA_HEADS, WIN])
        frow = sb("frow", [DA_HEADS, WIN])
        grid = sb("grid", [P, DA_HEADS, 2 * P])
        diff = sb("diff", [P, S])

        const_in = sem("const_in")
        rows_zero = sem("rows_zero")
        rows_in = sem("rows_in")
        lam_in = sem("lam_in")
        rel_in = sem("rel_in")
        wl_in = [sem(f"wl_in{j}") for j in range(3)]
        x_in = [sem("x_in0"), sem("x_in1")]
        x_turned = sem("x_turned")
        x_out = [sem("x_out_dve"), sem("x_out_act")]
        tab_turned = sem("tab_turned")
        tab_out = sem("tab_out")
        lora_mm = sem("lora_mm")
        raw_out = sem("raw_out")
        raw_zero = sem("raw_zero")
        lora_out = sem("lora_out")
        lora_act = sem("lora_act")
        rel_mm = sem("rel_mm")
        frow_out = sem("frow_out")
        frow_stored = sem("frow_stored")
        grid_in = sem("grid_in")
        flip_mm = sem("flip_mm")
        bias_out = sem("bias_out")
        lam_sum = sem("lam_sum")
        lam_exp = sem("lam_exp")
        chain = sem("setup_chain")

        block = ctx.enter_context(nc.Block())
        w_in = tile_cols(d["w_in"][0])
        vec_rows = dict(zip(PAIR_ROWS, [d["shift_mu"][0, 0:D], d["shift_mu"][0, D:2 * D],
                                        d["shift_mu"][0, 2 * D:3 * D], d["rw_w0"][0], d["rw_a0"][0],
                                        d["rw_k_k"][0], d["rw_k_a"][0],
                                        d["rw_r_k"][0].rearrange("h n -> (h n)"),
                                        d["rw_lnx_g"][0], d["rw_lnx_b"][0]]))

        @block.sync
        def _(sp):
            sp.dma_start(const[:, :], d["const"]).then_inc(const_in, 16)
            for t in range(NT):
                if t >= 2:
                    sp.wait_ge(x_turned, 2 * (t - 1))
                sp.dma_start(xin[:, t % 2, :], d["x"][0, t * P:(t + 1) * P, :]).then_inc(x_in[t % 2], 16)
                if t == 1:
                    sp.dma_start(wl[0][:, :, :], w_in[:, :, LW0:LG0]).then_inc(wl_in[0], 16)
                    sp.dma_start(wl[1][:, :, :], w_in[:, :, LG0:LG0 + P]).then_inc(wl_in[1], 16)
                    sp.dma_start(wl[2][:, :, :], w_in[:, :, LG0 + P:GATE0]).then_inc(wl_in[2], 16)
            sp.wait_ge(frow_out, 1)
            sp.dma_start(m.scratch, frow[:, :]).then_inc(frow_stored, 16)
            sp.wait_ge(frow_stored, 16)
            sp.dma_start(grid[:, :, :], bass.AP(tensor=m.scratch.tensor, offset=0,
                                                ap=[[1, P], [WIN, DA_HEADS], [1, 2 * P]])).then_inc(grid_in, 16)
            sp.wait_ge(grid_in, 16)

        @block.scalar
        def _(act):
            act.wait_ge(rows_zero, 2)
            for j, name in enumerate(PAIR_ROWS):
                act.dma_start(rows1[8 * j:8 * j + 8, :],
                              vec_rows[name].rearrange("(t p) -> t p", p=P)).then_inc(rows_in, 16)
            for j, name in enumerate(LN_ROWS):
                act.dma_start(rows2[8 * j:8 * j + 8, :],
                              d[name][0].rearrange("(t p) -> t p", p=P)).then_inc(rows_in, 16)
            mu = d["shift_mu"]
            act.dma_start(rows2[R_SUBLN:R_SUBLN + 1, :], d["da_subln_g"]).then_inc(rows_in, 16)
            act.dma_start(rows2[R_MUW:R_MUW + 1, :], mu[:, 3 * D:3 * D + P]).then_inc(rows_in, 16)
            act.dma_start(rows2[R_MUG:R_MUG + 1, :], mu[:, 3 * D + P:3 * D + 2 * P]).then_inc(rows_in, 16)
            act.dma_start(rows2[R_MUG2:R_MUG2 + 1, 0:32], mu[:, 3 * D + 2 * P:]).then_inc(rows_in, 16)
            for j, name in enumerate(("lambda_q1", "lambda_k1", "lambda_q2", "lambda_k2")):
                act.dma_start(lamv[:, j, :], d[name][0].partition_broadcast(P)).then_inc(lam_in, 16)
            act.dma_start(rel[:, :], d["rel_bias"]).then_inc(rel_in, 16)
            act.dma_start(pick[:, :], d["pick"]).then_inc(rel_in, 16)
            act.dma_start(future[:, :], d["future"]).then_inc(rel_in, 16)
            for t in range(NT):
                n = 2 * t + 1
                act.wait_ge(x_turned, n + 1)
                nc.scalar.copy(xT[:, 4:8, t * P:(t + 1) * P],
                               PS[:, n % 4, :].rearrange("p (k t) -> p k t", k=4)).then_inc(x_out[1], 1)
            act.wait_ge(lam_sum, 1)
            nc.scalar.activation(lexp[:, :], lsum[:, :], ACT.Exp).then_inc(lam_exp, 1)
            act.wait_ge(lora_out, 1)
            nc.scalar.activation(lora[0:LORA, :], lora[0:LORA, :], ACT.Tanh).then_inc(lora_act, 1)
            act.wait_ge(lora_out, 2)
            nc.scalar.activation(gd1[:, :], gd1[:, :], ACT.Sigmoid).then_inc(lora_act, 1)
            act.wait_ge(lora_out, 3)
            nc.scalar.activation(gd2[0:32, :], gd2[0:32, :], ACT.Sigmoid).then_inc(lora_act, 1)
            act.wait_ge(lora_act, 3)

        @block.tensor
        def _(pe):
            pe.wait_ge(const_in, 16)
            for t in range(NT):
                pe.wait_ge(x_in[t % 2], 16 * (t // 2 + 1))
                for half in range(2):
                    n = 2 * t + half
                    if n >= 4:
                        pe.wait_ge(x_out[n % 2], (n - 4) // 2 + 1)
                    for k in range(4):
                        f = 4 * half + k
                        last = nc.tensor.transpose(PS[:, n % 4, k * P:(k + 1) * P],
                                                   xin[:, t % 2, f * P:(f + 1) * P], m.c(C_IDENT))
                    last.then_inc(x_turned, 1)
            pe.wait_ge(rows_in, 16 * (len(PAIR_ROWS) + len(LN_ROWS) + 4))
            nc.tensor.transpose(PS[:, 4, 0:P], rows1[:, :], m.c(C_IDENT))
            nc.tensor.transpose(PS[:, 4, P:2 * P], rows2[:, :], m.c(C_IDENT)).then_inc(tab_turned, 1)
            pe.wait_ge(rel_in, 48)
            nc.tensor.matmul(PS[0:DA_HEADS, 5, 0:WIN], rel[:, :], pick[:, :], start=True,
                             stop=True).then_inc(rel_mm, 1)
            pe.wait_ge(x_out[0], NT)
            pe.wait_ge(x_out[1], NT)
            for j, rows in enumerate((P, P, 32)):
                pe.wait_ge(wl_in[j], 16)
                if j:
                    pe.wait_ge(raw_out, j)
                for h in range(2):
                    for k in range(KT):
                        last = nc.tensor.matmul(PS[0:rows, 6 + h, :], wl[j][:, k, :],
                                                xT[:, k, h * HALF:(h + 1) * HALF],
                                                start=k == 0, stop=k == KT - 1)
                last.then_inc(lora_mm, 1)
            pe.wait_ge(grid_in, 16)
            for h in range(DA_HEADS):
                last = nc.tensor.matmul(PS[:, h // 2, (h % 2) * 2 * P:(h % 2 + 1) * 2 * P], m.c(C_FLIP),
                                        grid[:, h, :], start=True, stop=True)
            last.then_inc(flip_mm, 1)

        @block.vector
        def _(dve):
            v = nc.vector
            steps = [0]

            def link(ins):
                steps[0] += 1
                ins.then_inc(chain, 1)
                dve.wait_ge(chain, steps[0])

            v.memset(rows1[:, :], 0.0).then_inc(rows_zero, 1)
            v.memset(rows2[:, :], 0.0).then_inc(rows_zero, 1)
            v.memset(m.eps[:, 0:1], LN_EPS)
            v.memset(m.eps[:, 1:2], LNX_EPS)
            v.memset(m.eps[:, 2:3], NORM_SHIFT)
            link(v.memset(raw[:, 0:1], 0.0))
            for t in range(NT):
                n = 2 * t
                dve.wait_ge(x_turned, n + 1)
                v.tensor_copy(xT[:, 0:4, t * P:(t + 1) * P],
                              PS[:, n % 4, :].rearrange("p (k t) -> p k t", k=4)).then_inc(x_out[0], 1)
            dve.wait_ge(tab_turned, 1)
            link(v.tensor_copy(m.tab1[:, :], PS[:, 4, 0:P]))
            link(v.tensor_copy(m.tab2[:, :], PS[:, 4, P:2 * P]))
            link(v.tensor_scalar(m.subln[:, :], m.tab2[:, R_SUBLN:R_SUBLN + 1], 1.0 - LAM_INIT, None, ALU.mult))
            dve.wait_ge(rel_mm, 1)
            v.tensor_tensor(frow[:, :], PS[0:DA_HEADS, 5, 0:WIN], future[:, :], ALU.add).then_inc(frow_out, 1)
            dve.wait_ge(lam_in, 64)
            link(v.tensor_tensor(lprod[:, :, :], lamv[:, 0:4:2, :], lamv[:, 1:4:2, :], ALU.mult))
            v.tensor_reduce(lsum[:, :], lprod[:, :, :], AX, ALU.add).then_inc(lam_sum, 1)
            dve.wait_ge(lam_exp, 1)
            link(v.tensor_tensor(m.lam[:, :], lexp[:, 0:1], lexp[:, 1:2], ALU.subtract))
            link(v.tensor_scalar(m.neglam[:, :], m.lam[:, :], LAM_INIT, -1.0, ALU.add, ALU.mult))
            for j, (dst, rows, row) in enumerate(((lora, P, R_MUW), (gd1, P, R_MUG), (gd2, 32, R_MUG2))):
                dve.wait_ge(lora_mm, j + 1)
                v.tensor_copy(raw[0:rows, 1:1 + HALF], PS[0:rows, 6, :])
                last = v.tensor_copy(raw[0:rows, 1 + HALF:1 + S], PS[0:rows, 7, :])
                last.then_inc(raw_out, 1)
                dve.wait_ge(raw_out, j + 1)
                link(v.tensor_tensor(diff[0:rows, :], raw[0:rows, 0:S], raw[0:rows, 1:1 + S], ALU.subtract))
                v.scalar_tensor_tensor(out=dst[0:rows, :], in0=diff[0:rows, :],
                                       scalar=m.tab2[0:rows, row:row + 1], in1=raw[0:rows, 1:1 + S],
                                       op0=ALU.mult, op1=ALU.add).then_inc(lora_out, 1)
                dve.wait_ge(lora_out, j + 1)
            dve.wait_ge(flip_mm, 1)
            for b in range(4):
                last = v.tensor_copy(m.bias[:, 2 * b:2 * b + 2, :],
                                     PS[:, b, :].rearrange("p (h k) -> p h k", h=2))
            link(last)


def attention_phase(nc, m, d):
    PS, big, W = m.PS, m.big, m.wslot
    nxt = [big[:, 8 + j, :] for j in range(3)]
    qT, kT = big[:, 11, :], big[:, 12, :]
    vtok = big[:, 13, :].rearrange("p (t c) -> p t c", c=P)
    prob = big[:, 14:16, :]
    attn = big[:, 16:18, :]
    attnT = big[:, 18:20, :]
    NQ = NT
    ring = []
    for qb in range(NQ):
        ring += [("T", qb, g) for g in range(qb // 4 + 1)]
        if qb:
            ring.append(("O", qb - 1, 0))
        ring.append(("V", qb, 0))
    ring.append(("O", NQ - 1, 0))
    place = {r: n for n, r in enumerate(ring)}
    N_RING = len(ring)
    assert N_RING % 2 == 0
    act_before = [sum(r[0] != "V" for r in ring[:n + 1]) for n in range(N_RING)]
    dve_before = [sum(r[0] == "V" for r in ring[:n + 1]) for n in range(N_RING)]
    PARTS = [(0, 1), (2, 3), (4, 5), (6, 7), (8,), (9,), (10,), (11,)]

    with ExitStack() as ctx:
        sem = semaphores(nc, ctx)

        small = ctx.enter_context(nc.sbuf_tensor("attn_small", [P, 12], F32))
        onorm = ctx.enter_context(nc.sbuf_tensor("onorm", [P, 2, P], F32))
        ojunk = ctx.enter_context(nc.sbuf_tensor("ojunk", [P, P], F32))
        nmax, lsum, rl = small[:, 0:2], small[:, 2:4], small[:, 4:6]
        ssq, lnv, rstd = small[:, 6:7], small[:, 7:8], small[:, 8:9]

        w_in = [sem(f"a_w_in{j}") for j in range(3)]
        proj_done = [sem("a_proj_lo"), sem("a_proj_hi")]
        proj_out = [sem("a_proj_out_dve"), sem("a_proj_out_act")]
        q_cur, k_cur = sem("q_cur"), sem("k_cur")
        v_turned, vtok_out = sem("v_turned"), sem("vtok_out")
        scores = sem("scores_ready")
        maxed = sem("max_ready")
        exped = sem("exp_ready")
        combined = sem("attn_ready")
        ring_full = sem("ring_full")
        ring_act, ring_dve = sem("ring_emptied_act"), sem("ring_emptied_dve")
        rstd_ready = sem("rstd_ready")
        dchain, achain = sem("a_dve_chain"), sem("a_act_chain")

        block = ctx.enter_context(nc.Block())
        wv = tile_cols(d["w_in"][0])

        @block.sync
        def _(sp):
            for j in range(3):
                sp.dma_start(W[:, j, :, :], wv[:, :, j * D:j * D + P]).then_inc(w_in[j], 16)
            with sp.Fori(0, DA_HEADS - 1) as i:
                for j in range(3):
                    sp.wait_ge(proj_done[1], 3 * i + (j + 1))
                    sp.dma_start(W[:, j, :, :],
                                 wv[:, :, bass.ds(i * P + (j * D + P), P)]).then_inc(w_in[j], 16)

        def project_part(pe, n, part):
            j, half, ks = part // 4, part // 2 % 2, part % 2
            if ks == 0:
                if half == 0:
                    pe.wait_ge(w_in[j], 16 * n + 16)
                pe.wait_ge(proj_out[half], 3 * n + j)
            for k in range(4 * ks, 4 * ks + 4):
                last = nc.tensor.matmul(PS[:, 6 + half, :], W[:, j, k, :],
                                        m.xT[:, k, half * HALF:(half + 1) * HALF],
                                        start=k == 0, stop=k == KT - 1)
            if ks == 1:
                last.then_inc(proj_done[half], 1)

        def copy_projection(eng, copy, n, j, half):
            eng.wait_ge(proj_done[half], 3 * n + j + 1)
            if j < 2:
                eng.wait_ge((q_cur, k_cur)[j], n)
            else:
                eng.wait_ge(v_turned, 2 * n)
            copy(nxt[j][:, half * HALF:(half + 1) * HALF], PS[:, 6 + half, :]).then_inc(proj_out[half], 1)

        def tensor_turn(pe, i, more):
            def width(qb):
                return (qb + 1) * P

            def score(qb):
                pe.wait_ge(exped, 16 * i + 2 * qb)
                for c in range(2):
                    for n0 in range(0, width(qb), 512):
                        w = min(512, width(qb) - n0)
                        last = nc.tensor.matmul(PS[:, 2 * c + n0 // 512, 0:w],
                                                qT[64 * c:64 * c + 64, qb * P:(qb + 1) * P],
                                                kT[64 * c:64 * c + 64, n0:n0 + w], start=True, stop=True)
                    last.then_inc(scores, 1)

            def ring_slot(r, act=0, dve=0):
                n = place[r]
                if n >= 2:
                    act, dve = max(act, act_before[n - 2]), max(dve, dve_before[n - 2])
                pe.wait_ge(ring_act, act_before[-1] * i + act)
                pe.wait_ge(ring_dve, dve_before[-1] * i + dve)
                return 4 + n % 2

            def turn_output(qb):
                bank = ring_slot(("O", qb, 0), dve=qb + 1)
                nc.tensor.transpose(PS[:, bank, 0:P], onorm[:, qb % 2, :], m.c(C_IDENT)).then_inc(ring_full, 1)

            pe.wait_ge(proj_out[0], 3 * i + 3)
            pe.wait_ge(proj_out[1], 3 * i + 3)
            for g in range(2):
                if g == 0:
                    pe.wait_ge(ring_act, act_before[-1] * i)
                for t in range(4):
                    last = nc.tensor.transpose(PS[:, 4 + g, t * P:(t + 1) * P],
                                               nxt[2][:, (4 * g + t) * P:(4 * g + t + 1) * P], m.c(C_IDENT))
                last.then_inc(v_turned, 1)
            pe.wait_ge(q_cur, i + 1)
            pe.wait_ge(k_cur, i + 1)
            score(0)
            pe.wait_ge(vtok_out, 2 * i + 2)
            for qb in range(NQ):
                if qb + 1 < NQ:
                    score(qb + 1)
                if more:
                    for part in PARTS[qb]:
                        project_part(pe, i + 1, part)
                pe.wait_ge(combined, NQ * i + qb + 1)
                for g in range(qb // 4 + 1):
                    bank = ring_slot(("T", qb, g))
                    for t in range(4 * g, min(4 * g + 4, qb + 1)):
                        last = nc.tensor.transpose(PS[:, bank, (t % 4) * P:(t % 4 + 1) * P],
                                                   attn[:, qb % 2, t * P:(t + 1) * P], m.c(C_IDENT))
                    last.then_inc(ring_full, 1)
                if qb:
                    turn_output(qb - 1)
                bank = ring_slot(("V", qb, 0), act=act_before[place[("T", qb, qb // 4)]])
                for t in range(qb + 1):
                    last = nc.tensor.matmul(PS[:, bank, 0:P], attnT[:, qb % 2, t * P:(t + 1) * P],
                                            vtok[:, t, :], start=t == 0, stop=t == qb)
                last.then_inc(ring_full, 1)
            turn_output(NQ - 1)

        def scalar_turn(act, i, more):
            def expo(qb):
                w = (qb + 1) * P
                for c in range(2):
                    act.wait_ge(maxed, 16 * i + 2 * qb + c + 1)
                    act.wait_ge(combined, NQ * i + qb)
                    nc.scalar.activation(prob[:, c, 0:w], PS[:, 2 * c:2 * c + 2, :].rearrange("p b n -> p (b n)")[:, 0:w],
                                         ACT.Exp, bias=nmax[:, c:c + 1],
                                         accum_out=lsum[:, c:c + 1]).then_inc(exped, 1)

            def output_out(qb):
                n = place[("O", qb, 0)]
                act.wait_ge(ring_full, N_RING * i + n + 1)
                nc.scalar.activation(big[:, bass.ds(i, 1), qb * P:(qb + 1) * P], PS[:, 4 + n % 2:5 + n % 2, 0:P],
                                     ACT.Copy, scale=m.subln[:, 0:1]).then_inc(ring_act, 1)

            act.wait_ge(proj_out[0], 3 * i + 3)
            act.wait_ge(proj_out[1], 3 * i + 3)
            nc.scalar.mul(qT[:, :], nxt[0][:, :], DA_HD ** -0.5).then_inc(q_cur, 1)
            for g in range(2):
                act.wait_ge(v_turned, 2 * i + g + 1)
                nc.scalar.copy(vtok[:, 4 * g:4 * g + 4, :].rearrange("p t c -> p (t c)"),
                               PS[:, 4 + g, :]).then_inc(vtok_out, 1)
            expo(0)
            for qb in range(NQ):
                for g in range(qb // 4 + 1):
                    n = place[("T", qb, g)]
                    act.wait_ge(ring_full, N_RING * i + n + 1)
                    t1 = min(4 * g + 4, qb + 1)
                    nc.scalar.copy(attnT[:, qb % 2, 4 * g * P:t1 * P],
                                   PS[:, 4 + n % 2, 0:(t1 - 4 * g) * P]).then_inc(ring_act, 1)
                if qb:
                    output_out(qb - 1)
                if qb + 1 < NQ:
                    expo(qb + 1)
                n = place[("V", qb, 0)]
                act.wait_ge(ring_full, N_RING * i + n + 1)
                act.wait_ge(ring_dve, dve_before[-1] * i + qb)
                nc.scalar.activation(ojunk[:, :], PS[:, 4 + n % 2, 0:P], ACT.Square,
                                     accum_out=ssq).then_inc(achain, 1)
                act.wait_ge(achain, 2 * NQ * i + 2 * qb + 1)
                nc.scalar.activation(lnv, ssq, ACT.Ln, bias=m.eps[:, 0:1], scale=1.0 / P).then_inc(achain, 1)
                act.wait_ge(achain, 2 * NQ * i + 2 * qb + 2)
                nc.scalar.activation(rstd, lnv, ACT.Exp, scale=-0.5).then_inc(rstd_ready, 1)
                if more:
                    for part in PARTS[qb]:
                        if part % 4 == 3:
                            copy_projection(act, nc.scalar.copy, i + 1, part // 4, 1)
            output_out(NQ - 1)

        def vector_turn(dve, i, more):
            v = nc.vector
            links = 3 * NQ + 2 * NQ
            done = [0]

            def link(ins):
                done[0] += 1
                ins.then_inc(dchain, 1)
                dve.wait_ge(dchain, links * i + done[0])

            def rowmax(qb):
                w = (qb + 1) * P
                wb = min(w, 2 * P)
                for c in range(2):
                    flat = PS[:, 2 * c:2 * c + 2, :].rearrange("p b n -> p (b n)")
                    dve.wait_ge(scores, 16 * i + 2 * qb + c + 1)
                    link(v.tensor_tensor(flat[:, w - wb:w], flat[:, w - wb:w],
                                         m.bias[:, bass.ds(i, 1), 2 * P - wb:2 * P].rearrange("p a n -> p (a n)"),
                                         ALU.add))
                    dve.wait_ge(exped, 16 * i + 2 * qb + c)
                    v.tensor_reduce(nmax[:, c:c + 1], flat[:, 0:w], AX, ALU.max,
                                    negate=True).then_inc(maxed, 1)

            dve.wait_ge(proj_out[0], 3 * i + 3)
            dve.wait_ge(proj_out[1], 3 * i + 3)
            v.tensor_copy(kT[:, :], nxt[1][:, :]).then_inc(k_cur, 1)
            rowmax(0)
            for qb in range(NQ):
                w = (qb + 1) * P
                dve.wait_ge(exped, 16 * i + 2 * qb + 2)
                link(v.reciprocal(rl, lsum))
                link(v.tensor_tensor(rl[:, 1:2], rl[:, 1:2], m.neglam[:, :], ALU.mult))
                link(v.tensor_scalar(prob[:, 1, 0:w], prob[:, 1, 0:w], rl[:, 1:2], None, ALU.mult))
                if qb >= 2:
                    dve.wait_ge(ring_full, N_RING * i + place[("T", qb - 2, (qb - 2) // 4)] + 1)
                v.scalar_tensor_tensor(out=attn[:, qb % 2, 0:w], in0=prob[:, 0, 0:w], scalar=rl[:, 0:1],
                                       in1=prob[:, 1, 0:w], op0=ALU.mult, op1=ALU.add).then_inc(combined, 1)
                if qb + 1 < NQ:
                    rowmax(qb + 1)
                n = place[("V", qb, 0)]
                dve.wait_ge(rstd_ready, NQ * i + qb + 1)
                if qb >= 2:
                    dve.wait_ge(ring_full, N_RING * i + place[("O", qb - 2, 0)] + 1)
                v.tensor_scalar(onorm[:, qb % 2, :], PS[:, 4 + n % 2, 0:P], rstd, None,
                                ALU.mult).then_inc(ring_dve, 1)
                if more:
                    for part in PARTS[qb]:
                        if part % 4 == 1:
                            copy_projection(dve, v.tensor_copy, i + 1, part // 4, 0)

        @block.tensor
        def _(pe):
            for part in range(12):
                project_part(pe, 0, part)
            with pe.Fori(0, DA_HEADS - 1) as i:
                tensor_turn(pe, i, True)
            tensor_turn(pe, DA_HEADS - 1, False)

        @block.scalar
        def _(act):
            nc.scalar.preload_act_table_set("natural_log_exp_and_others")
            for j in range(3):
                copy_projection(act, nc.scalar.copy, 0, j, 1)
            with act.Fori(0, DA_HEADS - 1) as i:
                scalar_turn(act, i, True)
            scalar_turn(act, DA_HEADS - 1, False)

        @block.vector
        def _(dve):
            for j in range(3):
                copy_projection(dve, nc.vector.tensor_copy, 0, j, 0)
            with dve.Fori(0, DA_HEADS - 1) as i:
                vector_turn(dve, i, True)
            vector_turn(dve, DA_HEADS - 1, False)


def rwkv_phase(nc, m, d):
    PS, big, W = m.PS, m.big, m.wslot
    G = NT // 2
    with ExitStack() as ctx:
        def sb(name, shape):
            return ctx.enter_context(nc.sbuf_tensor(name, shape, F32))

        sem = semaphores(nc, ctx)

        nxt = [sb(f"raw{j}", [P, 1 + S]) for j in range(3)]
        AR = big[:, 16:18, :].rearrange("p a n -> p (a n)").rearrange("p (t w n) -> p t w n", t=NT, w=2)
        Bt, Kt, V, bon = (big[:, 18 + j, :] for j in range(4))
        work = big[:, 22:24, :].rearrange("p a n -> p (a n)")
        more_work = sb("rw_work", [P, 5, HALF])
        t_r, t_k, t_s, t_a = (work[:, j * HALF:(j + 1) * HALF] for j in range(4))
        t_ip, t_q, t_n, t_d = (more_work[:, j, :] for j in range(4))
        t_p = sb("running_decay", [P, HALF // CHUNK, CHUNK + 1])
        MT = work.rearrange("p (i n) -> p i n", i=4)
        T, TT, X = (more_work[:, j, :] for j in range(3))
        Tq = more_work[:, 3, 0:4 * RW_HD]
        WT = more_work[:, 4, 0:2 * P].rearrange("p (l n) -> p l n", l=2)
        tok = sb("tok", [P, 2, 4, P])
        U = sb("U", [P, 2, RW_HD])
        H = sb("state", [P, 4, RW_HD])
        HP = sb("state_decayed", [P, RW_HD])
        pend = sb("chunk_decay", [P, S // CHUNK])
        reset = sb("reset", [P, HALF])
        cur = sb("cur_params", [P, len(PAIR_ROWS)])
        negkk = sb("neg_k_k", [P, 1])
        lup = sb("lora_up", [P, 3, P])
        par = {name: cur[:, j:j + 1] for j, name in enumerate(PAIR_ROWS)}

        w_in = [sem(f"r_w_in{j}") for j in range(3)]
        lup_in = sem("lup_in")
        proj_done = [sem("r_proj_lo"), sem("r_proj_hi")]
        proj_out = [sem("r_proj_out_dve"), sem("r_proj_out_act")]
        passed = sem("pe_passed_wait")
        preset, ones_set = sem("preset"), sem("ones_set")
        cur_ready, raw_used = sem("cur_ready"), sem("raw_used")
        lora_mm, sig_ready = sem("r_lora_mm"), sem("sig_ready")
        k_mixed, k_squared, ksum_mm = sem("k_mixed"), sem("k_squared"), sem("ksum_mm")
        scanned, decay_ready = sem("scanned"), sem("decay_ready")
        clamped, rinv_ready = sem("clamped"), sem("rinv_ready")
        rk_ready, bonus_mm = sem("rk_ready"), sem("bonus_mm")
        feat_ready = sem("feat_ready")
        chain, achain = sem("r_dve_chain"), sem("r_act_chain")
        tok_turned, tok_out = sem("tok_turned"), sem("tok_out")
        mt_mm, mt_out = sem("mt_mm"), sem("mt_out")
        tt_first, t_turned, t_out = sem("tt_first"), sem("t_turned"), sem("t_out")
        x_mm, x_out = sem("x_mm"), sem("x_out")
        tn_mm, tn_out = sem("tn_mm"), sem("tn_out")
        ttn_mm, ttn_out = sem("ttn_mm"), sem("ttn_out")
        q_mm, q_out, wt_mm, wt_out = sem("q_mm"), sem("q_out"), sem("wt_mm"), sem("wt_out")
        u_mm, u_out, h_mm, h_out = sem("u_mm"), sem("u_out"), sem("h_mm"), sem("h_out")
        y_mm, y_out = sem("y_mm"), sem("y_out")
        mean_mm, centered, squared = sem("mean_mm"), sem("centered"), sem("squared")
        var_mm, rstd_ready = sem("var_mm"), sem("lnx_rstd")
        gate_mm, pair_done = sem("gate_mm"), sem("pair_done")
        NL, NC = len(LEVELS), S // CHUNK

        block = ctx.enter_context(nc.Block())
        wv = tile_cols(d["w_in"][0])

        @block.sync
        def _(sp):
            def load_lora_up(i):
                sp.wait_ge(gate_mm, 2 * i)
                sp.dma_start(lup[0:LORA, 0, :], d["rw_w2"][0, :, bass.ds(i * P, P)]).then_inc(lup_in, 16)
                sp.dma_start(lup[LORA:P, 0, :], d["rw_a2"][0, :, bass.ds(i * P, P)]).then_inc(lup_in, 16)
                sp.dma_start(lup[:, 1, :], d["rw_g2"][0, 0:P, bass.ds(i * P, P)]).then_inc(lup_in, 16)
                sp.dma_start(lup[0:32, 2, :], d["rw_g2"][0, P:GATE_LORA, bass.ds(i * P, P)]).then_inc(lup_in, 16)

            for j in range(3):
                sp.dma_start(W[:, j, :, :], wv[:, :, RW0 + j * D:RW0 + j * D + P]).then_inc(w_in[j], 16)
            with sp.Fori(0, PAIRS - 1) as i:
                load_lora_up(i)
                for j in range(3):
                    sp.wait_ge(proj_done[1], 3 * i + (j + 1))
                    sp.dma_start(W[:, j, :, :],
                                 wv[:, :, bass.ds(i * P + (RW0 + j * D + P), P)]).then_inc(w_in[j], 16)
            load_lora_up(PAIRS - 1)

        def products(pe, n, first, count):
            for p in range(first, first + count):
                j, half, k = p // 16, p // 8 % 2, p % 8
                if k == 0:
                    if half == 0:
                        pe.wait_ge(w_in[j], 16 * n + 16)
                    pe.wait_ge(proj_out[half], 3 * n + j)
                last = nc.tensor.matmul(PS[:, half, :], W[:, j, k, :],
                                        m.xT[:, k, half * HALF:(half + 1) * HALF],
                                        start=k == 0, stop=k == KT - 1)
                if k == KT - 1:
                    last.then_inc(proj_done[half], 1)

        def copy_projection(eng, copy, n, j, half):
            eng.wait_ge(proj_done[half], 3 * n + j + 1)
            eng.wait_ge(raw_used, n)
            copy(nxt[j][:, 1 + half * HALF:1 + (half + 1) * HALF], PS[:, half, :]).then_inc(proj_out[half], 1)

        E_PRODUCTS, G_PRODUCTS = 16, 8

        def tensor_turn(pe, i, more):
            mm = nc.tensor.matmul

            def wait_apart(sem, value):
                pe.wait_ge(sem, value)
                pe.sem_inc(passed, 1)

            def fill(first, count):
                if more:
                    products(pe, i + 1, first, count)

            pe.wait_ge(lup_in, 64 * i + 64)
            for hh in range(2):
                tk = slice(hh * HALF, (hh + 1) * HALF)
                if hh == 0:
                    pe.wait_ge(pair_done, 2 * i)
                else:
                    pe.wait_ge(sig_ready, 2 * i + 1)
                mm(PS[:, 2, :], lup[0:LORA, 0, :], m.lora[0:LORA, tk], start=True, stop=True)
                mm(PS[:, 3, :], lup[LORA:P, 0, :], m.lora[LORA:P, tk], start=True,
                   stop=True).then_inc(lora_mm, 1)
                fill(8 * hh, 4)
                pe.wait_ge(k_squared, 2 * i + hh + 1)
                if hh:
                    pe.wait_ge(clamped, 2 * i + 1)
                mm(PS[:, 4, :], m.c(C_HSUM), t_q, start=True, stop=True).then_inc(ksum_mm, 1)
                fill(8 * hh + 4, 4)
                pe.wait_ge(rk_ready, 2 * i + hh + 1)
                if hh:
                    pe.wait_ge(feat_ready, 2 * i + 1)
                mm(PS[:, 5, :], m.c(C_HSUM), t_d, start=True, stop=True).then_inc(bonus_mm, 1)
            for g in range(G):
                n = G * i + g
                p0 = E_PRODUCTS + G_PRODUCTS * g
                if g == 0:
                    pe.wait_ge(feat_ready, 2 * i + 2)
                else:
                    pe.wait_ge(q_out, n)
                    pe.wait_ge(wt_out, n)
                for l in range(2):
                    t = 2 * g + l
                    for a, src in enumerate((AR[:, t, 0, :], Bt[:, t * P:(t + 1) * P],
                                             Kt[:, t * P:(t + 1) * P], V[:, t * P:(t + 1) * P])):
                        last = nc.tensor.transpose(PS[:, 2 + l, a * P:(a + 1) * P], src, m.c(C_IDENT))
                    last.then_inc(tok_turned, 1)
                if g:
                    pe.wait_ge(y_out, 2 * n)
                    pe.wait_ge(h_out, 4 * n)
                    pe.wait_ge(u_out, 4 * n)
                for l in range(2):
                    t = 2 * g + l
                    for h in range(2):
                        rows = slice(64 * h, 64 * h + 64)
                        mm(PS[:, 4 + 2 * l + h, 0:2 * P], Bt[rows, t * P:(t + 1) * P], AR[rows, t, :, :],
                           start=True, stop=True)
                        mm(PS[:, 4 + 2 * l + h, 2 * P:4 * P], Kt[rows, t * P:(t + 1) * P], AR[rows, t, :, :],
                           start=True, stop=True).then_inc(mt_mm, 1)
                fill(p0, 1)
                pe.wait_ge(tt_first, n + 1)
                pe.wait_ge(tok_out, 2 * n + 1)
                for q in range(4):
                    last = nc.tensor.transpose(PS[:, 2, q * P:(q + 1) * P], TT[:, q * P:(q + 1) * P],
                                               m.c(C_IDENT))
                last.then_inc(t_turned, 1)
                fill(p0 + 1, 1)
                pe.wait_ge(t_out, n + 1)
                for lv in range(NL):
                    if lv == 0:
                        pe.wait_ge(tok_out, 2 * n + 2)
                    else:
                        pe.wait_ge(tn_out, (NL - 1) * n + lv)
                        pe.wait_ge(ttn_out, NL * n + lv)
                    for q in range(4):
                        last = mm(PS[:, 3, q * P:(q + 1) * P], MT[:, q, 0:P], T[:, q * P:(q + 1) * P],
                                  start=True, stop=True)
                    last.then_inc(x_mm, 1)
                    fill(p0 + 2 + lv, 1)
                    pe.wait_ge(x_out, NL * n + lv + 1)
                    if lv < NL - 1:
                        for q in range(4):
                            c = slice(q * P, (q + 1) * P)
                            last = mm(PS[:, 4, c], TT[:, c], X[:, c], start=True, stop=True)
                        last.then_inc(tn_mm, 1)
                    for q in range(4):
                        c = slice(q * P, (q + 1) * P)
                        last = mm(PS[:, 5, c], X[:, c], TT[:, c], start=True, stop=True)
                    last.then_inc(ttn_mm, 1)
                for q in range(4):
                    last = mm(PS[:, 2, q * RW_HD:(q + 1) * RW_HD], MT[:, q, 2 * P:3 * P],
                              tok[:, q // 2, 3, q % 2 * 64:q % 2 * 64 + 64], start=True, stop=True)
                last.then_inc(q_mm, 1)
                pe.wait_ge(ttn_out, NL * n + NL)
                for q in range(4):
                    l, h = q // 2, q % 2
                    last = mm(PS[64 * h:64 * h + 64, 3, l * P:(l + 1) * P], tok[:, l, 0, 64 * h:64 * h + 64],
                              TT[:, q * P:(q + 1) * P], start=True, stop=True)
                last.then_inc(wt_mm, 1)
                fill(p0 + 7, 1)
                pe.wait_ge(q_out, n + 1)
                pe.wait_ge(wt_out, n + 1)
                for l in range(2):
                    t = 2 * g + l
                    if l:
                        pe.wait_ge(u_out, 4 * n + 2)
                    for h in range(2):
                        q = 2 * l + h
                        mm(PS[:, 6 + h, 0:RW_HD], TT[:, q * P:(q + 1) * P], Tq[:, q * RW_HD:(q + 1) * RW_HD],
                           start=True, stop=False, skip_group_check=True)
                    for cc in range(2):
                        c = 2 * t + cc
                        rows = slice(64 * cc, 64 * cc + 64)
                        wait_apart(h_out, NC * i + c)
                        for h in range(2):
                            hr = slice(64 * h, 64 * h + 64)
                            last = mm(PS[rows, 6 + h, 0:RW_HD], WT[hr, l, 64 * cc:64 * cc + 64], H[hr, c % 4, :],
                                      start=False, stop=True, skip_group_check=True)
                        last.then_inc(u_mm, 1)
                        for h in range(2):
                            hr = slice(64 * h, 64 * h + 64)
                            mm(PS[hr, 5, 0:RW_HD], tok[rows, l, 2, hr], tok[rows, l, 3, hr],
                               start=True, stop=False, skip_group_check=True)
                        wait_apart(u_out, NC * i + c + 1)
                        for h in range(2):
                            hr = slice(64 * h, 64 * h + 64)
                            last = mm(PS[hr, 5, 0:RW_HD], tok[rows, l, 1, hr], U[rows, h, :],
                                      start=False, stop=True, skip_group_check=True)
                        last.then_inc(h_mm, 1)
                    if t:
                        pe.wait_ge(y_out, NT * i + t)
                    for h in range(2):
                        q = 2 * l + h
                        hr = slice(64 * h, 64 * h + 64)
                        mm(PS[hr, 4, 0:P], U[:, h, :], MT[:, q, P:2 * P], start=True, stop=False,
                           skip_group_check=True)
                        mm(PS[hr, 4, 0:P], tok[:, l, 3, hr], MT[:, q, 3 * P:4 * P], start=False, stop=False,
                           skip_group_check=True)
                        for cc in range(2):
                            last = mm(PS[hr, 4, 64 * cc:64 * cc + 64], H[hr, (2 * t + cc) % 4, :],
                                      AR[hr, t, 1, 64 * cc:64 * cc + 64], start=False, stop=True,
                                      skip_group_check=True)
                    last.then_inc(y_mm, 1)
            pe.wait_ge(y_out, NT * i + NT)
            for hh in range(2):
                mm(PS[:, 2 + hh, :], m.c(C_HMEAN), AR[:, 4 * hh:4 * hh + 4, 0, :], start=True,
                   stop=True).then_inc(mean_mm, 1)
            for hh in range(2):
                tk = slice(hh * HALF, (hh + 1) * HALF)
                mm(PS[:, 6 + hh, :], lup[:, 1, :], m.gd1[:, tk], start=True, stop=False)
                mm(PS[:, 6 + hh, :], lup[0:32, 2, :], m.gd2[0:32, tk], start=False,
                   stop=True).then_inc(gate_mm, 1)
            pe.wait_ge(h_out, NC * i + NC)
            for hh in range(2):
                pe.wait_ge(squared, 2 * i + hh + 1)
                mm(PS[:, 4 + hh, :], m.c(C_HMEAN), work[:, (2 + hh) * HALF:(3 + hh) * HALF], start=True,
                   stop=True).then_inc(var_mm, 1)

        def scalar_turn(act, i, more):
            a = nc.scalar
            chained = 2 + 2
            act.wait_ge(cur_ready, i + 1)
            for hh in range(2):
                act.wait_ge(lora_mm, 2 * i + hh + 1)
                if hh:
                    act.wait_ge(feat_ready, 2 * i + 1)
                a.activation(t_n, PS[:, 2, :], ACT.Sigmoid, bias=par["w0"])
                a.activation(t_a, PS[:, 3, :], ACT.Sigmoid, bias=par["a0"]).then_inc(sig_ready, 1)
                act.wait_ge(k_mixed, 2 * i + hh + 1)
                a.activation(t_q, t_k, ACT.Square, scale=par["k_k"]).then_inc(k_squared, 1)
                a.preload_act_table_set("natural_log_exp_and_others")
                act.wait_ge(scanned, 2 * i + hh + 1)
                a.activation(t_p[:, :, 1:1 + CHUNK], t_s.rearrange("p (c n) -> p c n", n=CHUNK), ACT.Exp,
                             scale=-DECAY)
                a.activation(t_ip, t_s, ACT.Exp, scale=DECAY).then_inc(decay_ready, 1)
                act.wait_ge(clamped, 2 * i + hh + 1)
                a.activation(t_n, t_n, ACT.Ln, scale=NORM_SCALE).then_inc(achain, 1)
                act.wait_ge(achain, chained * i + hh + 1)
                a.activation(t_n, t_n, ACT.Exp, scale=-0.5, bias=m.eps[:, 2:3]).then_inc(rinv_ready, 1)
            if more:
                copy_projection(act, a.copy, i + 1, 0, 1)
            for g in range(G):
                n = G * i + g
                if more and g == 2:
                    copy_projection(act, a.copy, i + 1, 1, 1)
                for l in range(2):
                    act.wait_ge(tok_turned, 2 * n + l + 1)
                    if l == 0:
                        act.wait_ge(y_mm, 2 * n)
                    a.copy(tok[:, l, :, :].rearrange("p a n -> p (a n)"), PS[:, 2 + l, :]).then_inc(tok_out, 1)
                act.wait_ge(t_turned, n + 1)
                a.copy(T, PS[:, 2, :]).then_inc(t_out, 1)
                act.wait_ge(q_mm, n + 1)
                a.copy(Tq, PS[:, 2, 0:4 * RW_HD]).then_inc(q_out, 1)
                act.wait_ge(wt_mm, n + 1)
                a.copy(WT.rearrange("p l n -> p (l n)"), PS[:, 3, 0:2 * P]).then_inc(wt_out, 1)
                for l in range(2):
                    t = 2 * g + l
                    for cc in range(2):
                        rows = slice(64 * cc, 64 * cc + 64)
                        act.wait_ge(u_mm, NC * i + 2 * t + cc + 1)
                        if cc == 0:
                            act.wait_ge(y_mm, NT * i + t)
                        a.copy(U[rows, :, :], PS[rows, 6:8, 0:RW_HD]).then_inc(u_out, 1)
                    act.wait_ge(y_mm, NT * i + t + 1)
                    a.copy(AR[:, t, 0, :], PS[:, 4, 0:P]).then_inc(y_out, 1)
            if more:
                copy_projection(act, a.copy, i + 1, 2, 1)
            for hh in range(2):
                act.wait_ge(centered, 2 * i + hh + 1)
                a.activation(work[:, (2 + hh) * HALF:(3 + hh) * HALF], work[:, hh * HALF:(hh + 1) * HALF],
                             ACT.Square).then_inc(squared, 1)
            for hh in range(2):
                r = work[:, (2 + hh) * HALF:(3 + hh) * HALF]
                act.wait_ge(var_mm, 2 * i + hh + 1)
                a.activation(r, PS[:, 4 + hh, :], ACT.Ln, bias=m.eps[:, 1:2]).then_inc(achain, 1)
                act.wait_ge(achain, chained * i + 2 + hh + 1)
                a.activation(r, r, ACT.Exp, scale=-0.5).then_inc(rstd_ready, 1)

        def vector_turn(dve, i, more):
            v = nc.vector
            links = 2 + 27 + 4 + 16 + 4
            done = [0]

            def link(ins):
                done[0] += 1
                ins.then_inc(chain, 1)
                dve.wait_ge(chain, links * i + done[0])

            def tiles(x):
                return x.rearrange("p (t c n) -> p t c n", c=2, n=CHUNK)

            dve.wait_ge(sig_ready, 2 * i)
            link(v.tensor_copy(cur[:, :], m.tab1[:, 0:8 * len(PAIR_ROWS)].rearrange(
                "p (j t) -> p j t", t=8)[:, :, bass.ds(i, 1)].rearrange("p j a -> p (j a)")))
            link(v.tensor_scalar(negkk[:, :], par["k_k"], -1.0, None, ALU.mult))
            v.memset(H[:, 0, :], 0.0).then_inc(cur_ready, 1)
            dve.wait_ge(cur_ready, i + 1)
            dve.wait_ge(proj_out[0], 3 * i + 3)
            dve.wait_ge(proj_out[1], 3 * i + 3)
            for hh in range(2):
                t0 = hh * HALF
                tk = slice(t0, t0 + HALF)

                def mixed(j, mu, out):
                    link(v.tensor_tensor(t_d, nxt[j][:, t0:t0 + HALF], nxt[j][:, t0 + 1:t0 + 1 + HALF],
                                         ALU.subtract))
                    return v.scalar_tensor_tensor(out=out, in0=t_d, scalar=mu,
                                                  in1=nxt[j][:, t0 + 1:t0 + 1 + HALF], op0=ALU.mult, op1=ALU.add)

                mixed(1, par["mu_k"], t_k).then_inc(k_mixed, 1)
                dve.wait_ge(k_mixed, 2 * i + hh + 1)
                link(mixed(0, par["mu_r"], t_r))
                if hh == 0:
                    link(mixed(2, par["mu_v"], V[:, tk]))
                else:
                    mixed(2, par["mu_v"], V[:, tk]).then_inc(raw_used, 1)
                    dve.wait_ge(raw_used, i + 1)
                dve.wait_ge(sig_ready, 2 * i + hh + 1)
                v.tensor_tensor_scan(t_s, reset[:, :], t_n, 0.0, ALU.mult, ALU.add).then_inc(scanned, 1)
                dve.wait_ge(scanned, 2 * i + hh + 1)
                dve.wait_ge(ksum_mm, 2 * i + hh + 1)
                v.tensor_scalar(t_n, PS[:, 4, :], 1e-24, None, ALU.max).then_inc(clamped, 1)
                link(v.tensor_scalar(t_d, t_a, -1.0, par["k_a"], ALU.add, ALU.mult))
                dve.wait_ge(rinv_ready, 2 * i + hh + 1)
                link(v.scalar_tensor_tensor(out=t_q, in0=t_k, scalar=negkk[:, 0:1], in1=t_n, op0=ALU.mult,
                                            op1=ALU.mult))
                link(v.scalar_tensor_tensor(out=t_k, in0=t_d, scalar=1.0, in1=t_k, op0=ALU.add, op1=ALU.mult))
                v.scalar_tensor_tensor(out=t_d, in0=t_r, scalar=par["r_k"], in1=t_k, op0=ALU.mult,
                                       op1=ALU.mult).then_inc(rk_ready, 1)
                dve.wait_ge(decay_ready, 2 * i + hh + 1)
                link(v.tensor_tensor(AR[:, 4 * hh:4 * hh + 4, 0, :].rearrange("p t (c n) -> p t c n", n=CHUNK),
                                     tiles(t_q), t_p[:, :, 0:CHUNK].rearrange("p (t c) n -> p t c n", c=2), ALU.mult))
                link(v.tensor_tensor(AR[:, 4 * hh:4 * hh + 4, 1, :].rearrange("p t (c n) -> p t c n", n=CHUNK),
                                     tiles(t_r), t_p[:, :, 1:1 + CHUNK].rearrange("p (t c) n -> p t c n", c=2),
                                     ALU.mult))
                link(v.tensor_copy(pend[:, 8 * hh:8 * hh + 8], t_p[:, :, CHUNK]))
                link(v.tensor_tensor(Kt[:, tk], t_k, t_ip, ALU.mult))
                link(v.scalar_tensor_tensor(out=t_q, in0=t_q, scalar=-1.0, in1=t_a, op0=ALU.mult, op1=ALU.mult))
                link(v.tensor_tensor(Bt[:, tk], t_q, t_ip, ALU.mult))
                dve.wait_ge(bonus_mm, 2 * i + hh + 1)
                v.tensor_tensor(bon[:, tk], PS[:, 5, :], V[:, tk], ALU.mult).then_inc(feat_ready, 1)
                dve.wait_ge(feat_ready, 2 * i + hh + 1)
            if more:
                copy_projection(dve, v.tensor_copy, i + 1, 0, 0)
            four = [P, 4, P]

            def inst(x):
                return x.rearrange("p (q n) -> p q n", n=P)

            for g in range(G):
                n = G * i + g
                if more and g in (1, 3):
                    copy_projection(dve, v.tensor_copy, i + 1, (1, 2)[g // 2], 0)
                for q in range(4):
                    dve.wait_ge(mt_mm, 4 * n + q + 1)
                    if q == 0:
                        dve.wait_ge(y_mm, 2 * n)
                    v.tensor_tensor(MT[:, q, :].rearrange("p (a n) -> p a n", a=2),
                                    PS[:, 4 + q, :].rearrange("p (a n) -> p a n", a=2),
                                    m.c(C_STRICT, 2).unsqueeze(1).to_broadcast([P, 2, 2 * P]),
                                    ALU.mult).then_inc(mt_out, 1)
                dve.wait_ge(mt_out, 4 * n + 4)
                link(v.tensor_tensor(inst(TT), MT[:, :, 0:P], m.c(C_LEVEL1T).unsqueeze(1).to_broadcast(four),
                                     ALU.mult))
                v.tensor_tensor(inst(TT), inst(TT), m.c(C_IDENT).unsqueeze(1).to_broadcast(four),
                                ALU.add).then_inc(tt_first, 1)
                dve.wait_ge(tt_first, n + 1)
                for lv in range(NL):
                    dve.wait_ge(x_mm, NL * n + lv + 1)
                    v.tensor_tensor(inst(X), inst(PS[:, 3, :]),
                                    m.c(C_LEVEL + lv).unsqueeze(1).to_broadcast(four), ALU.mult).then_inc(x_out, 1)
                    if lv < NL - 1:
                        dve.wait_ge(tn_mm, (NL - 1) * n + lv + 1)
                        dve.wait_ge(t_out, n + 1)
                        v.tensor_tensor(T, PS[:, 4, :], T, ALU.add).then_inc(tn_out, 1)
                        dve.wait_ge(tn_out, (NL - 1) * n + lv + 1)
                    dve.wait_ge(ttn_mm, NL * n + lv + 1)
                    v.tensor_tensor(TT, PS[:, 5, :], TT, ALU.add).then_inc(ttn_out, 1)
                    dve.wait_ge(ttn_out, NL * n + lv + 1)
                for c in range(4 * g, 4 * g + 4):
                    link(v.tensor_scalar(HP[:, :], H[:, c % 4, :], pend[:, c:c + 1], None, ALU.mult))
                    dve.wait_ge(h_mm, NC * i + c + 1)
                    v.scalar_tensor_tensor(out=H[:, (c + 1) % 4, :], in0=PS[:, 5, 0:RW_HD],
                                           scalar=pend[:, c:c + 1], in1=HP[:, :], op0=ALU.mult,
                                           op1=ALU.add).then_inc(h_out, 1)
                    dve.wait_ge(h_out, NC * i + c + 1)
            for hh in range(2):
                yc = work[:, hh * HALF:(hh + 1) * HALF]
                dve.wait_ge(mean_mm, 2 * i + hh + 1)
                v.tensor_tensor(inst(yc), AR[:, 4 * hh:4 * hh + 4, 0, :], inst(PS[:, 2 + hh, :]),
                                ALU.subtract).then_inc(centered, 1)
            for hh in range(2):
                yc, r = work[:, hh * HALF:(hh + 1) * HALF], work[:, (2 + hh) * HALF:(3 + hh) * HALF]
                tk = slice(hh * HALF, (hh + 1) * HALF)
                dve.wait_ge(rstd_ready, 2 * i + hh + 1)
                link(v.scalar_tensor_tensor(out=yc, in0=yc, scalar=par["lnx_g"], in1=r, op0=ALU.mult, op1=ALU.mult))
                link(v.scalar_tensor_tensor(out=yc, in0=yc, scalar=par["lnx_b"], in1=bon[:, tk], op0=ALU.add,
                                            op1=ALU.add))
                dve.wait_ge(gate_mm, 2 * i + hh + 1)
                v.tensor_tensor(big[:, bass.ds(i + PAIRS, 1), tk].rearrange("p a n -> p (a n)"), yc,
                                PS[:, 6 + hh, :], ALU.mult).then_inc(pair_done, 1)
            assert done[0] == links, done

        @block.tensor
        def _(pe):
            products(pe, 0, 0, 48)
            with pe.Fori(0, PAIRS - 1) as i:
                tensor_turn(pe, i, True)
            tensor_turn(pe, PAIRS - 1, False)

        @block.scalar
        def _(act):
            for j in range(3):
                copy_projection(act, nc.scalar.copy, 0, j, 1)
            with act.Fori(0, PAIRS - 1) as i:
                scalar_turn(act, i, True)
            scalar_turn(act, PAIRS - 1, False)

        @block.vector
        def _(dve):
            dve.wait_ge(preset, 3)
            for j in range(3):
                copy_projection(dve, nc.vector.tensor_copy, 0, j, 0)
            with dve.Fori(0, PAIRS - 1) as i:
                vector_turn(dve, i, True)
            vector_turn(dve, PAIRS - 1, False)

        @block.gpsimd
        def _(pool):
            for j in range(3):
                last = nc.gpsimd.memset(nxt[j][:, 0:1], 0.0)
            last.then_inc(preset, 1)
            nc.gpsimd.memset(t_p[:, :, 0:1], 1.0).then_inc(preset, 1)
            nc.gpsimd.memset(reset[:, :], 1.0).then_inc(ones_set, 1)
            pool.wait_ge(ones_set, 1)
            nc.gpsimd.memset(reset[:, :].rearrange("p (c n) -> p c n", n=CHUNK)[:, :, 0:1], 0.0).then_inc(preset, 1)


def merge_phase(nc, m, d):
    PS, big, W = m.PS, m.big, m.wslot
    with ExitStack() as ctx:
        sem = semaphores(nc, ctx)

        sig = ctx.enter_context(nc.sbuf_tensor("gates", [P, 2, S], F32))
        w_in = [sem(f"c_w_in{j}") for j in range(4)]
        done = [sem(f"c_done{j}") for j in range(4)]
        sig_out = sem("gates_out")
        product_out, gated = sem("product_out"), sem("gated")
        passed = sem("passed")
        block = ctx.enter_context(nc.Block())
        w_in_view = tile_cols(d["w_in"][0])
        cols = [(w_in_view, GATE0), (tile_cols(d["w_da_proj"][0]), 0), (w_in_view, GATE0 + D),
                (tile_cols(d["w_rw_proj"][0]), 0)]

        @block.sync
        def _(sp):
            for j, (w, c0) in enumerate(cols):
                sp.dma_start(W[:, j, :, :], w[:, :, c0:c0 + P]).then_inc(w_in[j], 16)
            with sp.Fori(1, KT) as f:
                for j, (w, c0) in enumerate(cols):
                    sp.wait_ge(done[j], f)
                    sp.sem_inc(passed, 1)
                    sp.dma_start(W[:, j, :, :], w[:, :, bass.ds(f * P + c0, P)]).then_inc(w_in[j], 16)

        @block.tensor
        def _(pe):
            with pe.Fori(0, KT) as f:
                for j, (src, k0) in enumerate(((m.xT, 0), (big, 0), (m.xT, 0), (big, 8))):
                    pe.wait_ge(w_in[j], 16 * f + 16)
                    if j % 2 == 0:
                        pe.wait_ge(sig_out, 2 * f + j // 2)
                    else:
                        pe.wait_ge(gated, 2 * f + j // 2)
                    for half in range(2):
                        for k in range(KT):
                            last = nc.tensor.matmul(PS[:, 2 * j + half, :], W[:, j, k, :],
                                                    src[:, k0 + k, half * HALF:(half + 1) * HALF],
                                                    start=k == 0, stop=k == KT - 1)
                    last.then_inc(done[j], 1)

        @block.scalar
        def _(act):
            with act.Fori(0, KT) as f:
                for b in range(2):
                    act.wait_ge(done[2 * b], f + 1)
                    act.wait_ge(gated, 2 * f + b)
                    nc.scalar.activation(sig[:, b, :].rearrange("p (h n) -> p h n", h=2),
                                         PS[:, 4 * b:4 * b + 2, :], ACT.Sigmoid).then_inc(sig_out, 1)

        @block.vector
        def _(dve):
            v = nc.vector
            with dve.Fori(0, KT) as f:
                out = big[:, bass.ds(f + 16, 1), :].rearrange("p a n -> p (a n)")
                for b in range(2):
                    dve.wait_ge(sig_out, 2 * f + b + 1)
                    dve.wait_ge(done[2 * b + 1], f + 1)
                    gate = sig[:, b, :].rearrange("p (h n) -> p h n", h=2)
                    v.tensor_tensor(gate, gate, PS[:, 4 * b + 2:4 * b + 4, :], ALU.mult).then_inc(product_out, 1)
                    dve.wait_ge(product_out, 2 * f + b + 1)
                    if b == 0:
                        v.tensor_copy(out, sig[:, 0, :]).then_inc(gated, 1)
                        dve.wait_ge(gated, 2 * f + 1)
                    else:
                        v.tensor_tensor(out, out, sig[:, 1, :], ALU.add).then_inc(gated, 1)
                        dve.wait_ge(gated, 2 * f + 2)


def out_norm_phase(nc, m, d, name, w_dram, src, nk, g_row, b_row):
    PS, xT = m.PS, m.xT
    with ExitStack() as ctx:
        sem = semaphores(nc, ctx, name + "_")

        W = ctx.enter_context(nc.sbuf_tensor(f"{name}_w", [P, 2, nk, P], F32)) if nk > KT else m.wslot
        sq = ctx.enter_context(nc.sbuf_tensor(f"{name}_sq", [P, 2, HALF], F32))
        rstd = ctx.enter_context(nc.sbuf_tensor(f"{name}_rstd", [P, 2, HALF], F32))
        w_in = [sem("w_in0"), sem("w_in1")]
        done, added = sem("done"), sem("added")
        mean_mm, centered, squared, var_mm = sem("mean_mm"), sem("centered"), sem("squared"), sem("var_mm")
        ln_out, rstd_out, scaled, normed = sem("ln_out"), sem("rstd_out"), sem("scaled"), sem("normed")
        block = ctx.enter_context(nc.Block())
        wv = tile_cols(w_dram)

        @block.sync
        def _(sp):
            for j in range(2):
                sp.dma_start(W[:, j, 0:nk, :], wv[:, :, j * P:(j + 1) * P]).then_inc(w_in[j], 16)
            with sp.Fori(1, KT // 2) as f:
                for j in range(2):
                    sp.wait_ge(done, 2 * f + (j - 1))
                    sp.dma_start(W[:, j, 0:nk, :], wv[:, :, bass.ds(f * (2 * P) + j * P, P)]).then_inc(w_in[j], 16)

        @block.tensor
        def _(pe):
            with pe.Fori(0, KT // 2) as f:
                for j in range(2):
                    pe.wait_ge(w_in[j], 16 * f + 16)
                    pe.wait_ge(added, 2 * f)
                    for half in range(2):
                        for k in range(nk):
                            last = nc.tensor.matmul(PS[:, 2 * j + half, :], W[:, j, k, :],
                                                    src[:, k, half * HALF:(half + 1) * HALF],
                                                    start=k == 0, stop=k == nk - 1)
                    last.then_inc(done, 1)
            pe.wait_ge(added, KT)
            for hh in range(2):
                for k in range(KT):
                    last = nc.tensor.matmul(PS[:, 4 + hh, :], m.c(C_MEAN), xT[:, k, hh * HALF:(hh + 1) * HALF],
                                            start=k == 0, stop=k == KT - 1)
                last.then_inc(mean_mm, 1)
            for hh in range(2):
                for k in range(KT):
                    n = KT * hh + k
                    pe.wait_ge(squared, n + 1)
                    nc.tensor.matmul(PS[:, 6 + hh, :], m.c(C_MEAN), sq[:, k % 2, :], start=k == 0,
                                     stop=k == KT - 1).then_inc(var_mm, 1)

        @block.vector
        def _(dve):
            v = nc.vector
            with dve.Fori(0, KT // 2) as f:
                for j in range(2):
                    x = xT[:, bass.ds(2 * f + j, 1), :].rearrange("p a (h n) -> p (a h) n", h=2)
                    dve.wait_ge(done, 2 * f + (j + 1))
                    v.scalar_tensor_tensor(out=x, in0=x, scalar=ALPHA, in1=PS[:, 2 * j:2 * j + 2, :],
                                           op0=ALU.mult, op1=ALU.add).then_inc(added, 1)
            dve.wait_ge(added, KT)
            for hh in range(2):
                x = xT[:, :, hh * HALF:(hh + 1) * HALF]
                dve.wait_ge(mean_mm, hh + 1)
                for k in range(KT):
                    v.tensor_tensor(x[:, k, :], x[:, k, :], PS[:, 4 + hh, :], ALU.subtract).then_inc(centered, 1)
            for hh in range(2):
                dve.wait_ge(rstd_out, hh + 1)
                dve.wait_ge(centered, KT * (hh + 1))
                for k in range(KT):
                    x = xT[:, k, hh * HALF:(hh + 1) * HALF]
                    v.scalar_tensor_tensor(out=x, in0=x, scalar=m.tab2[:, g_row * 8 + k:g_row * 8 + k + 1],
                                           in1=rstd[:, hh, :], op0=ALU.mult, op1=ALU.mult).then_inc(scaled, 1)

        @block.scalar
        def _(act):
            a = nc.scalar
            a.preload_act_table_set("natural_log_exp_and_others")
            for hh in range(2):
                for k in range(KT):
                    n = KT * hh + k
                    act.wait_ge(centered, n + 1)
                    if n >= 2:
                        act.wait_ge(var_mm, n - 1)
                    a.activation(sq[:, k % 2, :], xT[:, k, hh * HALF:(hh + 1) * HALF],
                                 ACT.Square).then_inc(squared, 1)
                act.wait_ge(var_mm, KT * (hh + 1))
                a.activation(rstd[:, hh, :], PS[:, 6 + hh, :], ACT.Ln, bias=m.eps[:, 0:1]).then_inc(ln_out, 1)
                act.wait_ge(ln_out, hh + 1)
                a.activation(rstd[:, hh, :], rstd[:, hh, :], ACT.Exp, scale=-0.5).then_inc(rstd_out, 1)
            for hh in range(2):
                for k in range(KT):
                    act.wait_ge(scaled, KT * hh + k + 1)
                    x = xT[:, k, hh * HALF:(hh + 1) * HALF]
                    a.activation(x, x, ACT.Identity,
                                 bias=m.tab2[:, b_row * 8 + k:b_row * 8 + k + 1]).then_inc(normed, 1)
            act.wait_ge(normed, 2 * KT)


def memory_phase(nc, m, d):
    PS, memT = m.PS, m.memT
    MT_ = MEM // P
    with ExitStack() as ctx:
        sem = semaphores(nc, ctx, "mem_")

        mem_in = ctx.enter_context(nc.sbuf_tensor("mem_tok", [P, MT_, D], F32))
        sq = ctx.enter_context(nc.sbuf_tensor("mem_sq", [P, KT, MEM], F32))
        rstd = ctx.enter_context(nc.sbuf_tensor("mem_rstd", [P, MEM], F32))
        loaded, turned, copied = sem("loaded"), sem("turned"), sem("copied")
        mean_mm, centered, squared, var_mm = sem("mean_mm"), sem("centered"), sem("squared"), sem("var_mm")
        ln_out, rstd_out, scaled, normed = sem("ln_out"), sem("rstd_out"), sem("scaled"), sem("normed")
        block = ctx.enter_context(nc.Block())

        @block.sync
        def _(sp):
            sp.dma_start(mem_in[:, :, :], d["mem"][0].rearrange("(t p) n -> p t n", p=P)).then_inc(loaded, 16)

        @block.tensor
        def _(pe):
            pe.wait_ge(loaded, 16)
            for t in range(MT_):
                for half in range(2):
                    for k in range(4):
                        last = nc.tensor.transpose(PS[:, 2 * t + half, k * P:(k + 1) * P],
                                                   mem_in[:, t, (4 * half + k) * P:(4 * half + k + 1) * P],
                                                   m.c(C_IDENT))
                    last.then_inc(turned, 1)
            pe.wait_ge(copied, 4)
            for k in range(KT):
                last = nc.tensor.matmul(PS[:, 4, 0:MEM], m.c(C_MEAN), memT[:, k, :], start=k == 0,
                                        stop=k == KT - 1)
            last.then_inc(mean_mm, 1)
            pe.wait_ge(squared, 1)
            for k in range(KT):
                last = nc.tensor.matmul(PS[:, 5, 0:MEM], m.c(C_MEAN), sq[:, k, :], start=k == 0,
                                        stop=k == KT - 1)
            last.then_inc(var_mm, 1)

        @block.vector
        def _(dve):
            v = nc.vector
            for t in range(MT_):
                for half in range(2):
                    dve.wait_ge(turned, 2 * t + half + 1)
                    v.tensor_copy(memT[:, 4 * half:4 * half + 4, t * P:(t + 1) * P],
                                  PS[:, 2 * t + half, :].rearrange("p (k t) -> p k t", k=4)).then_inc(copied, 1)
            dve.wait_ge(copied, 4)
            dve.wait_ge(mean_mm, 1)
            v.tensor_tensor(memT[:, :, :], memT[:, :, :],
                            PS[:, 4:5, 0:MEM].to_broadcast([P, KT, MEM]), ALU.subtract).then_inc(centered, 1)
            dve.wait_ge(centered, 1)
            dve.wait_ge(rstd_out, 1)
            for k in range(KT):
                v.scalar_tensor_tensor(out=memT[:, k, :], in0=memT[:, k, :],
                                       scalar=m.tab2[:, 48 + k:49 + k], in1=rstd[:, :], op0=ALU.mult,
                                       op1=ALU.mult).then_inc(scaled, 1)

        @block.scalar
        def _(act):
            a = nc.scalar
            a.preload_act_table_set("natural_log_exp_and_others")
            act.wait_ge(centered, 1)
            a.activation(sq[:, :, :], memT[:, :, :], ACT.Square).then_inc(squared, 1)
            act.wait_ge(var_mm, 1)
            a.activation(rstd[:, :], PS[:, 5, 0:MEM], ACT.Ln, bias=m.eps[:, 0:1]).then_inc(ln_out, 1)
            act.wait_ge(ln_out, 1)
            a.activation(rstd[:, :], rstd[:, :], ACT.Exp, scale=-0.5).then_inc(rstd_out, 1)
            for k in range(KT):
                act.wait_ge(scaled, k + 1)
                a.activation(memT[:, k, :], memT[:, k, :], ACT.Identity,
                             bias=m.tab2[:, 56 + k:57 + k]).then_inc(normed, 1)
            act.wait_ge(normed, KT)


def cross_phase(nc, m, d):
    PS, big, xT, memT = m.PS, m.big, m.xT, m.memT
    HT = CA_HD // P
    MT_ = MEM // P
    with ExitStack() as ctx:
        sem = semaphores(nc, ctx, "x_")

        W = [big[:, 8 + 2 * j:10 + 2 * j, :].rearrange("p a n -> p (a n)").rearrange(
            "p (k n) -> p k n", n=CA_HD) for j in range(3)]
        cq = big[:, 14:16, :]
        ck = big[:, 16, 0:HT * MEM].rearrange("p (t n) -> p t n", n=MEM)
        cv = big[:, 16, HT * MEM:2 * HT * MEM].rearrange("p (t n) -> p t n", n=CA_HD)
        prob = big[:, 17:19, :].rearrange("p a n -> p (a n)").rearrange("p (t n) -> p t n", n=MEM)
        probT = big[:, 19:21, :]
        stat = ctx.enter_context(nc.sbuf_tensor("x_stat", [P, 3, NT], F32))
        w_in = [sem(f"w_in{j}") for j in range(3)]
        q_mm, q_out = sem("q_mm"), sem("q_out")
        k_mm, k_out, v_mm, v_out = sem("k_mm"), sem("k_out"), sem("v_mm"), sem("v_out")
        s_mm, maxed, exped, normed = sem("s_mm"), sem("maxed"), sem("exped"), sem("normed")
        rec = sem("reciprocal")
        p_turned, p_out = sem("p_turned"), sem("p_out")
        o_mm, o_out = sem("o_mm"), sem("o_out")
        block = ctx.enter_context(nc.Block())
        views = [tile_cols(d["w_cq"][0]), tile_cols(d["w_ckv"][0]), tile_cols(d["w_ckv"][0])]

        @block.sync
        def _(sp):
            for j in range(3):
                c0 = D if j == 2 else 0
                sp.dma_start(W[j], views[j][:, :, c0:c0 + CA_HD]).then_inc(w_in[j], 16)
            with sp.Fori(1, CA_HEADS) as h:
                for j, (sm, per) in enumerate(((q_mm, 4), (k_mm, 1), (v_mm, 1))):
                    c0 = D if j == 2 else 0
                    sp.wait_ge(sm, per * h)
                    sp.dma_start(W[j], views[j][:, :, bass.ds(h * CA_HD + c0, CA_HD)]).then_inc(w_in[j], 16)

        @block.tensor
        def _(pe):
            mm = nc.tensor.matmul
            with pe.Fori(0, CA_HEADS) as h:
                pe.wait_ge(w_in[0], 16 * h + 16)
                pe.wait_ge(o_out, 4 * h)
                for n in range(4):
                    ft, half = n // 2, n % 2
                    for k in range(KT):
                        last = mm(PS[:, n, :], W[0][:, k, ft * P:(ft + 1) * P],
                                  xT[:, k, half * HALF:(half + 1) * HALF], start=k == 0, stop=k == KT - 1)
                    last.then_inc(q_mm, 1)
                pe.wait_ge(w_in[1], 16 * h + 16)
                pe.wait_ge(p_out, 4 * h)
                for ft in range(HT):
                    for k in range(KT):
                        last = mm(PS[:, 4, ft * MEM:(ft + 1) * MEM], W[1][:, k, ft * P:(ft + 1) * P],
                                  memT[:, k, :], start=k == 0, stop=k == KT - 1)
                last.then_inc(k_mm, 1)
                pe.wait_ge(w_in[2], 16 * h + 16)
                for mt in range(MT_):
                    for k in range(KT):
                        last = mm(PS[:, 5, mt * CA_HD:(mt + 1) * CA_HD], memT[:, k, mt * P:(mt + 1) * P],
                                  W[2][:, k, :], start=k == 0, stop=k == KT - 1)
                last.then_inc(v_mm, 1)
                pe.wait_ge(q_out, 4 * h + 4)
                pe.wait_ge(k_out, h + 1)
                for t in range(NT):
                    bank = (6, 7, 4, 5)[t // 2]
                    if t == 6:
                        pe.wait_ge(v_out, h + 1)
                    for ft in range(HT):
                        last = mm(PS[:, bank, t % 2 * MEM:(t % 2 + 1) * MEM], cq[:, ft, t * P:(t + 1) * P],
                                  ck[:, ft, :], start=ft == 0, stop=ft == HT - 1)
                    last.then_inc(s_mm, 1)
                pe.wait_ge(exped, NT * h + NT)
                for half in range(2):
                    pe.wait_ge(normed, NT * h + 4 * half + 4)
                    for mt in range(MT_):
                        for t in range(4):
                            last = nc.tensor.transpose(PS[:, 4 + 2 * half + mt, t * P:(t + 1) * P],
                                                       prob[:, 4 * half + t, mt * P:(mt + 1) * P], m.c(C_IDENT))
                        last.then_inc(p_turned, 1)
                pe.wait_ge(p_out, 4 * h + 4)
                pe.wait_ge(v_out, h + 1)
                for n in range(4):
                    ft, half = n // 2, n % 2
                    for mt in range(MT_):
                        last = mm(PS[:, n, :], cv[:, mt, ft * P:(ft + 1) * P],
                                  probT[:, mt, half * HALF:(half + 1) * HALF], start=mt == 0, stop=mt == MT_ - 1)
                    last.then_inc(o_mm, 1)

        @block.scalar
        def _(act):
            a = nc.scalar
            a.preload_act_table_set("natural_log_exp_and_others")
            with act.Fori(0, CA_HEADS) as h:
                for n in range(4):
                    act.wait_ge(q_mm, 4 * h + n + 1)
                    act.wait_ge(s_mm, NT * h)
                    a.mul(cq[:, n // 2, n % 2 * HALF:(n % 2 + 1) * HALF], PS[:, n, :],
                          CA_HD ** -0.5).then_inc(q_out, 1)
                for t in range(NT):
                    bank = (6, 7, 4, 5)[t // 2]
                    act.wait_ge(maxed, NT // 2 * h + t // 2 + 1)
                    act.wait_ge(p_turned, 4 * h)
                    a.activation(prob[:, t, :], PS[:, bank, t % 2 * MEM:(t % 2 + 1) * MEM], ACT.Exp,
                                 bias=stat[:, 0, t:t + 1], accum_out=stat[:, 1, t:t + 1]).then_inc(exped, 1)
                for n in range(4):
                    half, mt = n // 2, n % 2
                    act.wait_ge(p_turned, 4 * h + n + 1)
                    act.wait_ge(o_mm, 4 * h)
                    a.copy(probT[:, mt, half * HALF:(half + 1) * HALF], PS[:, 4 + n, :]).then_inc(p_out, 1)

        @block.vector
        def _(dve):
            v = nc.vector
            with dve.Fori(0, CA_HEADS) as h:
                dve.wait_ge(k_mm, h + 1)
                dve.wait_ge(s_mm, NT * h)
                v.tensor_copy(ck.rearrange("p t n -> p (t n)"), PS[:, 4, :]).then_inc(k_out, 1)
                dve.wait_ge(v_mm, h + 1)
                v.tensor_copy(cv.rearrange("p t n -> p (t n)"), PS[:, 5, :]).then_inc(v_out, 1)
                for b in range(NT // 2):
                    dve.wait_ge(s_mm, NT * h + 2 * b + 2)
                    v.tensor_reduce(stat[:, 0, 2 * b:2 * b + 2],
                                    PS[:, (6, 7, 4, 5)[b], :].rearrange("p (t n) -> p t n", n=MEM), AX, ALU.max,
                                    negate=True).then_inc(maxed, 1)
                for t in range(NT):
                    dve.wait_ge(exped, NT * h + t + 1)
                    v.reciprocal(stat[:, 2, t:t + 1], stat[:, 1, t:t + 1]).then_inc(rec, 1)
                    dve.wait_ge(rec, NT * h + t + 1)
                    v.tensor_scalar(prob[:, t, :], prob[:, t, :], stat[:, 2, t:t + 1], None,
                                    ALU.mult).then_inc(normed, 1)
                for n in range(4):
                    ft, half = n // 2, n % 2
                    dve.wait_ge(o_mm, 4 * h + n + 1)
                    v.tensor_copy(big[:, bass.ds(HT * h + ft, 1), half * HALF:(half + 1) * HALF],
                                  PS[:, n:n + 1, :]).then_inc(o_out, 1)


def hidden_phase(nc, m, d):
    PS, big, W, xT = m.PS, m.big, m.wslot, m.xT
    with ExitStack() as ctx:
        sem = semaphores(nc, ctx, "h_")

        act_buf = ctx.enter_context(nc.sbuf_tensor("silu", [P, 2, S], F32))
        w_in = [sem(f"w_in{j}") for j in range(4)]
        done = [sem(f"done{j}") for j in range(4)]
        silu_out, up_used = sem("silu_out"), sem("up_used")
        block = ctx.enter_context(nc.Block())
        wv = tile_cols(d["w_ffn_in"][0])
        col = (0, FF, P, FF + P)

        @block.sync
        def _(sp):
            for j in range(4):
                sp.dma_start(W[:, j, :, :], wv[:, :, col[j]:col[j] + P]).then_inc(w_in[j], 16)
            with sp.Fori(1, FT // 2) as f:
                for j in range(4):
                    sp.wait_ge(done[j], f)
                    sp.dma_start(W[:, j, :, :], wv[:, :, bass.ds(f * (2 * P) + col[j], P)]).then_inc(w_in[j], 16)

        @block.tensor
        def _(pe):
            with pe.Fori(0, FT // 2) as f:
                for j in range(4):
                    pe.wait_ge(w_in[j], 16 * f + 16)
                    if j % 2 == 0:
                        pe.wait_ge(silu_out, 2 * f + j // 2)
                    else:
                        pe.wait_ge(up_used, 2 * f + j // 2)
                    for half in range(2):
                        for k in range(KT):
                            last = nc.tensor.matmul(PS[:, 2 * j + half, :], W[:, j, k, :],
                                                    xT[:, k, half * HALF:(half + 1) * HALF],
                                                    start=k == 0, stop=k == KT - 1)
                    last.then_inc(done[j], 1)

        @block.scalar
        def _(act):
            with act.Fori(0, FT // 2) as f:
                for b in range(2):
                    act.wait_ge(done[2 * b], f + 1)
                    act.wait_ge(up_used, 2 * f + b)
                    nc.scalar.activation(act_buf[:, b, :].rearrange("p (h n) -> p h n", h=2),
                                         PS[:, 4 * b:4 * b + 2, :], ACT.Silu).then_inc(silu_out, 1)

        @block.vector
        def _(dve):
            with dve.Fori(0, FT // 2) as f:
                for b in range(2):
                    dve.wait_ge(silu_out, 2 * f + b + 1)
                    dve.wait_ge(done[2 * b + 1], f + 1)
                    nc.vector.tensor_tensor(big[:, bass.ds(2 * f + b, 1), :].rearrange("p a (h n) -> p (a h) n", h=2),
                                            act_buf[:, b, :].rearrange("p (h n) -> p h n", h=2),
                                            PS[:, 4 * b + 2:4 * b + 4, :], ALU.mult).then_inc(up_used, 1)


def store_phase(nc, m, d):
    PS = m.PS
    with ExitStack() as ctx:
        sem = semaphores(nc, ctx, "o_")

        rows = m.big[:, 0:4, :]
        turned = sem("turned")
        copied = [sem("copied_dve"), sem("copied_act")]
        stored = [sem(f"stored{j}") for j in range(4)]
        block = ctx.enter_context(nc.Block())

        @block.tensor
        def _(pe):
            for t in range(NT):
                for half in range(2):
                    n = 2 * t + half
                    if n >= 8:
                        pe.wait_ge(copied[half], (n - 8) // 2 + 1)
                    for k in range(4):
                        last = nc.tensor.transpose(PS[:, n % 8, k * P:(k + 1) * P],
                                                   m.xT[:, 4 * half + k, t * P:(t + 1) * P], m.c(C_IDENT))
                    last.then_inc(turned, 1)

        def copy_out(eng, copy, half):
            for t in range(NT):
                n = 2 * t + half
                eng.wait_ge(turned, n + 1)
                if t >= 4:
                    eng.wait_ge(stored[t % 4], 16)
                copy(rows[:, t % 4, half * HALF:(half + 1) * HALF], PS[:, n % 8, :]).then_inc(copied[half], 1)

        @block.vector
        def _(dve):
            copy_out(dve, nc.vector.tensor_copy, 0)

        @block.scalar
        def _(act):
            copy_out(act, nc.scalar.copy, 1)

        @block.sync
        def _(sp):
            for t in range(NT):
                sp.wait_ge(copied[0], t + 1)
                sp.wait_ge(copied[1], t + 1)
                sp.dma_start(d["out"][0, t * P:(t + 1) * P, :], rows[:, t % 4, :]).then_inc(stored[t % 4], 16)
            for j in range(4):
                sp.wait_ge(stored[j], 32)


def layer(nc, d):
    with ExitStack() as ctx:
        m = Memory(nc, ctx)
        big = m.big
        setup_phase(nc, m, d)
        attention_phase(nc, m, d)
        rwkv_phase(nc, m, d)
        merge_phase(nc, m, d)
        out_norm_phase(nc, m, d, "mix", d["w_mix_out"][0], big[:, 16:24, :], KT, 0, 1)
        memory_phase(nc, m, d)
        cross_phase(nc, m, d)
        out_norm_phase(nc, m, d, "co", d["w_co"][0], big[:, 0:8, :], KT, 2, 3)
        hidden_phase(nc, m, d)
        out_norm_phase(nc, m, d, "ffn", d["w_ffn_out"][0], big[:, 0:FT, :], FT, 4, 5)
        store_phase(nc, m, d)


_INS = ['x', 'mem', 'rel_bias', 'w_in', 'shift_mu', 'lambda_q1', 'lambda_k1', 'lambda_q2', 'lambda_k2',
        'da_subln_g', 'w_da_proj', 'rw_w0', 'rw_w2', 'rw_a0', 'rw_a2', 'rw_g2', 'rw_k_k', 'rw_k_a', 'rw_r_k',
        'rw_lnx_g', 'rw_lnx_b', 'w_rw_proj', 'w_mix_out', 'ln1_g', 'ln1_b', 'mem_ln_g', 'mem_ln_b', 'w_cq',
        'w_ckv', 'w_co', 'ln2_g', 'ln2_b', 'w_ffn_in', 'w_ffn_out', 'ln3_g', 'ln3_b']


def kernel(**inputs):
    import numpy as _np
    import concourse.bacc as _bacc
    from concourse import mybir as _mybir
    from concourse.bass_utils import run_bass_kernel_spmd as _run

    nc = _bacc.Bacc("TRN2", target_bir_lowering=False, num_devices=1)
    arrays, d = {}, {}
    const, pick, future = shape_constants()
    for name, a in [(n, inputs[n]) for n in _INS] + [("const", const), ("pick", pick), ("future", future)]:
        a = _np.ascontiguousarray(a)
        arrays[f"in_{name}_dram"] = a
        d[name] = nc.dram_tensor(f"in_{name}_dram", a.shape, _mybir.dt.from_np(a.dtype), kind="ExternalInput").ap()
    d["out"] = nc.dram_tensor("out_0_dram", (1, S, D), F32, kind="ExternalOutput").ap()
    layer(nc, d)
    r = _run(nc, [arrays], core_ids=[0])
    return r.results[0]["out_0_dram"]
```

```python
import math
from contextlib import ExitStack

import numpy as np

import concourse.bass as bass
from concourse import mybir

P = 128
F32 = mybir.dt.float32
ALU = mybir.AluOpType
ACT = mybir.ActivationFunctionType
AX = mybir.AxisListType.X

D = 1024
S = 1024
KT = D // P
NT = S // P
HALF = S // 2
DA_HEADS, DA_HD = 8, 64
BUCKETS, MAX_DIST = 32, 128
RW_HD = 64
PAIRS = D // P
CHUNK = 64
LORA, GATE_LORA = 64, 160
RW0 = 3 * D
LW0 = RW0 + 3 * D
LG0 = LW0 + 2 * LORA
GATE0 = LG0 + GATE_LORA
MEM = 256
CA_HEADS, CA_HD = 4, 256
FF = 2816
FT = FF // P
ALPHA = 2.0 ** 0.25
LN_EPS = 1e-5
LNX_EPS = 64e-5
LAM_INIT = 0.8 - 0.6 * math.exp(0.0)
DECAY = math.exp(-0.5)
MASKED = -1e30
NORM_SCALE = 2.0 ** 20
NORM_SHIFT = 10 * math.log(2.0)

C_IDENT, C_FLIP, C_HSUM, C_HMEAN, C_MEAN, C_STRICT, C_INCL, C_LEVEL1T = range(8)
LEVELS = (2, 4, 8, 16, 32)
C_LEVEL = 8
N_CONST = C_LEVEL + len(LEVELS)
WIN = 3 * P

PAIR_ROWS = ("mu_r", "mu_k", "mu_v", "w0", "a0", "k_k", "k_a", "r_k", "lnx_g", "lnx_b")
LN_ROWS = ("ln1_g", "ln1_b", "ln2_g", "ln2_b", "ln3_g", "ln3_b", "mem_ln_g", "mem_ln_b")
R_SUBLN, R_MUW, R_MUG, R_MUG2 = 64, 65, 66, 67


def shape_constants():
    i = np.arange(P)[:, None]
    j = np.arange(P)[None, :]
    same_head = i // RW_HD == j // RW_HD
    same_chunk = i // CHUNK == j // CHUNK
    tiles = [i == j, i + j == P - 1, same_head, same_head / RW_HD, np.full((P, P), 1.0 / D),
             same_chunk & (i < j), same_chunk & (i <= j), (i % 2 == 0) & (j == i + 1)]
    for s in LEVELS:
        tiles.append(((i // s) % 2 == 1) & (j // s == i // s - 1))
    const = np.concatenate([np.asarray(t, np.float32) for t in tiles], axis=1)
    rel = 2 * P - 1 - np.arange(WIN)
    n = np.maximum(rel, 0)
    exact = BUCKETS // 2
    nf = np.maximum(n, 1).astype(np.float32)
    large = exact + (np.log(nf / np.float32(exact)) / np.float32(math.log(MAX_DIST / exact))
                     * np.float32(BUCKETS - exact)).astype(np.int32)
    bucket = np.where(n < exact, n, np.minimum(large, BUCKETS - 1))
    pick = (np.arange(BUCKETS)[:, None] == bucket[None, :]).astype(np.float32)
    pick[BUCKETS - 1] -= 1.0
    future = np.where(rel < 0, np.float32(MASKED), np.float32(0.0))[None, :].repeat(DA_HEADS, 0)
    return const, pick, np.ascontiguousarray(future, np.float32)


class Memory:

    def __init__(self, nc, ctx):
        def sb(name, shape):
            return ctx.enter_context(nc.sbuf_tensor(name, shape, F32))

        self.PS = ctx.enter_context(nc.psum_tensor("PS", [P, 8, 512], F32))
        self.xT = sb("xT", [P, KT, S])
        self.big = sb("big", [P, 24, S])
        self.wslot = sb("wslot", [P, 4, KT, P])
        self.const = sb("const_sb", [P, N_CONST * P])
        self.tab1 = sb("tab1", [P, P])
        self.tab2 = sb("tab2", [P, P])
        self.subln = sb("subln", [P, 1])
        self.lam = sb("lam", [P, 1])
        self.neglam = sb("neglam", [P, 1])
        self.eps = sb("eps", [P, 3])
        self.lora = sb("lora", [P, S])
        self.gd1 = sb("gd1", [P, S])
        self.gd2 = sb("gd2", [32, S])
        self.bias = self.big[:, 22:24, :].rearrange("p a (h k) -> p (a h) k", k=2 * P)
        self.memT = self.big[:, 21:23, :].rearrange("p a n -> p (a n)").rearrange("p (k n) -> p k n", n=MEM)
        self.scratch = nc.dram_tensor("bias_rows", [DA_HEADS, WIN], F32, kind="Internal").ap()

    def c(self, n, count=1):
        return self.const[:, n * P:(n + count) * P]


def semaphores(nc, ctx, prefix=""):
    taken = []

    def sem(name):
        taken.append(nc.alloc_semaphore(name=prefix + name))
        return taken[-1]

    def clear():
        nc.clear_and_free_semaphores(taken)
        nc.all_engine_barrier()

    ctx.callback(clear)
    return sem


def tile_cols(w):
    return w.rearrange("(k p) n -> p k n", p=P)


def setup_phase(nc, m, d):
    xT, lora, gd1, gd2 = m.xT, m.lora, m.gd1, m.gd2
    PS, const = m.PS, m.const
    with ExitStack() as ctx:
        def sb(name, shape):
            return ctx.enter_context(nc.sbuf_tensor(name, shape, F32))

        sem = semaphores(nc, ctx)

        xin = sb("xin", [P, 2, D])
        rows1 = sb("rows1", [P, P])
        rows2 = sb("rows2", [P, P])
        wl = [sb("wl0", [P, KT, P]), sb("wl1", [P, KT, P]), sb("wl2", [P, KT, 32])]
        raw = sb("raw_lora", [P, 1 + S])
        lamv = sb("lamv", [P, 4, DA_HD])
        lprod = sb("lprod", [P, 2, DA_HD])
        lsum = sb("lsum", [P, 2])
        lexp = sb("lexp", [P, 2])
        rel = sb("rel", [BUCKETS, DA_HEADS])
        pick = sb("pick_sb", [BUCKETS, WIN])
        future = sb("future_sb", [DA_HEADS, WIN])
        frow = sb("frow", [DA_HEADS, WIN])
        grid = sb("grid", [P, DA_HEADS, 2 * P])
        diff = sb("diff", [P, S])

        const_in = sem("const_in")
        rows_zero = sem("rows_zero")
        rows_in = sem("rows_in")
        lam_in = sem("lam_in")
        rel_in = sem("rel_in")
        wl_in = [sem(f"wl_in{j}") for j in range(3)]
        x_in = [sem("x_in0"), sem("x_in1")]
        x_turned = sem("x_turned")
        x_out = [sem("x_out_dve"), sem("x_out_act")]
        tab_turned = sem("tab_turned")
        tab_out = sem("tab_out")
        lora_mm = sem("lora_mm")
        raw_out = sem("raw_out")
        raw_zero = sem("raw_zero")
        lora_out = sem("lora_out")
        lora_act = sem("lora_act")
        rel_mm = sem("rel_mm")
        frow_out = sem("frow_out")
        frow_stored = sem("frow_stored")
        grid_in = sem("grid_in")
        flip_mm = sem("flip_mm")
        bias_out = sem("bias_out")
        lam_sum = sem("lam_sum")
        lam_exp = sem("lam_exp")
        chain = sem("setup_chain")

        block = ctx.enter_context(nc.Block())
        w_in = tile_cols(d["w_in"][0])
        vec_rows = dict(zip(PAIR_ROWS, [d["shift_mu"][0, 0:D], d["shift_mu"][0, D:2 * D],
                                        d["shift_mu"][0, 2 * D:3 * D], d["rw_w0"][0], d["rw_a0"][0],
                                        d["rw_k_k"][0], d["rw_k_a"][0],
                                        d["rw_r_k"][0].rearrange("h n -> (h n)"),
                                        d["rw_lnx_g"][0], d["rw_lnx_b"][0]]))

        @block.sync
        def _(sp):
            sp.dma_start(const[:, :], d["const"]).then_inc(const_in, 16)
            for t in range(NT):
                if t >= 2:
                    sp.wait_ge(x_turned, 2 * (t - 1))
                sp.dma_start(xin[:, t % 2, :], d["x"][0, t * P:(t + 1) * P, :]).then_inc(x_in[t % 2], 16)
                if t == 1:
                    sp.dma_start(wl[0][:, :, :], w_in[:, :, LW0:LG0]).then_inc(wl_in[0], 16)
                    sp.dma_start(wl[1][:, :, :], w_in[:, :, LG0:LG0 + P]).then_inc(wl_in[1], 16)
                    sp.dma_start(wl[2][:, :, :], w_in[:, :, LG0 + P:GATE0]).then_inc(wl_in[2], 16)
            sp.wait_ge(frow_out, 1)
            sp.dma_start(m.scratch, frow[:, :]).then_inc(frow_stored, 16)
            sp.wait_ge(frow_stored, 16)
            sp.dma_start(grid[:, :, :], bass.AP(tensor=m.scratch.tensor, offset=0,
                                                ap=[[1, P], [WIN, DA_HEADS], [1, 2 * P]])).then_inc(grid_in, 16)
            sp.wait_ge(grid_in, 16)

        @block.scalar
        def _(act):
            act.wait_ge(rows_zero, 2)
            for j, name in enumerate(PAIR_ROWS):
                act.dma_start(rows1[8 * j:8 * j + 8, :],
                              vec_rows[name].rearrange("(t p) -> t p", p=P)).then_inc(rows_in, 16)
            for j, name in enumerate(LN_ROWS):
                act.dma_start(rows2[8 * j:8 * j + 8, :],
                              d[name][0].rearrange("(t p) -> t p", p=P)).then_inc(rows_in, 16)
            mu = d["shift_mu"]
            act.dma_start(rows2[R_SUBLN:R_SUBLN + 1, :], d["da_subln_g"]).then_inc(rows_in, 16)
            act.dma_start(rows2[R_MUW:R_MUW + 1, :], mu[:, 3 * D:3 * D + P]).then_inc(rows_in, 16)
            act.dma_start(rows2[R_MUG:R_MUG + 1, :], mu[:, 3 * D + P:3 * D + 2 * P]).then_inc(rows_in, 16)
            act.dma_start(rows2[R_MUG2:R_MUG2 + 1, 0:32], mu[:, 3 * D + 2 * P:]).then_inc(rows_in, 16)
            for j, name in enumerate(("lambda_q1", "lambda_k1", "lambda_q2", "lambda_k2")):
                act.dma_start(lamv[:, j, :], d[name][0].partition_broadcast(P)).then_inc(lam_in, 16)
            act.dma_start(rel[:, :], d["rel_bias"]).then_inc(rel_in, 16)
            act.dma_start(pick[:, :], d["pick"]).then_inc(rel_in, 16)
            act.dma_start(future[:, :], d["future"]).then_inc(rel_in, 16)
            for t in range(NT):
                n = 2 * t + 1
                act.wait_ge(x_turned, n + 1)
                nc.scalar.copy(xT[:, 4:8, t * P:(t + 1) * P],
                               PS[:, n % 4, :].rearrange("p (k t) -> p k t", k=4)).then_inc(x_out[1], 1)
            act.wait_ge(lam_sum, 1)
            nc.scalar.activation(lexp[:, :], lsum[:, :], ACT.Exp).then_inc(lam_exp, 1)
            act.wait_ge(lora_out, 1)
            nc.scalar.activation(lora[0:LORA, :], lora[0:LORA, :], ACT.Tanh).then_inc(lora_act, 1)
            act.wait_ge(lora_out, 2)
            nc.scalar.activation(gd1[:, :], gd1[:, :], ACT.Sigmoid).then_inc(lora_act, 1)
            act.wait_ge(lora_out, 3)
            nc.scalar.activation(gd2[0:32, :], gd2[0:32, :], ACT.Sigmoid).then_inc(lora_act, 1)
            act.wait_ge(lora_act, 3)

        @block.tensor
        def _(pe):
            pe.wait_ge(const_in, 16)
            for t in range(NT):
                pe.wait_ge(x_in[t % 2], 16 * (t // 2 + 1))
                for half in range(2):
                    n = 2 * t + half
                    if n >= 4:
                        pe.wait_ge(x_out[n % 2], (n - 4) // 2 + 1)
                    for k in range(4):
                        f = 4 * half + k
                        last = nc.tensor.transpose(PS[:, n % 4, k * P:(k + 1) * P],
                                                   xin[:, t % 2, f * P:(f + 1) * P], m.c(C_IDENT))
                    last.then_inc(x_turned, 1)
            pe.wait_ge(rows_in, 16 * (len(PAIR_ROWS) + len(LN_ROWS) + 4))
            nc.tensor.transpose(PS[:, 4, 0:P], rows1[:, :], m.c(C_IDENT))
            nc.tensor.transpose(PS[:, 4, P:2 * P], rows2[:, :], m.c(C_IDENT)).then_inc(tab_turned, 1)
            pe.wait_ge(rel_in, 48)
            nc.tensor.matmul(PS[0:DA_HEADS, 5, 0:WIN], rel[:, :], pick[:, :], start=True,
                             stop=True).then_inc(rel_mm, 1)
            pe.wait_ge(x_out[0], NT)
            pe.wait_ge(x_out[1], NT)
            for j, rows in enumerate((P, P, 32)):
                pe.wait_ge(wl_in[j], 16)
                if j:
                    pe.wait_ge(raw_out, j)
                for h in range(2):
                    for k in range(KT):
                        last = nc.tensor.matmul(PS[0:rows, 6 + h, :], wl[j][:, k, :],
                                                xT[:, k, h * HALF:(h + 1) * HALF],
                                                start=k == 0, stop=k == KT - 1)
                last.then_inc(lora_mm, 1)
            pe.wait_ge(grid_in, 16)
            for h in range(DA_HEADS):
                last = nc.tensor.matmul(PS[:, h // 2, (h % 2) * 2 * P:(h % 2 + 1) * 2 * P], m.c(C_FLIP),
                                        grid[:, h, :], start=True, stop=True)
            last.then_inc(flip_mm, 1)

        @block.vector
        def _(dve):
            v = nc.vector
            steps = [0]

            def link(ins):
                steps[0] += 1
                ins.then_inc(chain, 1)
                dve.wait_ge(chain, steps[0])

            v.memset(rows1[:, :], 0.0).then_inc(rows_zero, 1)
            v.memset(rows2[:, :], 0.0).then_inc(rows_zero, 1)
            v.memset(m.eps[:, 0:1], LN_EPS)
            v.memset(m.eps[:, 1:2], LNX_EPS)
            v.memset(m.eps[:, 2:3], NORM_SHIFT)
            link(v.memset(raw[:, 0:1], 0.0))
            for t in range(NT):
                n = 2 * t
                dve.wait_ge(x_turned, n + 1)
                v.tensor_copy(xT[:, 0:4, t * P:(t + 1) * P],
                              PS[:, n % 4, :].rearrange("p (k t) -> p k t", k=4)).then_inc(x_out[0], 1)
            dve.wait_ge(tab_turned, 1)
            link(v.tensor_copy(m.tab1[:, :], PS[:, 4, 0:P]))
            link(v.tensor_copy(m.tab2[:, :], PS[:, 4, P:2 * P]))
            link(v.tensor_scalar(m.subln[:, :], m.tab2[:, R_SUBLN:R_SUBLN + 1], 1.0 - LAM_INIT, None, ALU.mult))
            dve.wait_ge(rel_mm, 1)
            v.tensor_tensor(frow[:, :], PS[0:DA_HEADS, 5, 0:WIN], future[:, :], ALU.add).then_inc(frow_out, 1)
            dve.wait_ge(lam_in, 64)
            link(v.tensor_tensor(lprod[:, :, :], lamv[:, 0:4:2, :], lamv[:, 1:4:2, :], ALU.mult))
            v.tensor_reduce(lsum[:, :], lprod[:, :, :], AX, ALU.add).then_inc(lam_sum, 1)
            dve.wait_ge(lam_exp, 1)
            link(v.tensor_tensor(m.lam[:, :], lexp[:, 0:1], lexp[:, 1:2], ALU.subtract))
            link(v.tensor_scalar(m.neglam[:, :], m.lam[:, :], LAM_INIT, -1.0, ALU.add, ALU.mult))
            for j, (dst, rows, row) in enumerate(((lora, P, R_MUW), (gd1, P, R_MUG), (gd2, 32, R_MUG2))):
                dve.wait_ge(lora_mm, j + 1)
                v.tensor_copy(raw[0:rows, 1:1 + HALF], PS[0:rows, 6, :])
                last = v.tensor_copy(raw[0:rows, 1 + HALF:1 + S], PS[0:rows, 7, :])
                last.then_inc(raw_out, 1)
                dve.wait_ge(raw_out, j + 1)
                link(v.tensor_tensor(diff[0:rows, :], raw[0:rows, 0:S], raw[0:rows, 1:1 + S], ALU.subtract))
                v.scalar_tensor_tensor(out=dst[0:rows, :], in0=diff[0:rows, :],
                                       scalar=m.tab2[0:rows, row:row + 1], in1=raw[0:rows, 1:1 + S],
                                       op0=ALU.mult, op1=ALU.add).then_inc(lora_out, 1)
                dve.wait_ge(lora_out, j + 1)
            dve.wait_ge(flip_mm, 1)
            for b in range(4):
                last = v.tensor_copy(m.bias[:, 2 * b:2 * b + 2, :],
                                     PS[:, b, :].rearrange("p (h k) -> p h k", h=2))
            link(last)


def attention_phase(nc, m, d):
    PS, big, W = m.PS, m.big, m.wslot
    nxt = [big[:, 8 + j, :] for j in range(3)]
    qT, kT = big[:, 11, :], big[:, 12, :]
    vtok = big[:, 13, :].rearrange("p (t c) -> p t c", c=P)
    prob = big[:, 14:16, :]
    attn = big[:, 16:18, :]
    attnT = big[:, 18:20, :]
    NQ = NT
    ring = []
    for qb in range(NQ):
        ring += [("T", qb, g) for g in range(qb // 4 + 1)]
        if qb:
            ring.append(("O", qb - 1, 0))
        ring.append(("V", qb, 0))
    ring.append(("O", NQ - 1, 0))
    place = {r: n for n, r in enumerate(ring)}
    N_RING = len(ring)
    assert N_RING % 2 == 0
    act_before = [sum(r[0] != "V" for r in ring[:n + 1]) for n in range(N_RING)]
    dve_before = [sum(r[0] == "V" for r in ring[:n + 1]) for n in range(N_RING)]
    PARTS = [(0, 1), (2, 3), (4, 5), (6, 7), (8,), (9,), (10,), (11,)]

    with ExitStack() as ctx:
        sem = semaphores(nc, ctx)

        small = ctx.enter_context(nc.sbuf_tensor("attn_small", [P, 12], F32))
        onorm = ctx.enter_context(nc.sbuf_tensor("onorm", [P, 2, P], F32))
        ojunk = ctx.enter_context(nc.sbuf_tensor("ojunk", [P, P], F32))
        nmax, lsum, rl = small[:, 0:2], small[:, 2:4], small[:, 4:6]
        ssq, lnv, rstd = small[:, 6:7], small[:, 7:8], small[:, 8:9]

        w_in = [sem(f"a_w_in{j}") for j in range(3)]
        proj_done = [sem("a_proj_lo"), sem("a_proj_hi")]
        proj_out = [sem("a_proj_out_dve"), sem("a_proj_out_act")]
        q_cur, k_cur = sem("q_cur"), sem("k_cur")
        v_turned, vtok_out = sem("v_turned"), sem("vtok_out")
        scores = sem("scores_ready")
        maxed = sem("max_ready")
        exped = sem("exp_ready")
        combined = sem("attn_ready")
        ring_full = sem("ring_full")
        ring_act, ring_dve = sem("ring_emptied_act"), sem("ring_emptied_dve")
        rstd_ready = sem("rstd_ready")
        dchain, achain = sem("a_dve_chain"), sem("a_act_chain")

        block = ctx.enter_context(nc.Block())
        wv = tile_cols(d["w_in"][0])

        @block.sync
        def _(sp):
            for j in range(3):
                sp.dma_start(W[:, j, :, :], wv[:, :, j * D:j * D + P]).then_inc(w_in[j], 16)
            with sp.Fori(0, DA_HEADS - 1) as i:
                for j in range(3):
                    sp.wait_ge(proj_done[1], 3 * i + (j + 1))
                    sp.dma_start(W[:, j, :, :],
                                 wv[:, :, bass.ds(i * P + (j * D + P), P)]).then_inc(w_in[j], 16)

        def project_part(pe, n, part):
            j, half, ks = part // 4, part // 2 % 2, part % 2
            if ks == 0:
                if half == 0:
                    pe.wait_ge(w_in[j], 16 * n + 16)
                pe.wait_ge(proj_out[half], 3 * n + j)
            for k in range(4 * ks, 4 * ks + 4):
                last = nc.tensor.matmul(PS[:, 6 + half, :], W[:, j, k, :],
                                        m.xT[:, k, half * HALF:(half + 1) * HALF],
                                        start=k == 0, stop=k == KT - 1)
            if ks == 1:
                last.then_inc(proj_done[half], 1)

        def copy_projection(eng, copy, n, j, half):
            eng.wait_ge(proj_done[half], 3 * n + j + 1)
            if j < 2:
                eng.wait_ge((q_cur, k_cur)[j], n)
            else:
                eng.wait_ge(v_turned, 2 * n)
            copy(nxt[j][:, half * HALF:(half + 1) * HALF], PS[:, 6 + half, :]).then_inc(proj_out[half], 1)

        def tensor_turn(pe, i, more):
            def width(qb):
                return (qb + 1) * P

            def score(qb):
                pe.wait_ge(exped, 16 * i + 2 * qb)
                for c in range(2):
                    for n0 in range(0, width(qb), 512):
                        w = min(512, width(qb) - n0)
                        last = nc.tensor.matmul(PS[:, 2 * c + n0 // 512, 0:w],
                                                qT[64 * c:64 * c + 64, qb * P:(qb + 1) * P],
                                                kT[64 * c:64 * c + 64, n0:n0 + w], start=True, stop=True)
                    last.then_inc(scores, 1)

            def ring_slot(r, act=0, dve=0):
                n = place[r]
                if n >= 2:
                    act, dve = max(act, act_before[n - 2]), max(dve, dve_before[n - 2])
                pe.wait_ge(ring_act, act_before[-1] * i + act)
                pe.wait_ge(ring_dve, dve_before[-1] * i + dve)
                return 4 + n % 2

            def turn_output(qb):
                bank = ring_slot(("O", qb, 0), dve=qb + 1)
                nc.tensor.transpose(PS[:, bank, 0:P], onorm[:, qb % 2, :], m.c(C_IDENT)).then_inc(ring_full, 1)

            pe.wait_ge(proj_out[0], 3 * i + 3)
            pe.wait_ge(proj_out[1], 3 * i + 3)
            for g in range(2):
                if g == 0:
                    pe.wait_ge(ring_act, act_before[-1] * i)
                for t in range(4):
                    last = nc.tensor.transpose(PS[:, 4 + g, t * P:(t + 1) * P],
                                               nxt[2][:, (4 * g + t) * P:(4 * g + t + 1) * P], m.c(C_IDENT))
                last.then_inc(v_turned, 1)
            pe.wait_ge(q_cur, i + 1)
            pe.wait_ge(k_cur, i + 1)
            score(0)
            pe.wait_ge(vtok_out, 2 * i + 2)
            for qb in range(NQ):
                if qb + 1 < NQ:
                    score(qb + 1)
                if more:
                    for part in PARTS[qb]:
                        project_part(pe, i + 1, part)
                pe.wait_ge(combined, NQ * i + qb + 1)
                for g in range(qb // 4 + 1):
                    bank = ring_slot(("T", qb, g))
                    for t in range(4 * g, min(4 * g + 4, qb + 1)):
                        last = nc.tensor.transpose(PS[:, bank, (t % 4) * P:(t % 4 + 1) * P],
                                                   attn[:, qb % 2, t * P:(t + 1) * P], m.c(C_IDENT))
                    last.then_inc(ring_full, 1)
                if qb:
                    turn_output(qb - 1)
                bank = ring_slot(("V", qb, 0), act=act_before[place[("T", qb, qb // 4)]])
                for t in range(qb + 1):
                    last = nc.tensor.matmul(PS[:, bank, 0:P], attnT[:, qb % 2, t * P:(t + 1) * P],
                                            vtok[:, t, :], start=t == 0, stop=t == qb)
                last.then_inc(ring_full, 1)
            turn_output(NQ - 1)

        def scalar_turn(act, i, more):
            def expo(qb):
                w = (qb + 1) * P
                for c in range(2):
                    act.wait_ge(maxed, 16 * i + 2 * qb + c + 1)
                    act.wait_ge(combined, NQ * i + qb)
                    nc.scalar.activation(prob[:, c, 0:w], PS[:, 2 * c:2 * c + 2, :].rearrange("p b n -> p (b n)")[:, 0:w],
                                         ACT.Exp, bias=nmax[:, c:c + 1],
                                         accum_out=lsum[:, c:c + 1]).then_inc(exped, 1)

            def output_out(qb):
                n = place[("O", qb, 0)]
                act.wait_ge(ring_full, N_RING * i + n + 1)
                nc.scalar.activation(big[:, bass.ds(i, 1), qb * P:(qb + 1) * P], PS[:, 4 + n % 2:5 + n % 2, 0:P],
                                     ACT.Copy, scale=m.subln[:, 0:1]).then_inc(ring_act, 1)

            act.wait_ge(proj_out[0], 3 * i + 3)
            act.wait_ge(proj_out[1], 3 * i + 3)
            nc.scalar.mul(qT[:, :], nxt[0][:, :], DA_HD ** -0.5).then_inc(q_cur, 1)
            for g in range(2):
                act.wait_ge(v_turned, 2 * i + g + 1)
                nc.scalar.copy(vtok[:, 4 * g:4 * g + 4, :].rearrange("p t c -> p (t c)"),
                               PS[:, 4 + g, :]).then_inc(vtok_out, 1)
            expo(0)
            for qb in range(NQ):
                for g in range(qb // 4 + 1):
                    n = place[("T", qb, g)]
                    act.wait_ge(ring_full, N_RING * i + n + 1)
                    t1 = min(4 * g + 4, qb + 1)
                    nc.scalar.copy(attnT[:, qb % 2, 4 * g * P:t1 * P],
                                   PS[:, 4 + n % 2, 0:(t1 - 4 * g) * P]).then_inc(ring_act, 1)
                if qb:
                    output_out(qb - 1)
                if qb + 1 < NQ:
                    expo(qb + 1)
                n = place[("V", qb, 0)]
                act.wait_ge(ring_full, N_RING * i + n + 1)
                act.wait_ge(ring_dve, dve_before[-1] * i + qb)
                nc.scalar.activation(ojunk[:, :], PS[:, 4 + n % 2, 0:P], ACT.Square,
                                     accum_out=ssq).then_inc(achain, 1)
                act.wait_ge(achain, 2 * NQ * i + 2 * qb + 1)
                nc.scalar.activation(lnv, ssq, ACT.Ln, bias=m.eps[:, 0:1], scale=1.0 / P).then_inc(achain, 1)
                act.wait_ge(achain, 2 * NQ * i + 2 * qb + 2)
                nc.scalar.activation(rstd, lnv, ACT.Exp, scale=-0.5).then_inc(rstd_ready, 1)
                if more:
                    for part in PARTS[qb]:
                        if part % 4 == 3:
                            copy_projection(act, nc.scalar.copy, i + 1, part // 4, 1)
            output_out(NQ - 1)

        def vector_turn(dve, i, more):
            v = nc.vector
            links = 3 * NQ + 2 * NQ
            done = [0]

            def link(ins):
                done[0] += 1
                ins.then_inc(dchain, 1)
                dve.wait_ge(dchain, links * i + done[0])

            def rowmax(qb):
                w = (qb + 1) * P
                wb = min(w, 2 * P)
                for c in range(2):
                    flat = PS[:, 2 * c:2 * c + 2, :].rearrange("p b n -> p (b n)")
                    dve.wait_ge(scores, 16 * i + 2 * qb + c + 1)
                    link(v.tensor_tensor(flat[:, w - wb:w], flat[:, w - wb:w],
                                         m.bias[:, bass.ds(i, 1), 2 * P - wb:2 * P].rearrange("p a n -> p (a n)"),
                                         ALU.add))
                    dve.wait_ge(exped, 16 * i + 2 * qb + c)
                    v.tensor_reduce(nmax[:, c:c + 1], flat[:, 0:w], AX, ALU.max,
                                    negate=True).then_inc(maxed, 1)

            dve.wait_ge(proj_out[0], 3 * i + 3)
            dve.wait_ge(proj_out[1], 3 * i + 3)
            v.tensor_copy(kT[:, :], nxt[1][:, :]).then_inc(k_cur, 1)
            rowmax(0)
            for qb in range(NQ):
                w = (qb + 1) * P
                dve.wait_ge(exped, 16 * i + 2 * qb + 2)
                link(v.reciprocal(rl, lsum))
                link(v.tensor_tensor(rl[:, 1:2], rl[:, 1:2], m.neglam[:, :], ALU.mult))
                link(v.tensor_scalar(prob[:, 1, 0:w], prob[:, 1, 0:w], rl[:, 1:2], None, ALU.mult))
                if qb >= 2:
                    dve.wait_ge(ring_full, N_RING * i + place[("T", qb - 2, (qb - 2) // 4)] + 1)
                v.scalar_tensor_tensor(out=attn[:, qb % 2, 0:w], in0=prob[:, 0, 0:w], scalar=rl[:, 0:1],
                                       in1=prob[:, 1, 0:w], op0=ALU.mult, op1=ALU.add).then_inc(combined, 1)
                if qb + 1 < NQ:
                    rowmax(qb + 1)
                n = place[("V", qb, 0)]
                dve.wait_ge(rstd_ready, NQ * i + qb + 1)
                if qb >= 2:
                    dve.wait_ge(ring_full, N_RING * i + place[("O", qb - 2, 0)] + 1)
                v.tensor_scalar(onorm[:, qb % 2, :], PS[:, 4 + n % 2, 0:P], rstd, None,
                                ALU.mult).then_inc(ring_dve, 1)
                if more:
                    for part in PARTS[qb]:
                        if part % 4 == 1:
                            copy_projection(dve, v.tensor_copy, i + 1, part // 4, 0)

        @block.tensor
        def _(pe):
            for part in range(12):
                project_part(pe, 0, part)
            with pe.Fori(0, DA_HEADS - 1) as i:
                tensor_turn(pe, i, True)
            tensor_turn(pe, DA_HEADS - 1, False)

        @block.scalar
        def _(act):
            nc.scalar.preload_act_table_set("natural_log_exp_and_others")
            for j in range(3):
                copy_projection(act, nc.scalar.copy, 0, j, 1)
            with act.Fori(0, DA_HEADS - 1) as i:
                scalar_turn(act, i, True)
            scalar_turn(act, DA_HEADS - 1, False)

        @block.vector
        def _(dve):
            for j in range(3):
                copy_projection(dve, nc.vector.tensor_copy, 0, j, 0)
            with dve.Fori(0, DA_HEADS - 1) as i:
                vector_turn(dve, i, True)
            vector_turn(dve, DA_HEADS - 1, False)


def rwkv_phase(nc, m, d):
    PS, big, W = m.PS, m.big, m.wslot
    G = NT // 2
    with ExitStack() as ctx:
        def sb(name, shape):
            return ctx.enter_context(nc.sbuf_tensor(name, shape, F32))

        sem = semaphores(nc, ctx)

        nxt = [sb(f"raw{j}", [P, 1 + S]) for j in range(3)]
        AR = big[:, 16:18, :].rearrange("p a n -> p (a n)").rearrange("p (t w n) -> p t w n", t=NT, w=2)
        Bt, Kt, V, bon = (big[:, 18 + j, :] for j in range(4))
        work = big[:, 22:24, :].rearrange("p a n -> p (a n)")
        more_work = sb("rw_work", [P, 5, HALF])
        t_r, t_k, t_s, t_a = (work[:, j * HALF:(j + 1) * HALF] for j in range(4))
        t_ip, t_q, t_n, t_d = (more_work[:, j, :] for j in range(4))
        t_p = sb("running_decay", [P, HALF // CHUNK, CHUNK + 1])
        MT = [x.rearrange("p (i n) -> p i n", i=4)
              for x in (work, sb("chunk_maps", [P, 4 * 4 * P])[:, :])]
        T, X = more_work[:, 0, :], more_work[:, 2, :]
        TT = [more_work[:, 1, :], W[:, 3, 0:4, :].rearrange("p k n -> p (k n)")]
        Tq = [more_work[:, 3, j * 4 * RW_HD:(j + 1) * 4 * RW_HD] for j in range(2)]
        WT = [more_work[:, 4, j * 2 * P:(j + 1) * 2 * P].rearrange("p (l n) -> p l n", l=2) for j in range(2)]
        tok2 = sb("tok", [P, 2, 2, 4, P])
        tok = [tok2[:, j] for j in range(2)]
        U = sb("U", [P, 2, RW_HD])
        H = sb("state", [P, 4, RW_HD])
        HP = sb("state_decayed", [P, RW_HD])
        pend = sb("chunk_decay", [P, S // CHUNK])
        reset = sb("reset", [P, HALF])
        cur = sb("cur_params", [P, len(PAIR_ROWS)])
        negkk = sb("neg_k_k", [P, 1])
        lup = W[:, 3, 4:7, :]
        par = {name: cur[:, j:j + 1] for j, name in enumerate(PAIR_ROWS)}

        w_in = [sem(f"r_w_in{j}") for j in range(3)]
        lup_in = sem("lup_in")
        proj_done = [sem("r_proj_lo"), sem("r_proj_hi")]
        proj_out = [sem("r_proj_out_dve"), sem("r_proj_out_act")]
        passed = sem("pe_passed_wait")
        preset, ones_set = sem("preset"), sem("ones_set")
        cur_ready, raw_used = sem("cur_ready"), sem("raw_used")
        lora_mm, sig_ready = sem("r_lora_mm"), sem("sig_ready")
        k_mixed, k_squared, ksum_mm = sem("k_mixed"), sem("k_squared"), sem("ksum_mm")
        scanned, decay_ready = sem("scanned"), sem("decay_ready")
        clamped, rinv_ready = sem("clamped"), sem("rinv_ready")
        rk_ready, bonus_mm = sem("rk_ready"), sem("bonus_mm")
        feat_ready = sem("feat_ready")
        chain, achain = sem("r_dve_chain"), sem("r_act_chain")
        tok_turned, tok_out = sem("tok_turned"), sem("tok_out")
        mt_mm, mt_out = sem("mt_mm"), sem("mt_out")
        tt_first, t_turned, t_out = sem("tt_first"), sem("t_turned"), sem("t_out")
        x_mm, x_out = sem("x_mm"), sem("x_out")
        tn_mm, tn_out = sem("tn_mm"), sem("tn_out")
        ttn_mm, ttn_out = sem("ttn_mm"), sem("ttn_out")
        q_mm, q_out, wt_mm, wt_out = sem("q_mm"), sem("q_out"), sem("wt_mm"), sem("wt_out")
        u_mm, u_out, h_mm, h_out = sem("u_mm"), sem("u_out"), sem("h_mm"), sem("h_out")
        y_mm, y_out = sem("y_mm"), sem("y_out")
        mean_mm, centered, squared = sem("mean_mm"), sem("centered"), sem("squared")
        var_mm, rstd_ready = sem("var_mm"), sem("lnx_rstd")
        gate_mm, pair_done = sem("gate_mm"), sem("pair_done")
        NL, NC = len(LEVELS), S // CHUNK

        block = ctx.enter_context(nc.Block())
        wv = tile_cols(d["w_in"][0])

        @block.sync
        def _(sp):
            def load_lora_up(i):
                sp.wait_ge(gate_mm, 2 * i)
                sp.dma_start(lup[0:LORA, 0, :], d["rw_w2"][0, :, bass.ds(i * P, P)]).then_inc(lup_in, 16)
                sp.dma_start(lup[LORA:P, 0, :], d["rw_a2"][0, :, bass.ds(i * P, P)]).then_inc(lup_in, 16)
                sp.dma_start(lup[:, 1, :], d["rw_g2"][0, 0:P, bass.ds(i * P, P)]).then_inc(lup_in, 16)
                sp.dma_start(lup[0:32, 2, :], d["rw_g2"][0, P:GATE_LORA, bass.ds(i * P, P)]).then_inc(lup_in, 16)

            for j in range(3):
                sp.dma_start(W[:, j, :, :], wv[:, :, RW0 + j * D:RW0 + j * D + P]).then_inc(w_in[j], 16)
            with sp.Fori(0, PAIRS - 1) as i:
                load_lora_up(i)
                for j in range(3):
                    sp.wait_ge(proj_done[1], 3 * i + (j + 1))
                    sp.dma_start(W[:, j, :, :],
                                 wv[:, :, bass.ds(i * P + (RW0 + j * D + P), P)]).then_inc(w_in[j], 16)
            load_lora_up(PAIRS - 1)

        def part_bank(j, half):
            return ((0, 1), (6, 0), (0, 0))[j][half]

        def products(pe, n, first, count):
            for p in range(first, first + count):
                j, half, k = p // 16, p // 8 % 2, p % 8
                if k == 0:
                    if half == 0:
                        pe.wait_ge(w_in[j], 16 * n + 16)
                    if (j, half) == (0, 0):
                        pe.wait_ge(proj_out[1], 3 * n)
                    elif (j, half) == (1, 1):
                        pe.wait_ge(proj_out[0], 3 * n + 1)
                    elif (j, half) == (2, 0):
                        pe.wait_ge(proj_out[1], 3 * n + 2)
                    elif (j, half) == (2, 1):
                        pe.wait_ge(proj_out[0], 3 * n + 3)
                last = nc.tensor.matmul(PS[:, part_bank(j, half), :], W[:, j, k, :],
                                        m.xT[:, k, half * HALF:(half + 1) * HALF],
                                        start=k == 0, stop=k == KT - 1)
                if k == KT - 1:
                    last.then_inc(proj_done[half], 1)

        def copy_projection(eng, copy, n, j, half):
            eng.wait_ge(proj_done[half], 3 * n + j + 1)
            eng.wait_ge(raw_used, n)
            copy(nxt[j][:, 1 + half * HALF:1 + (half + 1) * HALF], PS[:, part_bank(j, half), :]).then_inc(
                proj_out[half], 1)

        def tensor_turn(pe, i, more):
            mm = nc.tensor.matmul

            def wait_apart(sem, value):
                pe.wait_ge(sem, value)
                pe.sem_inc(passed, 1)

            def fill(first, count):
                if more:
                    products(pe, i + 1, first, count)

            pe.wait_ge(lup_in, 64 * i + 64)
            for hh in range(2):
                tk = slice(hh * HALF, (hh + 1) * HALF)
                if hh == 0:
                    pe.wait_ge(pair_done, 2 * i)
                else:
                    pe.wait_ge(sig_ready, 2 * i + 1)
                mm(PS[:, 2, :], lup[0:LORA, 0, :], m.lora[0:LORA, tk], start=True, stop=True)
                mm(PS[:, 3, :], lup[LORA:P, 0, :], m.lora[LORA:P, tk], start=True,
                   stop=True).then_inc(lora_mm, 1)
                fill(12 * hh, 4)
                pe.wait_ge(k_squared, 2 * i + hh + 1)
                if hh:
                    pe.wait_ge(clamped, 2 * i + 1)
                mm(PS[:, 4, :], m.c(C_HSUM), t_q, start=True, stop=True).then_inc(ksum_mm, 1)
                fill(12 * hh + 4, 4)
                pe.wait_ge(rk_ready, 2 * i + hh + 1)
                if hh:
                    pe.wait_ge(feat_ready, 2 * i + 1)
                mm(PS[:, 5, :], m.c(C_HSUM), t_d, start=True, stop=True).then_inc(bonus_mm, 1)
                fill(12 * hh + 8, 4)
            def state_begin(g, l):
                n, s = G * i + g, g % 2
                if l == 0:
                    pe.wait_ge(q_out, n + 1)
                    pe.wait_ge(wt_out, n + 1)
                    pe.wait_ge(u_out, 4 * n)
                    if g == 0 and more:
                        pe.wait_ge(proj_out[0], 3 * i + 5)
                else:
                    pe.wait_ge(u_out, 4 * n + 2)
                for h in range(2):
                    q = 2 * l + h
                    mm(PS[:, 6 + h, 0:RW_HD], TT[s][:, q * P:(q + 1) * P], Tq[s][:, q * RW_HD:(q + 1) * RW_HD],
                       start=True, stop=False, skip_group_check=True)

            def state_u(g, l, cc):
                s, c = g % 2, 4 * g + 2 * l + cc
                rows = slice(64 * cc, 64 * cc + 64)
                wait_apart(h_out, NC * i + c)
                for h in range(2):
                    hr = slice(64 * h, 64 * h + 64)
                    last = mm(PS[rows, 6 + h, 0:RW_HD], WT[s][hr, l, 64 * cc:64 * cc + 64], H[hr, c % 4, :],
                              start=False, stop=True, skip_group_check=True)
                last.then_inc(u_mm, 1)
                for h in range(2):
                    hr = slice(64 * h, 64 * h + 64)
                    mm(PS[hr, 5, 0:RW_HD], tok[s][rows, l, 2, hr], tok[s][rows, l, 3, hr],
                       start=True, stop=False, skip_group_check=True)

            def state_h(g, l, cc):
                s, c = g % 2, 4 * g + 2 * l + cc
                rows = slice(64 * cc, 64 * cc + 64)
                wait_apart(u_out, NC * i + c + 1)
                for h in range(2):
                    hr = slice(64 * h, 64 * h + 64)
                    last = mm(PS[hr, 5, 0:RW_HD], tok[s][rows, l, 1, hr], U[rows, h, :],
                              start=False, stop=True, skip_group_check=True)
                last.then_inc(h_mm, 1)

            def outputs(g, l):
                s, t = g % 2, 2 * g + l
                if t:
                    pe.wait_ge(y_out, NT * i + t)
                for h in range(2):
                    q = 2 * l + h
                    hr = slice(64 * h, 64 * h + 64)
                    mm(PS[hr, 4, 0:P], U[:, h, :], MT[s][:, q, P:2 * P], start=True, stop=False,
                       skip_group_check=True)
                    mm(PS[hr, 4, 0:P], tok[s][:, l, 3, hr], MT[s][:, q, 3 * P:4 * P], start=False, stop=False,
                       skip_group_check=True)
                    for cc in range(2):
                        last = mm(PS[hr, 4, 64 * cc:64 * cc + 64], H[hr, (2 * t + cc) % 4, :],
                                  AR[hr, t, 1, 64 * cc:64 * cc + 64], start=False, stop=True,
                                  skip_group_check=True)
                last.then_inc(y_mm, 1)

            def state_step(g, step):
                if step == 8:
                    outputs(g, 1)
                    return
                l, cc = step // 4, step // 2 % 2
                if step == 4:
                    outputs(g, 0)
                if step % 4 == 0:
                    state_begin(g, l)
                if step % 2 == 0:
                    state_u(g, l, cc)
                else:
                    state_h(g, l, cc)

            for g in range(G):
                n, s = G * i + g, g % 2
                before = (lambda step: state_step(g - 1, step)) if g else (lambda step: None)
                p, end = [(24, 32, 35, 38)[g]], (32, 35, 38, 40)[g]

                def fill_one():
                    if p[0] < end:
                        fill(p[0], 1)
                        p[0] += 1

                if g == 0:
                    pe.wait_ge(feat_ready, 2 * i + 2)
                else:
                    pe.wait_ge(q_out, n)
                    pe.wait_ge(wt_out, n)
                for l in range(2):
                    t = 2 * g + l
                    for a, src in enumerate((AR[:, t, 0, :], Bt[:, t * P:(t + 1) * P],
                                             Kt[:, t * P:(t + 1) * P], V[:, t * P:(t + 1) * P])):
                        last = nc.tensor.transpose(PS[:, 2 + l, a * P:(a + 1) * P], src, m.c(C_IDENT))
                    last.then_inc(tok_turned, 1)
                before(0)
                for q in range(4):
                    l, h = q // 2, q % 2
                    t = 2 * g + l
                    rows = slice(64 * h, 64 * h + 64)
                    if q == 0:
                        pe.wait_ge(ttn_out, NL * n)
                        if g == 0 and more:
                            pe.wait_ge(proj_out[1], 3 * i + 4)
                    elif q < 3:
                        pe.wait_ge(tok_out, 2 * n + q)
                    else:
                        pe.wait_ge(mt_out, 4 * n + 1)
                    bank = (1, 2, 3, 1)[q]
                    mm(PS[:, bank, 0:2 * P], Bt[rows, t * P:(t + 1) * P], AR[rows, t, :, :],
                       start=True, stop=True)
                    mm(PS[:, bank, 2 * P:4 * P], Kt[rows, t * P:(t + 1) * P], AR[rows, t, :, :],
                       start=True, stop=True).then_inc(mt_mm, 1)
                    if q == 1:
                        before(1)
                before(2)
                fill_one()
                pe.wait_ge(tt_first, n + 1)
                for q in range(4):
                    last = nc.tensor.transpose(PS[:, 2, q * P:(q + 1) * P], TT[s][:, q * P:(q + 1) * P],
                                               m.c(C_IDENT))
                last.then_inc(t_turned, 1)
                before(3)
                fill_one()
                pe.wait_ge(t_out, n + 1)
                for lv in range(NL):
                    if lv:
                        pe.wait_ge(tn_out, (NL - 1) * n + lv)
                        pe.wait_ge(ttn_out, NL * n + lv)
                    for q in range(4):
                        last = mm(PS[:, 3, q * P:(q + 1) * P], MT[s][:, q, 0:P], T[:, q * P:(q + 1) * P],
                                  start=True, stop=True)
                    last.then_inc(x_mm, 1)
                    if lv in (0, 2):
                        before((4, None, 7)[lv])
                    if g == 0 or lv:
                        fill_one()
                    pe.wait_ge(x_out, NL * n + lv + 1)
                    if lv < NL - 1:
                        for q in range(4):
                            c = slice(q * P, (q + 1) * P)
                            last = mm(PS[:, 2, c], TT[s][:, c], X[:, c], start=True, stop=True)
                        last.then_inc(tn_mm, 1)
                    for q in range(4):
                        c = slice(q * P, (q + 1) * P)
                        last = mm(PS[:, 1, c], X[:, c], TT[s][:, c], start=True, stop=True)
                    last.then_inc(ttn_mm, 1)
                    if lv < 3:
                        before((5, 6, 8)[lv])
                    if lv == 3:
                        fill_one()
                for q in range(4):
                    last = mm(PS[:, 2, q * RW_HD:(q + 1) * RW_HD], MT[s][:, q, 2 * P:3 * P],
                              tok[s][:, q // 2, 3, q % 2 * 64:q % 2 * 64 + 64], start=True, stop=True)
                last.then_inc(q_mm, 1)
                pe.wait_ge(ttn_out, NL * n + NL)
                for q in range(4):
                    l, h = q // 2, q % 2
                    last = mm(PS[64 * h:64 * h + 64, 3, l * P:(l + 1) * P], tok[s][:, l, 0, 64 * h:64 * h + 64],
                              TT[s][:, q * P:(q + 1) * P], start=True, stop=True)
                last.then_inc(wt_mm, 1)
            for step in range(9):
                if step:
                    fill(39 + step, 1)
                state_step(G - 1, step)
            pe.wait_ge(y_out, NT * i + NT)
            for hh in range(2):
                mm(PS[:, 2 + hh, :], m.c(C_HMEAN), AR[:, 4 * hh:4 * hh + 4, 0, :], start=True,
                   stop=True).then_inc(mean_mm, 1)
            for hh in range(2):
                tk = slice(hh * HALF, (hh + 1) * HALF)
                mm(PS[:, 6 + hh, :], lup[:, 1, :], m.gd1[:, tk], start=True, stop=False)
                mm(PS[:, 6 + hh, :], lup[0:32, 2, :], m.gd2[0:32, tk], start=False,
                   stop=True).then_inc(gate_mm, 1)
            pe.wait_ge(h_out, NC * i + NC)
            for hh in range(2):
                pe.wait_ge(squared, 2 * i + hh + 1)
                mm(PS[:, 4 + hh, :], m.c(C_HMEAN), work[:, (2 + hh) * HALF:(3 + hh) * HALF], start=True,
                   stop=True).then_inc(var_mm, 1)

        def scalar_turn(act, i, more):
            a = nc.scalar
            chained = 2 + 2
            act.wait_ge(cur_ready, i + 1)
            for hh in range(2):
                act.wait_ge(lora_mm, 2 * i + hh + 1)
                if hh:
                    act.wait_ge(feat_ready, 2 * i + 1)
                a.activation(t_n, PS[:, 2, :], ACT.Sigmoid, bias=par["w0"])
                a.activation(t_a, PS[:, 3, :], ACT.Sigmoid, bias=par["a0"]).then_inc(sig_ready, 1)
                act.wait_ge(k_mixed, 2 * i + hh + 1)
                a.activation(t_q, t_k, ACT.Square, scale=par["k_k"]).then_inc(k_squared, 1)
                a.preload_act_table_set("natural_log_exp_and_others")
                act.wait_ge(scanned, 2 * i + hh + 1)
                a.activation(t_p[:, :, 1:1 + CHUNK], t_s.rearrange("p (c n) -> p c n", n=CHUNK), ACT.Exp,
                             scale=-DECAY)
                a.activation(t_ip, t_s, ACT.Exp, scale=DECAY).then_inc(decay_ready, 1)
                act.wait_ge(clamped, 2 * i + hh + 1)
                a.activation(t_n, t_n, ACT.Ln, scale=NORM_SCALE).then_inc(achain, 1)
                act.wait_ge(achain, chained * i + hh + 1)
                a.activation(t_n, t_n, ACT.Exp, scale=-0.5, bias=m.eps[:, 2:3]).then_inc(rinv_ready, 1)
            if more:
                copy_projection(act, a.copy, i + 1, 0, 1)
            def copy_u(g, c):
                cc, t = c % 2, 2 * g + c // 2
                rows = slice(64 * cc, 64 * cc + 64)
                act.wait_ge(u_mm, NC * i + 4 * g + c + 1)
                if cc == 0:
                    act.wait_ge(y_mm, NT * i + t)
                a.copy(U[rows, :, :], PS[rows, 6:8, 0:RW_HD]).then_inc(u_out, 1)

            def copy_y(t):
                act.wait_ge(y_mm, NT * i + t + 1)
                a.copy(AR[:, t, 0, :], PS[:, 4, 0:P]).then_inc(y_out, 1)

            for g in range(G):
                n, s = G * i + g, g % 2
                for l in range(2):
                    act.wait_ge(tok_turned, 2 * n + l + 1)
                    if l == 0 and g >= 2:
                        act.wait_ge(y_mm, 2 * n - 2)
                    a.copy(tok[s][:, l, :, :].rearrange("p a n -> p (a n)"), PS[:, 2 + l, :]).then_inc(tok_out, 1)
                if more and g == 1:
                    copy_projection(act, a.copy, i + 1, 1, 1)
                if g:
                    copy_u(g - 1, 0)
                    copy_u(g - 1, 1)
                act.wait_ge(t_turned, n + 1)
                a.copy(T, PS[:, 2, :]).then_inc(t_out, 1)
                if g:
                    copy_y(2 * g - 2)
                    copy_u(g - 1, 2)
                    copy_u(g - 1, 3)
                    copy_y(2 * g - 1)
                act.wait_ge(q_mm, n + 1)
                a.copy(Tq[s], PS[:, 2, 0:4 * RW_HD]).then_inc(q_out, 1)
                act.wait_ge(wt_mm, n + 1)
                a.copy(WT[s].rearrange("p l n -> p (l n)"), PS[:, 3, 0:2 * P]).then_inc(wt_out, 1)
            copy_u(G - 1, 0)
            copy_u(G - 1, 1)
            copy_y(2 * G - 2)
            copy_u(G - 1, 2)
            copy_u(G - 1, 3)
            copy_y(2 * G - 1)
            if more:
                copy_projection(act, a.copy, i + 1, 2, 1)
            for hh in range(2):
                act.wait_ge(centered, 2 * i + hh + 1)
                a.activation(work[:, (2 + hh) * HALF:(3 + hh) * HALF], work[:, hh * HALF:(hh + 1) * HALF],
                             ACT.Square).then_inc(squared, 1)
            for hh in range(2):
                r = work[:, (2 + hh) * HALF:(3 + hh) * HALF]
                act.wait_ge(var_mm, 2 * i + hh + 1)
                a.activation(r, PS[:, 4 + hh, :], ACT.Ln, bias=m.eps[:, 1:2]).then_inc(achain, 1)
                act.wait_ge(achain, chained * i + 2 + hh + 1)
                a.activation(r, r, ACT.Exp, scale=-0.5).then_inc(rstd_ready, 1)

        def vector_turn(dve, i, more):
            v = nc.vector
            links = 2 + 27 + 4 + 16 + 4
            done = [0]

            def link(ins):
                done[0] += 1
                ins.then_inc(chain, 1)
                dve.wait_ge(chain, links * i + done[0])

            def tiles(x):
                return x.rearrange("p (t c n) -> p t c n", c=2, n=CHUNK)

            dve.wait_ge(sig_ready, 2 * i)
            link(v.tensor_copy(cur[:, :], m.tab1[:, 0:8 * len(PAIR_ROWS)].rearrange(
                "p (j t) -> p j t", t=8)[:, :, bass.ds(i, 1)].rearrange("p j a -> p (j a)")))
            link(v.tensor_scalar(negkk[:, :], par["k_k"], -1.0, None, ALU.mult))
            v.memset(H[:, 0, :], 0.0).then_inc(cur_ready, 1)
            dve.wait_ge(cur_ready, i + 1)
            dve.wait_ge(proj_out[0], 3 * i + 3)
            dve.wait_ge(proj_out[1], 3 * i + 3)
            for hh in range(2):
                t0 = hh * HALF
                tk = slice(t0, t0 + HALF)

                def mixed(j, mu, out):
                    link(v.tensor_tensor(t_d, nxt[j][:, t0:t0 + HALF], nxt[j][:, t0 + 1:t0 + 1 + HALF],
                                         ALU.subtract))
                    return v.scalar_tensor_tensor(out=out, in0=t_d, scalar=mu,
                                                  in1=nxt[j][:, t0 + 1:t0 + 1 + HALF], op0=ALU.mult, op1=ALU.add)

                mixed(1, par["mu_k"], t_k).then_inc(k_mixed, 1)
                dve.wait_ge(k_mixed, 2 * i + hh + 1)
                link(mixed(0, par["mu_r"], t_r))
                if hh == 0:
                    link(mixed(2, par["mu_v"], V[:, tk]))
                else:
                    mixed(2, par["mu_v"], V[:, tk]).then_inc(raw_used, 1)
                    dve.wait_ge(raw_used, i + 1)
                dve.wait_ge(sig_ready, 2 * i + hh + 1)
                v.tensor_tensor_scan(t_s, reset[:, :], t_n, 0.0, ALU.mult, ALU.add).then_inc(scanned, 1)
                dve.wait_ge(scanned, 2 * i + hh + 1)
                dve.wait_ge(ksum_mm, 2 * i + hh + 1)
                v.tensor_scalar(t_n, PS[:, 4, :], 1e-24, None, ALU.max).then_inc(clamped, 1)
                link(v.tensor_scalar(t_d, t_a, -1.0, par["k_a"], ALU.add, ALU.mult))
                dve.wait_ge(rinv_ready, 2 * i + hh + 1)
                link(v.scalar_tensor_tensor(out=t_q, in0=t_k, scalar=negkk[:, 0:1], in1=t_n, op0=ALU.mult,
                                            op1=ALU.mult))
                link(v.scalar_tensor_tensor(out=t_k, in0=t_d, scalar=1.0, in1=t_k, op0=ALU.add, op1=ALU.mult))
                v.scalar_tensor_tensor(out=t_d, in0=t_r, scalar=par["r_k"], in1=t_k, op0=ALU.mult,
                                       op1=ALU.mult).then_inc(rk_ready, 1)
                dve.wait_ge(decay_ready, 2 * i + hh + 1)
                link(v.tensor_tensor(AR[:, 4 * hh:4 * hh + 4, 0, :].rearrange("p t (c n) -> p t c n", n=CHUNK),
                                     tiles(t_q), t_p[:, :, 0:CHUNK].rearrange("p (t c) n -> p t c n", c=2), ALU.mult))
                link(v.tensor_tensor(AR[:, 4 * hh:4 * hh + 4, 1, :].rearrange("p t (c n) -> p t c n", n=CHUNK),
                                     tiles(t_r), t_p[:, :, 1:1 + CHUNK].rearrange("p (t c) n -> p t c n", c=2),
                                     ALU.mult))
                link(v.tensor_copy(pend[:, 8 * hh:8 * hh + 8], t_p[:, :, CHUNK]))
                link(v.tensor_tensor(Kt[:, tk], t_k, t_ip, ALU.mult))
                link(v.scalar_tensor_tensor(out=t_q, in0=t_q, scalar=-1.0, in1=t_a, op0=ALU.mult, op1=ALU.mult))
                link(v.tensor_tensor(Bt[:, tk], t_q, t_ip, ALU.mult))
                dve.wait_ge(bonus_mm, 2 * i + hh + 1)
                v.tensor_tensor(bon[:, tk], PS[:, 5, :], V[:, tk], ALU.mult).then_inc(feat_ready, 1)
                dve.wait_ge(feat_ready, 2 * i + hh + 1)
            if more:
                copy_projection(dve, v.tensor_copy, i + 1, 0, 0)
            four = [P, 4, P]

            def inst(x):
                return x.rearrange("p (q n) -> p q n", n=P)

            def new_state(c):
                link(v.tensor_scalar(HP[:, :], H[:, c % 4, :], pend[:, c:c + 1], None, ALU.mult))
                dve.wait_ge(h_mm, NC * i + c + 1)
                v.scalar_tensor_tensor(out=H[:, (c + 1) % 4, :], in0=PS[:, 5, 0:RW_HD],
                                       scalar=pend[:, c:c + 1], in1=HP[:, :], op0=ALU.mult,
                                       op1=ALU.add).then_inc(h_out, 1)
                dve.wait_ge(h_out, NC * i + c + 1)

            for g in range(G):
                n, s = G * i + g, g % 2
                for q in range(4):
                    dve.wait_ge(mt_mm, 4 * n + q + 1)
                    if q == 0 and g >= 2:
                        dve.wait_ge(y_mm, 2 * n - 2)
                    v.tensor_tensor(MT[s][:, q, :].rearrange("p (a n) -> p a n", a=2),
                                    PS[:, (1, 2, 3, 1)[q], :].rearrange("p (a n) -> p a n", a=2),
                                    m.c(C_STRICT, 2).unsqueeze(1).to_broadcast([P, 2, 2 * P]),
                                    ALU.mult).then_inc(mt_out, 1)
                    if q == 1 and g:
                        new_state(4 * g - 4)
                dve.wait_ge(mt_out, 4 * n + 4)
                link(v.tensor_tensor(inst(TT[s]), MT[s][:, :, 0:P], m.c(C_LEVEL1T).unsqueeze(1).to_broadcast(four),
                                     ALU.mult))
                v.tensor_tensor(inst(TT[s]), inst(TT[s]), m.c(C_IDENT).unsqueeze(1).to_broadcast(four),
                                ALU.add).then_inc(tt_first, 1)
                dve.wait_ge(tt_first, n + 1)
                if g:
                    new_state(4 * g - 3)
                elif more:
                    copy_projection(dve, v.tensor_copy, i + 1, 1, 0)
                for lv in range(NL):
                    dve.wait_ge(x_mm, NL * n + lv + 1)
                    v.tensor_tensor(inst(X), inst(PS[:, 3, :]),
                                    m.c(C_LEVEL + lv).unsqueeze(1).to_broadcast(four), ALU.mult).then_inc(x_out, 1)
                    if g and lv in (1, 3):
                        new_state(4 * g - 2 + lv // 2)
                    if lv < NL - 1:
                        dve.wait_ge(tn_mm, (NL - 1) * n + lv + 1)
                        dve.wait_ge(t_out, n + 1)
                        v.tensor_tensor(T, PS[:, 2, :], T, ALU.add).then_inc(tn_out, 1)
                        dve.wait_ge(tn_out, (NL - 1) * n + lv + 1)
                    dve.wait_ge(ttn_mm, NL * n + lv + 1)
                    v.tensor_tensor(TT[s], PS[:, 1, :], TT[s], ALU.add).then_inc(ttn_out, 1)
                    dve.wait_ge(ttn_out, NL * n + lv + 1)
            if more:
                copy_projection(dve, v.tensor_copy, i + 1, 2, 0)
            for c in range(NC - 4, NC):
                new_state(c)
            for hh in range(2):
                yc = work[:, hh * HALF:(hh + 1) * HALF]
                dve.wait_ge(mean_mm, 2 * i + hh + 1)
                v.tensor_tensor(inst(yc), AR[:, 4 * hh:4 * hh + 4, 0, :], inst(PS[:, 2 + hh, :]),
                                ALU.subtract).then_inc(centered, 1)
            for hh in range(2):
                yc, r = work[:, hh * HALF:(hh + 1) * HALF], work[:, (2 + hh) * HALF:(3 + hh) * HALF]
                tk = slice(hh * HALF, (hh + 1) * HALF)
                dve.wait_ge(rstd_ready, 2 * i + hh + 1)
                link(v.scalar_tensor_tensor(out=yc, in0=yc, scalar=par["lnx_g"], in1=r, op0=ALU.mult, op1=ALU.mult))
                link(v.scalar_tensor_tensor(out=yc, in0=yc, scalar=par["lnx_b"], in1=bon[:, tk], op0=ALU.add,
                                            op1=ALU.add))
                dve.wait_ge(gate_mm, 2 * i + hh + 1)
                v.tensor_tensor(big[:, bass.ds(i + PAIRS, 1), tk].rearrange("p a n -> p (a n)"), yc,
                                PS[:, 6 + hh, :], ALU.mult).then_inc(pair_done, 1)
            assert done[0] == links, done

        @block.tensor
        def _(pe):
            products(pe, 0, 0, 48)
            with pe.Fori(0, PAIRS - 1) as i:
                tensor_turn(pe, i, True)
            tensor_turn(pe, PAIRS - 1, False)

        @block.scalar
        def _(act):
            for j in range(3):
                copy_projection(act, nc.scalar.copy, 0, j, 1)
            with act.Fori(0, PAIRS - 1) as i:
                scalar_turn(act, i, True)
            scalar_turn(act, PAIRS - 1, False)

        @block.vector
        def _(dve):
            dve.wait_ge(preset, 3)
            for j in range(3):
                copy_projection(dve, nc.vector.tensor_copy, 0, j, 0)
            with dve.Fori(0, PAIRS - 1) as i:
                vector_turn(dve, i, True)
            vector_turn(dve, PAIRS - 1, False)

        @block.gpsimd
        def _(pool):
            for j in range(3):
                last = nc.gpsimd.memset(nxt[j][:, 0:1], 0.0)
            last.then_inc(preset, 1)
            nc.gpsimd.memset(t_p[:, :, 0:1], 1.0).then_inc(preset, 1)
            nc.gpsimd.memset(reset[:, :], 1.0).then_inc(ones_set, 1)
            pool.wait_ge(ones_set, 1)
            nc.gpsimd.memset(reset[:, :].rearrange("p (c n) -> p c n", n=CHUNK)[:, :, 0:1], 0.0).then_inc(preset, 1)


class Split:
    COLS = 4 * P

    def __init__(self, nc, m, ctx, sem, prefix, raw_slots):
        def f32r(name, n):
            return ctx.enter_context(nc.sbuf_tensor(prefix + name, [P, 2, n], mybir.dt.float32r))

        self.nc, self.m, self.R = nc, m, raw_slots
        self.raw = m.wslot[:, :, :, :].rearrange("p a k n -> p (a k n)").rearrange("p (s n) -> p s n", n=self.COLS)
        self.xh, self.xl, self.wh, self.wl = f32r("xh", S), f32r("xl", S), f32r("wh", self.COLS), f32r("wl", self.COLS)
        self.w_in = [sem(f"w_in{j}") for j in range(raw_slots)]
        self.hi_out, self.lo_out, self.used = sem("hi_out"), sem("lo_out"), sem("step_done")
        self.filled = sem("filled")

    def raw_slot(self, s):
        return self.raw[:, s, :]

    def hi(self, act, x, n, slot, raw, turn):
        if not (isinstance(n, int) and n < 2):
            act.wait_ge(self.used, n - 1)
        self.nc.scalar.copy(self.xh[:, slot, :], x).then_inc(self.hi_out, 1)
        act.wait_ge(self.w_in[raw], 16 * turn + 16)
        self.nc.scalar.copy(self.wh[:, slot, :], self.raw_slot(raw)).then_inc(self.hi_out, 1)

    def lo(self, dve, x, n, slot, raw):
        v = self.nc.vector
        dve.wait_ge(self.hi_out, 2 * n + 1)
        v.tensor_tensor(self.xl[:, slot, :], x, self.xh[:, slot, :], ALU.subtract).then_inc(self.lo_out, 1)
        dve.wait_ge(self.hi_out, 2 * n + 2)
        v.tensor_tensor(self.wl[:, slot, :], self.raw_slot(raw), self.wh[:, slot, :],
                        ALU.subtract).then_inc(self.lo_out, 1)

    def step(self, pe, n, slot, first, last, bank_free=None):
        PS, mm = self.m.PS, self.nc.tensor.matmul
        pe.wait_ge(self.lo_out, 2 * n + 2)
        for c in range(4):
            if first and bank_free:
                bank_free(c)
            for half in range(2):
                wh, wl = (w[:, slot, c * P:(c + 1) * P] for w in (self.wh, self.wl))
                xh, xl = (x[:, slot, half * HALF:(half + 1) * HALF] for x in (self.xh, self.xl))
                out = PS[:, 2 * c + half, :]
                mm(out, wh, xh, start=first, stop=False)
                mm(out, wh, xl, start=False, stop=False)
                op = mm(out, wl, xh, start=False, stop=last)
                if last and (c, half) != (3, 1):
                    op.then_inc(self.filled, 1)
        op.then_inc(self.used, 1)

    def wait_filled(self, eng, g, c, nk=KT):
        if c < 3:
            eng.wait_ge(self.filled, 7 * g + (2 * c + 2))
        else:
            eng.wait_ge(self.used, nk * g + nk)


def merge_phase(nc, m, d):
    PS, big, xT = m.PS, m.big, m.xT
    with ExitStack() as ctx:
        sem = semaphores(nc, ctx)
        split = Split(nc, m, ctx, sem, "merge_", 4)
        sig = ctx.enter_context(nc.sbuf_tensor("gates", [P, 4, S], F32))
        sig_out = sem("gates_out")
        product_out, summed = sem("product_out"), sem("summed")
        block = ctx.enter_context(nc.Block())
        rows = lambda w: w.rearrange("(k p) n -> p k n", p=P)
        sources = [(rows(d["w_in"][0]), GATE0, xT, 0), (rows(d["w_da_proj"][0]), 0, big, 0),
                   (rows(d["w_in"][0]), GATE0 + D, xT, 0), (rows(d["w_rw_proj"][0]), 0, big, 8)]
        groups = [(w, c0 + cg * 4 * P, x, k0, j, cg) for cg in range(2) for j, (w, c0, x, k0) in enumerate(sources)]
        STEPS = KT * len(groups)

        @block.sync
        def _(sp):
            for n in range(STEPS):
                w, c0 = groups[n // KT][:2]
                if n >= 4:
                    sp.wait_ge(split.lo_out, 2 * n - 6)
                sp.dma_start(split.raw_slot(n % 4), w[:, n % KT, c0:c0 + 4 * P]).then_inc(split.w_in[n % 4], 16)

        def source(n):
            _, _, x, k0, _, _ = groups[n // KT]
            return x[:, k0 + n % KT, :]

        @block.tensor
        def _(pe):
            for g in range(len(groups)):
                for k in range(KT):
                    def bank_free(c):
                        if g == 0:
                            return
                        if g % 2:
                            pe.wait_ge(sig_out, 4 * (g // 2) + c + 1)
                        else:
                            pe.wait_ge(product_out, 4 * (g // 2 - 1) + c + 1)
                    split.step(pe, KT * g + k, k % 2, k == 0, k == KT - 1, bank_free)

        @block.scalar
        def _(act):
            for n in range(STEPS + 1):
                if n < STEPS:
                    split.hi(act, source(n), n, n % 2, n % 4, n // 4)
                if n and n % KT == 0 and (n // KT - 1) % 2 == 0:
                    g = n // KT - 1
                    for c in range(4):
                        split.wait_filled(act, g, c)
                        if g >= 2:
                            act.wait_ge(product_out, 4 * (g // 2 - 1) + c + 1)
                            act.wait_ge(summed, 4 * (g // 2 - 1) + c + 1)
                        nc.scalar.activation(sig[:, c, :].rearrange("p (h n) -> p h n", h=2),
                                             PS[:, 2 * c:2 * c + 2, :], ACT.Sigmoid).then_inc(sig_out, 1)

        @block.vector
        def _(dve):
            v = nc.vector
            for n in range(STEPS + 1):
                if n < STEPS:
                    split.lo(dve, source(n), n, n % 2, n % 4)
                if n and n % KT == 0 and (n // KT - 1) % 2 == 1:
                    g = n // KT - 1
                    for c in range(4):
                        split.wait_filled(dve, g, c)
                        dve.wait_ge(sig_out, 4 * (g // 2) + c + 1)
                        gate = sig[:, c, :].rearrange("p (h n) -> p h n", h=2)
                        v.tensor_tensor(gate, gate, PS[:, 2 * c:2 * c + 2, :], ALU.mult).then_inc(product_out, 1)
                    for c in range(4):
                        out = big[:, 16 + 4 * groups[g][5] + c, :]
                        dve.wait_ge(product_out, 4 * (g // 2) + c + 1)
                        if g % 4 == 1:
                            v.tensor_copy(out, sig[:, c, :]).then_inc(summed, 1)
                        else:
                            dve.wait_ge(summed, 4 * (g // 2 - 1) + c + 1)
                            v.tensor_tensor(out, out, sig[:, c, :], ALU.add).then_inc(summed, 1)
            dve.wait_ge(summed, 4 * (len(groups) // 2))


def out_norm_phase(nc, m, d, name, w_dram, src, nk, g_row, b_row):
    PS, xT = m.PS, m.xT
    with ExitStack() as ctx:
        sem = semaphores(nc, ctx, name + "_")
        split = Split(nc, m, ctx, sem, name + "_", 2)
        sq = ctx.enter_context(nc.sbuf_tensor(f"{name}_sq", [P, 2, HALF], F32))
        rstd = ctx.enter_context(nc.sbuf_tensor(f"{name}_rstd", [P, 2, HALF], F32))
        added = sem("added")
        mean_mm, centered, squared, var_mm = sem("mean_mm"), sem("centered"), sem("squared"), sem("var_mm")
        ln_out, rstd_out, scaled, normed = sem("ln_out"), sem("rstd_out"), sem("scaled"), sem("normed")
        block = ctx.enter_context(nc.Block())
        wv = w_dram.rearrange("(k p) n -> p k n", p=P)
        PAIRS_K = nk // 2

        @block.sync
        def _(sp):
            for g in range(2):
                cols = slice(g * 4 * P, (g + 1) * 4 * P)
                if g == 0:
                    for j in range(2):
                        sp.dma_start(split.raw_slot(j), wv[:, j, cols]).then_inc(split.w_in[j], 16)
                with sp.Fori(1 - g, PAIRS_K) as f:
                    for j in range(2):
                        sp.wait_ge(split.lo_out, 4 * f + (2 * (nk * g + j) - 2))
                        sp.dma_start(split.raw_slot(j), wv[:, bass.ds(2 * f + j, 1), cols].rearrange(
                            "p a n -> p (a n)")).then_inc(split.w_in[j], 16)

        def tile(k):
            return src[:, bass.ds(k, 1), :].rearrange("p a n -> p (a n)")

        @block.tensor
        def _(pe):
            for g in range(2):
                def bank_free(c):
                    if g:
                        pe.wait_ge(added, c + 1)
                split.step(pe, nk * g, 0, True, False, bank_free)
                split.step(pe, nk * g + 1, 1, False, False)
                with pe.Fori(1, PAIRS_K - 1) as f:
                    for j in range(2):
                        split.step(pe, 2 * f + (nk * g + j), j, False, False)
                split.step(pe, nk * g + nk - 2, 0, False, False)
                split.step(pe, nk * g + nk - 1, 1, False, True)
            pe.wait_ge(added, KT)
            for hh in range(2):
                for k in range(KT):
                    last = nc.tensor.matmul(PS[:, 4 + hh, :], m.c(C_MEAN), xT[:, k, hh * HALF:(hh + 1) * HALF],
                                            start=k == 0, stop=k == KT - 1)
                last.then_inc(mean_mm, 1)
            for hh in range(2):
                for k in range(KT):
                    n = KT * hh + k
                    pe.wait_ge(squared, n + 1)
                    nc.tensor.matmul(PS[:, 6 + hh, :], m.c(C_MEAN), sq[:, k % 2, :], start=k == 0,
                                     stop=k == KT - 1).then_inc(var_mm, 1)

        @block.vector
        def _(dve):
            v = nc.vector
            split.lo(dve, tile(0), 0, 0, 0)
            for g in range(2):
                n0 = nk * g
                with dve.Fori(0, PAIRS_K - 1) as f:
                    split.lo(dve, tile(2 * f + 1), 2 * f + (n0 + 1), 1, 1)
                    split.lo(dve, tile(2 * f + 2), 2 * f + (n0 + 2), 0, 0)
                split.lo(dve, tile(nk - 1), n0 + nk - 1, 1, 1)
                if g == 0:
                    split.lo(dve, tile(0), nk, 0, 0)
                for c in range(4):
                    x = xT[:, 4 * g + c, :].rearrange("p (h n) -> p h n", h=2)
                    split.wait_filled(dve, g, c, nk)
                    v.scalar_tensor_tensor(out=x, in0=x, scalar=ALPHA, in1=PS[:, 2 * c:2 * c + 2, :],
                                           op0=ALU.mult, op1=ALU.add).then_inc(added, 1)
            dve.wait_ge(added, KT)
            for hh in range(2):
                x = xT[:, :, hh * HALF:(hh + 1) * HALF]
                dve.wait_ge(mean_mm, hh + 1)
                for k in range(KT):
                    v.tensor_tensor(x[:, k, :], x[:, k, :], PS[:, 4 + hh, :], ALU.subtract).then_inc(centered, 1)
            for hh in range(2):
                dve.wait_ge(rstd_out, hh + 1)
                dve.wait_ge(centered, KT * (hh + 1))
                for k in range(KT):
                    x = xT[:, k, hh * HALF:(hh + 1) * HALF]
                    v.scalar_tensor_tensor(out=x, in0=x, scalar=m.tab2[:, g_row * 8 + k:g_row * 8 + k + 1],
                                           in1=rstd[:, hh, :], op0=ALU.mult, op1=ALU.mult).then_inc(scaled, 1)

        @block.scalar
        def _(act):
            a = nc.scalar
            a.preload_act_table_set("natural_log_exp_and_others")
            split.hi(act, tile(0), 0, 0, 0, 0)
            for g in range(2):
                n0 = nk * g
                with act.Fori(0, PAIRS_K - 1) as f:
                    split.hi(act, tile(2 * f + 1), 2 * f + (n0 + 1), 1, 1, f + n0 // 2)
                    split.hi(act, tile(2 * f + 2), 2 * f + (n0 + 2), 0, 0, f + (n0 // 2 + 1))
                split.hi(act, tile(nk - 1), n0 + nk - 1, 1, 1, (n0 + nk) // 2 - 1)
                if g == 0:
                    split.hi(act, tile(0), nk, 0, 0, nk // 2)
            for hh in range(2):
                for k in range(KT):
                    n = KT * hh + k
                    act.wait_ge(centered, n + 1)
                    if n >= 2:
                        act.wait_ge(var_mm, n - 1)
                    a.activation(sq[:, k % 2, :], xT[:, k, hh * HALF:(hh + 1) * HALF],
                                 ACT.Square).then_inc(squared, 1)
                act.wait_ge(var_mm, KT * (hh + 1))
                a.activation(rstd[:, hh, :], PS[:, 6 + hh, :], ACT.Ln, bias=m.eps[:, 0:1]).then_inc(ln_out, 1)
                act.wait_ge(ln_out, hh + 1)
                a.activation(rstd[:, hh, :], rstd[:, hh, :], ACT.Exp, scale=-0.5).then_inc(rstd_out, 1)
            for hh in range(2):
                for k in range(KT):
                    act.wait_ge(scaled, KT * hh + k + 1)
                    x = xT[:, k, hh * HALF:(hh + 1) * HALF]
                    a.activation(x, x, ACT.Identity,
                                 bias=m.tab2[:, b_row * 8 + k:b_row * 8 + k + 1]).then_inc(normed, 1)
            act.wait_ge(normed, 2 * KT)


def memory_phase(nc, m, d):
    PS, memT = m.PS, m.memT
    MT_ = MEM // P
    with ExitStack() as ctx:
        sem = semaphores(nc, ctx, "mem_")

        mem_in = ctx.enter_context(nc.sbuf_tensor("mem_tok", [P, MT_, D], F32))
        sq = ctx.enter_context(nc.sbuf_tensor("mem_sq", [P, KT, MEM], F32))
        rstd = ctx.enter_context(nc.sbuf_tensor("mem_rstd", [P, MEM], F32))
        loaded, turned, copied = sem("loaded"), sem("turned"), sem("copied")
        mean_mm, centered, squared, var_mm = sem("mean_mm"), sem("centered"), sem("squared"), sem("var_mm")
        ln_out, rstd_out, scaled, normed = sem("ln_out"), sem("rstd_out"), sem("scaled"), sem("normed")
        block = ctx.enter_context(nc.Block())

        @block.sync
        def _(sp):
            sp.dma_start(mem_in[:, :, :], d["mem"][0].rearrange("(t p) n -> p t n", p=P)).then_inc(loaded, 16)

        @block.tensor
        def _(pe):
            pe.wait_ge(loaded, 16)
            for t in range(MT_):
                for half in range(2):
                    for k in range(4):
                        last = nc.tensor.transpose(PS[:, 2 * t + half, k * P:(k + 1) * P],
                                                   mem_in[:, t, (4 * half + k) * P:(4 * half + k + 1) * P],
                                                   m.c(C_IDENT))
                    last.then_inc(turned, 1)
            pe.wait_ge(copied, 4)
            for k in range(KT):
                last = nc.tensor.matmul(PS[:, 4, 0:MEM], m.c(C_MEAN), memT[:, k, :], start=k == 0,
                                        stop=k == KT - 1)
            last.then_inc(mean_mm, 1)
            pe.wait_ge(squared, 1)
            for k in range(KT):
                last = nc.tensor.matmul(PS[:, 5, 0:MEM], m.c(C_MEAN), sq[:, k, :], start=k == 0,
                                        stop=k == KT - 1)
            last.then_inc(var_mm, 1)

        @block.vector
        def _(dve):
            v = nc.vector
            for t in range(MT_):
                for half in range(2):
                    dve.wait_ge(turned, 2 * t + half + 1)
                    v.tensor_copy(memT[:, 4 * half:4 * half + 4, t * P:(t + 1) * P],
                                  PS[:, 2 * t + half, :].rearrange("p (k t) -> p k t", k=4)).then_inc(copied, 1)
            dve.wait_ge(copied, 4)
            dve.wait_ge(mean_mm, 1)
            v.tensor_tensor(memT[:, :, :], memT[:, :, :],
                            PS[:, 4:5, 0:MEM].to_broadcast([P, KT, MEM]), ALU.subtract).then_inc(centered, 1)
            dve.wait_ge(centered, 1)
            dve.wait_ge(rstd_out, 1)
            for k in range(KT):
                v.scalar_tensor_tensor(out=memT[:, k, :], in0=memT[:, k, :],
                                       scalar=m.tab2[:, 48 + k:49 + k], in1=rstd[:, :], op0=ALU.mult,
                                       op1=ALU.mult).then_inc(scaled, 1)

        @block.scalar
        def _(act):
            a = nc.scalar
            a.preload_act_table_set("natural_log_exp_and_others")
            act.wait_ge(centered, 1)
            a.activation(sq[:, :, :], memT[:, :, :], ACT.Square).then_inc(squared, 1)
            act.wait_ge(var_mm, 1)
            a.activation(rstd[:, :], PS[:, 5, 0:MEM], ACT.Ln, bias=m.eps[:, 0:1]).then_inc(ln_out, 1)
            act.wait_ge(ln_out, 1)
            a.activation(rstd[:, :], rstd[:, :], ACT.Exp, scale=-0.5).then_inc(rstd_out, 1)
            for k in range(KT):
                act.wait_ge(scaled, k + 1)
                a.activation(memT[:, k, :], memT[:, k, :], ACT.Identity,
                             bias=m.tab2[:, 56 + k:57 + k]).then_inc(normed, 1)
            act.wait_ge(normed, KT)


def cross_phase(nc, m, d):
    PS, big, xT, memT = m.PS, m.big, m.xT, m.memT
    HT = CA_HD // P
    MT_ = MEM // P
    with ExitStack() as ctx:
        sem = semaphores(nc, ctx, "x_")

        W = [big[:, 8 + 2 * j:10 + 2 * j, :].rearrange("p a n -> p (a n)").rearrange(
            "p (k n) -> p k n", n=CA_HD) for j in range(3)]
        cq = big[:, 14:16, :]
        ck = big[:, 16, 0:HT * MEM].rearrange("p (t n) -> p t n", n=MEM)
        cv = big[:, 16, HT * MEM:2 * HT * MEM].rearrange("p (t n) -> p t n", n=CA_HD)
        prob = big[:, 17:19, :].rearrange("p a n -> p (a n)").rearrange("p (t n) -> p t n", n=MEM)
        probT = big[:, 19:21, :]
        stat = ctx.enter_context(nc.sbuf_tensor("x_stat", [P, 3, NT], F32))
        w_in = [sem(f"w_in{j}") for j in range(3)]
        q_mm, q_out = sem("q_mm"), sem("q_out")
        k_mm, k_out, v_mm, v_out = sem("k_mm"), sem("k_out"), sem("v_mm"), sem("v_out")
        s_mm, maxed, exped, normed = sem("s_mm"), sem("maxed"), sem("exped"), sem("normed")
        rec = sem("reciprocal")
        p_turned, p_out = sem("p_turned"), sem("p_out")
        o_mm, o_out = sem("o_mm"), sem("o_out")
        block = ctx.enter_context(nc.Block())
        views = [tile_cols(d["w_cq"][0]), tile_cols(d["w_ckv"][0]), tile_cols(d["w_ckv"][0])]

        @block.sync
        def _(sp):
            for j in range(3):
                c0 = D if j == 2 else 0
                sp.dma_start(W[j], views[j][:, :, c0:c0 + CA_HD]).then_inc(w_in[j], 16)
            with sp.Fori(1, CA_HEADS) as h:
                for j, (sm, per) in enumerate(((q_mm, 4), (k_mm, 1), (v_mm, 1))):
                    c0 = D if j == 2 else 0
                    sp.wait_ge(sm, per * h)
                    sp.dma_start(W[j], views[j][:, :, bass.ds(h * CA_HD + c0, CA_HD)]).then_inc(w_in[j], 16)

        @block.tensor
        def _(pe):
            mm = nc.tensor.matmul
            with pe.Fori(0, CA_HEADS) as h:
                pe.wait_ge(w_in[0], 16 * h + 16)
                pe.wait_ge(o_out, 4 * h)
                for n in range(4):
                    ft, half = n // 2, n % 2
                    for k in range(KT):
                        last = mm(PS[:, n, :], W[0][:, k, ft * P:(ft + 1) * P],
                                  xT[:, k, half * HALF:(half + 1) * HALF], start=k == 0, stop=k == KT - 1)
                    last.then_inc(q_mm, 1)
                pe.wait_ge(w_in[1], 16 * h + 16)
                pe.wait_ge(p_out, 4 * h)
                for ft in range(HT):
                    for k in range(KT):
                        last = mm(PS[:, 4, ft * MEM:(ft + 1) * MEM], W[1][:, k, ft * P:(ft + 1) * P],
                                  memT[:, k, :], start=k == 0, stop=k == KT - 1)
                last.then_inc(k_mm, 1)
                pe.wait_ge(w_in[2], 16 * h + 16)
                for mt in range(MT_):
                    for k in range(KT):
                        last = mm(PS[:, 5, mt * CA_HD:(mt + 1) * CA_HD], memT[:, k, mt * P:(mt + 1) * P],
                                  W[2][:, k, :], start=k == 0, stop=k == KT - 1)
                last.then_inc(v_mm, 1)
                pe.wait_ge(q_out, 4 * h + 4)
                pe.wait_ge(k_out, h + 1)
                for t in range(NT):
                    bank = (6, 7, 4, 5)[t // 2]
                    if t == 6:
                        pe.wait_ge(v_out, h + 1)
                    for ft in range(HT):
                        last = mm(PS[:, bank, t % 2 * MEM:(t % 2 + 1) * MEM], cq[:, ft, t * P:(t + 1) * P],
                                  ck[:, ft, :], start=ft == 0, stop=ft == HT - 1)
                    last.then_inc(s_mm, 1)
                pe.wait_ge(exped, NT * h + NT)
                for half in range(2):
                    pe.wait_ge(normed, NT * h + 4 * half + 4)
                    for mt in range(MT_):
                        for t in range(4):
                            last = nc.tensor.transpose(PS[:, 4 + 2 * half + mt, t * P:(t + 1) * P],
                                                       prob[:, 4 * half + t, mt * P:(mt + 1) * P], m.c(C_IDENT))
                        last.then_inc(p_turned, 1)
                pe.wait_ge(p_out, 4 * h + 4)
                pe.wait_ge(v_out, h + 1)
                for n in range(4):
                    ft, half = n // 2, n % 2
                    for mt in range(MT_):
                        last = mm(PS[:, n, :], cv[:, mt, ft * P:(ft + 1) * P],
                                  probT[:, mt, half * HALF:(half + 1) * HALF], start=mt == 0, stop=mt == MT_ - 1)
                    last.then_inc(o_mm, 1)

        @block.scalar
        def _(act):
            a = nc.scalar
            a.preload_act_table_set("natural_log_exp_and_others")
            with act.Fori(0, CA_HEADS) as h:
                for n in range(4):
                    act.wait_ge(q_mm, 4 * h + n + 1)
                    act.wait_ge(s_mm, NT * h)
                    a.mul(cq[:, n // 2, n % 2 * HALF:(n % 2 + 1) * HALF], PS[:, n, :],
                          CA_HD ** -0.5).then_inc(q_out, 1)
                for t in range(NT):
                    bank = (6, 7, 4, 5)[t // 2]
                    act.wait_ge(maxed, NT // 2 * h + t // 2 + 1)
                    act.wait_ge(p_turned, 4 * h)
                    a.activation(prob[:, t, :], PS[:, bank, t % 2 * MEM:(t % 2 + 1) * MEM], ACT.Exp,
                                 bias=stat[:, 0, t:t + 1], accum_out=stat[:, 1, t:t + 1]).then_inc(exped, 1)
                for n in range(4):
                    half, mt = n // 2, n % 2
                    act.wait_ge(p_turned, 4 * h + n + 1)
                    act.wait_ge(o_mm, 4 * h)
                    a.copy(probT[:, mt, half * HALF:(half + 1) * HALF], PS[:, 4 + n, :]).then_inc(p_out, 1)

        @block.vector
        def _(dve):
            v = nc.vector
            with dve.Fori(0, CA_HEADS) as h:
                dve.wait_ge(k_mm, h + 1)
                dve.wait_ge(s_mm, NT * h)
                v.tensor_copy(ck.rearrange("p t n -> p (t n)"), PS[:, 4, :]).then_inc(k_out, 1)
                dve.wait_ge(v_mm, h + 1)
                v.tensor_copy(cv.rearrange("p t n -> p (t n)"), PS[:, 5, :]).then_inc(v_out, 1)
                for b in range(NT // 2):
                    dve.wait_ge(s_mm, NT * h + 2 * b + 2)
                    v.tensor_reduce(stat[:, 0, 2 * b:2 * b + 2],
                                    PS[:, (6, 7, 4, 5)[b], :].rearrange("p (t n) -> p t n", n=MEM), AX, ALU.max,
                                    negate=True).then_inc(maxed, 1)
                for t in range(NT):
                    dve.wait_ge(exped, NT * h + t + 1)
                    v.reciprocal(stat[:, 2, t:t + 1], stat[:, 1, t:t + 1]).then_inc(rec, 1)
                    dve.wait_ge(rec, NT * h + t + 1)
                    v.tensor_scalar(prob[:, t, :], prob[:, t, :], stat[:, 2, t:t + 1], None,
                                    ALU.mult).then_inc(normed, 1)
                for n in range(4):
                    ft, half = n // 2, n % 2
                    dve.wait_ge(o_mm, 4 * h + n + 1)
                    v.tensor_copy(big[:, bass.ds(HT * h + ft, 1), half * HALF:(half + 1) * HALF],
                                  PS[:, n:n + 1, :]).then_inc(o_out, 1)


def hidden_phase(nc, m, d):
    PS, big, xT = m.PS, m.big, m.xT
    GROUPS = FT // 2
    with ExitStack() as ctx:
        sem = semaphores(nc, ctx, "h_")
        split = Split(nc, m, ctx, sem, "hidden_", 4)
        act_buf = ctx.enter_context(nc.sbuf_tensor("silu", [P, 2, S], F32))
        silu_out, up_used = sem("silu_out"), sem("up_used")
        block = ctx.enter_context(nc.Block())
        wv = d["w_ffn_in"][0].rearrange("(k p) (u n) -> p k u n", p=P, u=2)

        @block.sync
        def _(sp):
            def load(g, k):
                c0 = g * (2 * P)
                cols = slice(c0, c0 + 2 * P) if isinstance(g, int) else bass.ds(c0, 2 * P)
                sp.dma_start(split.raw_slot(k % 4).rearrange("p (u n) -> p u n", u=2),
                             wv[:, k, :, cols]).then_inc(split.w_in[k % 4], 16)
            for k in range(4):
                load(0, k)
            for k in range(4, KT):
                sp.wait_ge(split.lo_out, 2 * k - 6)
                load(0, k)
            with sp.Fori(1, GROUPS) as g:
                for k in range(KT):
                    sp.wait_ge(split.lo_out, 2 * KT * g + (2 * k - 6))
                    load(g, k)

        @block.tensor
        def _(pe):
            with pe.Fori(0, GROUPS) as g:
                for k in range(KT):
                    def bank_free(c):
                        if c == 0:
                            pe.wait_ge(silu_out, 2 * g)
                        if c == 2:
                            pe.wait_ge(up_used, 2 * g)
                    split.step(pe, KT * g + k, k % 2, k == 0, k == KT - 1, bank_free)

        def for_groups(eng, halve, evacuate):
            halve(0, 0)
            with eng.Fori(0, GROUPS - 1) as g:
                for k in range(1, KT + 1):
                    halve(g, k)
                evacuate(g)
            for k in range(1, KT):
                halve(GROUPS - 1, k)
            evacuate(GROUPS - 1)

        @block.scalar
        def _(act):
            def halve(g, k):
                split.hi(act, xT[:, k % KT, :], KT * g + k, k % 2, k % 4, 2 * g + k // 4)

            def silu(g):
                for c in range(2):
                    split.wait_filled(act, g, c)
                    act.wait_ge(up_used, 2 * g + c)
                    nc.scalar.activation(act_buf[:, c, :].rearrange("p (h n) -> p h n", h=2),
                                         PS[:, 2 * c:2 * c + 2, :], ACT.Silu).then_inc(silu_out, 1)
            for_groups(act, halve, silu)

        @block.vector
        def _(dve):
            def halve(g, k):
                split.lo(dve, xT[:, k % KT, :], KT * g + k, k % 2, k % 4)

            def times_up(g):
                for c in range(2):
                    split.wait_filled(dve, g, c + 2)
                    dve.wait_ge(silu_out, 2 * g + c + 1)
                    nc.vector.tensor_tensor(big[:, bass.ds(2 * g + c, 1), :].rearrange("p a (h n) -> p (a h) n", h=2),
                                            act_buf[:, c, :].rearrange("p (h n) -> p h n", h=2),
                                            PS[:, 2 * c + 4:2 * c + 6, :], ALU.mult).then_inc(up_used, 1)
            for_groups(dve, halve, times_up)


def store_phase(nc, m, d):
    PS = m.PS
    with ExitStack() as ctx:
        sem = semaphores(nc, ctx, "o_")

        rows = m.big[:, 0:4, :]
        turned = sem("turned")
        copied = [sem("copied_dve"), sem("copied_act")]
        stored = [sem(f"stored{j}") for j in range(4)]
        block = ctx.enter_context(nc.Block())

        @block.tensor
        def _(pe):
            for t in range(NT):
                for half in range(2):
                    n = 2 * t + half
                    if n >= 8:
                        pe.wait_ge(copied[half], (n - 8) // 2 + 1)
                    for k in range(4):
                        last = nc.tensor.transpose(PS[:, n % 8, k * P:(k + 1) * P],
                                                   m.xT[:, 4 * half + k, t * P:(t + 1) * P], m.c(C_IDENT))
                    last.then_inc(turned, 1)

        def copy_out(eng, copy, half):
            for t in range(NT):
                n = 2 * t + half
                eng.wait_ge(turned, n + 1)
                if t >= 4:
                    eng.wait_ge(stored[t % 4], 16)
                copy(rows[:, t % 4, half * HALF:(half + 1) * HALF], PS[:, n % 8, :]).then_inc(copied[half], 1)

        @block.vector
        def _(dve):
            copy_out(dve, nc.vector.tensor_copy, 0)

        @block.scalar
        def _(act):
            copy_out(act, nc.scalar.copy, 1)

        @block.sync
        def _(sp):
            for t in range(NT):
                sp.wait_ge(copied[0], t + 1)
                sp.wait_ge(copied[1], t + 1)
                sp.dma_start(d["out"][0, t * P:(t + 1) * P, :], rows[:, t % 4, :]).then_inc(stored[t % 4], 16)
            for j in range(4):
                sp.wait_ge(stored[j], 32)


def layer(nc, d):
    with ExitStack() as ctx:
        m = Memory(nc, ctx)
        big = m.big
        setup_phase(nc, m, d)
        attention_phase(nc, m, d)
        rwkv_phase(nc, m, d)
        merge_phase(nc, m, d)
        out_norm_phase(nc, m, d, "mix", d["w_mix_out"][0], big[:, 16:24, :], KT, 0, 1)
        memory_phase(nc, m, d)
        cross_phase(nc, m, d)
        out_norm_phase(nc, m, d, "co", d["w_co"][0], big[:, 0:8, :], KT, 2, 3)
        hidden_phase(nc, m, d)
        out_norm_phase(nc, m, d, "ffn", d["w_ffn_out"][0], big[:, 0:FT, :], FT, 4, 5)
        store_phase(nc, m, d)


_INS = ['x', 'mem', 'rel_bias', 'w_in', 'shift_mu', 'lambda_q1', 'lambda_k1', 'lambda_q2', 'lambda_k2',
        'da_subln_g', 'w_da_proj', 'rw_w0', 'rw_w2', 'rw_a0', 'rw_a2', 'rw_g2', 'rw_k_k', 'rw_k_a', 'rw_r_k',
        'rw_lnx_g', 'rw_lnx_b', 'w_rw_proj', 'w_mix_out', 'ln1_g', 'ln1_b', 'mem_ln_g', 'mem_ln_b', 'w_cq',
        'w_ckv', 'w_co', 'ln2_g', 'ln2_b', 'w_ffn_in', 'w_ffn_out', 'ln3_g', 'ln3_b']


def kernel(**inputs):
    import numpy as _np
    import concourse.bacc as _bacc
    from concourse import mybir as _mybir
    from concourse.bass_utils import run_bass_kernel_spmd as _run

    nc = _bacc.Bacc("TRN2", target_bir_lowering=False, num_devices=1)
    arrays, d = {}, {}
    const, pick, future = shape_constants()
    for name, a in [(n, inputs[n]) for n in _INS] + [("const", const), ("pick", pick), ("future", future)]:
        a = _np.ascontiguousarray(a)
        arrays[f"in_{name}_dram"] = a
        d[name] = nc.dram_tensor(f"in_{name}_dram", a.shape, _mybir.dt.from_np(a.dtype), kind="ExternalInput").ap()
    d["out"] = nc.dram_tensor("out_0_dram", (1, S, D), F32, kind="ExternalOutput").ap()
    layer(nc, d)
    r = _run(nc, [arrays], core_ids=[0])
    return r.results[0]["out_0_dram"]
```

```python
import math
from contextlib import ExitStack

import numpy as np

import concourse.bass as bass
from concourse import mybir

P = 128
F32 = mybir.dt.float32
ALU = mybir.AluOpType
ACT = mybir.ActivationFunctionType
AX = mybir.AxisListType.X

D = 1024
S = 1024
KT = D // P
NT = S // P
HALF = S // 2
DA_HEADS, DA_HD = 8, 64
BUCKETS, MAX_DIST = 32, 128
RW_HD = 64
PAIRS = D // P
CHUNK = 64
LORA, GATE_LORA = 64, 160
RW0 = 3 * D
LW0 = RW0 + 3 * D
LG0 = LW0 + 2 * LORA
GATE0 = LG0 + GATE_LORA
MEM = 256
CA_HEADS, CA_HD = 4, 256
FF = 2816
FT = FF // P
ALPHA = 2.0 ** 0.25
LN_EPS = 1e-5
LNX_EPS = 64e-5
LAM_INIT = 0.8 - 0.6 * math.exp(0.0)
DECAY = math.exp(-0.5)
MASKED = -1e30
NORM_SCALE = 2.0 ** 20
NORM_SHIFT = 10 * math.log(2.0)

C_IDENT, C_FLIP, C_HSUM, C_HMEAN, C_MEAN, C_STRICT, C_INCL, C_LEVEL1T = range(8)
LEVELS = (2, 4, 8, 16, 32)
C_LEVEL = 8
N_CONST = C_LEVEL + len(LEVELS)
WIN = 3 * P

PAIR_ROWS = ("mu_r", "mu_k", "mu_v", "w0", "a0", "k_k", "k_a", "r_k", "lnx_g", "lnx_b")
LN_ROWS = ("ln1_g", "ln1_b", "ln2_g", "ln2_b", "ln3_g", "ln3_b", "mem_ln_g", "mem_ln_b")
R_SUBLN, R_MUW, R_MUG, R_MUG2 = 64, 65, 66, 67


def shape_constants():
    i = np.arange(P)[:, None]
    j = np.arange(P)[None, :]
    same_head = i // RW_HD == j // RW_HD
    same_chunk = i // CHUNK == j // CHUNK
    tiles = [i == j, i + j == P - 1, same_head, same_head / RW_HD, np.full((P, P), 1.0 / D),
             same_chunk & (i < j), same_chunk & (i <= j), (i % 2 == 0) & (j == i + 1)]
    for s in LEVELS:
        tiles.append(((i // s) % 2 == 1) & (j // s == i // s - 1))
    const = np.concatenate([np.asarray(t, np.float32) for t in tiles], axis=1)
    rel = 2 * P - 1 - np.arange(WIN)
    n = np.maximum(rel, 0)
    exact = BUCKETS // 2
    nf = np.maximum(n, 1).astype(np.float32)
    large = exact + (np.log(nf / np.float32(exact)) / np.float32(math.log(MAX_DIST / exact))
                     * np.float32(BUCKETS - exact)).astype(np.int32)
    bucket = np.where(n < exact, n, np.minimum(large, BUCKETS - 1))
    pick = (np.arange(BUCKETS)[:, None] == bucket[None, :]).astype(np.float32)
    pick[BUCKETS - 1] -= 1.0
    future = np.where(rel < 0, np.float32(MASKED), np.float32(0.0))[None, :].repeat(DA_HEADS, 0)
    return const, pick, np.ascontiguousarray(future, np.float32)


class Memory:

    def __init__(self, nc, ctx):
        def sb(name, shape):
            return ctx.enter_context(nc.sbuf_tensor(name, shape, F32))

        self.PS = ctx.enter_context(nc.psum_tensor("PS", [P, 8, 512], F32))
        self.xT = sb("xT", [P, KT, S])
        self.big = sb("big", [P, 24, S])
        self.wslot = sb("wslot", [P, 4, KT, P])
        self.const = sb("const_sb", [P, N_CONST * P])
        self.tab1 = sb("tab1", [P, P])
        self.tab2 = sb("tab2", [P, P])
        self.subln = sb("subln", [P, 1])
        self.lam = sb("lam", [P, 1])
        self.neglam = sb("neglam", [P, 1])
        self.eps = sb("eps", [P, 3])
        self.lora = sb("lora", [P, S])
        self.gd1 = sb("gd1", [P, S])
        self.gd2 = sb("gd2", [32, S])
        self.bias = self.big[:, 22:24, :].rearrange("p a (h k) -> p (a h) k", k=2 * P)
        self.memT = self.big[:, 21:23, :].rearrange("p a n -> p (a n)").rearrange("p (k n) -> p k n", n=MEM)
        self.scratch = nc.dram_tensor("bias_rows", [DA_HEADS, WIN], F32, kind="Internal").ap()

    def take_raw(self, nc, ctx):
        self.raw = [ctx.enter_context(nc.sbuf_tensor(f"raw{j}", [P, 1 + S], F32)) for j in range(3)]

    def c(self, n, count=1):
        return self.const[:, n * P:(n + count) * P]


def semaphores(nc, ctx, prefix=""):
    taken = []

    def sem(name):
        taken.append(nc.alloc_semaphore(name=prefix + name))
        return taken[-1]

    def clear():
        nc.clear_and_free_semaphores(taken)
        nc.all_engine_barrier()

    ctx.callback(clear)
    return sem


def tile_cols(w):
    return w.rearrange("(k p) n -> p k n", p=P)


def setup_phase(nc, m, d):
    xT, lora, gd1, gd2 = m.xT, m.lora, m.gd1, m.gd2
    PS, const = m.PS, m.const
    with ExitStack() as ctx:
        def sb(name, shape):
            return ctx.enter_context(nc.sbuf_tensor(name, shape, F32))

        sem = semaphores(nc, ctx)

        xin = sb("xin", [P, 2, D])
        rows1 = sb("rows1", [P, P])
        rows2 = sb("rows2", [P, P])
        wl = [sb("wl0", [P, KT, P]), sb("wl1", [P, KT, P]), sb("wl2", [P, KT, 32])]
        raw = sb("raw_lora", [P, 1 + S])
        lamv = sb("lamv", [P, 4, DA_HD])
        lprod = sb("lprod", [P, 2, DA_HD])
        lsum = sb("lsum", [P, 2])
        lexp = sb("lexp", [P, 2])
        rel = sb("rel", [BUCKETS, DA_HEADS])
        pick = sb("pick_sb", [BUCKETS, WIN])
        future = sb("future_sb", [DA_HEADS, WIN])
        frow = sb("frow", [DA_HEADS, WIN])
        grid = sb("grid", [P, DA_HEADS, 2 * P])
        diff = sb("diff", [P, S])

        const_in = sem("const_in")
        rows_zero = sem("rows_zero")
        rows_in = sem("rows_in")
        lam_in = sem("lam_in")
        rel_in = sem("rel_in")
        wl_in = [sem(f"wl_in{j}") for j in range(3)]
        x_in = [sem("x_in0"), sem("x_in1")]
        x_turned = sem("x_turned")
        x_out = [sem("x_out_dve"), sem("x_out_act")]
        tab_turned = sem("tab_turned")
        lora_mm = sem("lora_mm")
        raw_out = sem("raw_out")
        lora_out = sem("lora_out")
        lora_act = sem("lora_act")
        rel_mm = sem("rel_mm")
        frow_out = sem("frow_out")
        frow_stored = sem("frow_stored")
        grid_in = sem("grid_in")
        flip_mm = sem("flip_mm")
        lam_sum = sem("lam_sum")
        lam_exp = sem("lam_exp")
        chain = sem("setup_chain")

        block = ctx.enter_context(nc.Block())
        w_in = tile_cols(d["w_in"][0])
        vec_rows = dict(zip(PAIR_ROWS, [d["shift_mu"][0, 0:D], d["shift_mu"][0, D:2 * D],
                                        d["shift_mu"][0, 2 * D:3 * D], d["rw_w0"][0], d["rw_a0"][0],
                                        d["rw_k_k"][0], d["rw_k_a"][0],
                                        d["rw_r_k"][0].rearrange("h n -> (h n)"),
                                        d["rw_lnx_g"][0], d["rw_lnx_b"][0]]))

        @block.sync
        def _(sp):
            sp.dma_start(const[:, :], d["const"]).then_inc(const_in, 16)
            for t in range(NT):
                if t >= 2:
                    sp.wait_ge(x_turned, 2 * (t - 1))
                sp.dma_start(xin[:, t % 2, :], d["x"][0, t * P:(t + 1) * P, :]).then_inc(x_in[t % 2], 16)
                if t == 1:
                    sp.dma_start(wl[0][:, :, :], w_in[:, :, LW0:LG0]).then_inc(wl_in[0], 16)
                    sp.dma_start(wl[1][:, :, :], w_in[:, :, LG0:LG0 + P]).then_inc(wl_in[1], 16)
                    sp.dma_start(wl[2][:, :, :], w_in[:, :, LG0 + P:GATE0]).then_inc(wl_in[2], 16)
            sp.wait_ge(frow_out, 1)
            sp.dma_start(m.scratch, frow[:, :]).then_inc(frow_stored, 16)
            sp.wait_ge(frow_stored, 16)
            sp.dma_start(grid[:, :, :], bass.AP(tensor=m.scratch.tensor, offset=0,
                                                ap=[[1, P], [WIN, DA_HEADS], [1, 2 * P]])).then_inc(grid_in, 16)
            sp.wait_ge(grid_in, 16)

        @block.scalar
        def _(act):
            act.wait_ge(rows_zero, 2)
            for j, name in enumerate(PAIR_ROWS):
                act.dma_start(rows1[8 * j:8 * j + 8, :],
                              vec_rows[name].rearrange("(t p) -> t p", p=P)).then_inc(rows_in, 16)
            for j, name in enumerate(LN_ROWS):
                act.dma_start(rows2[8 * j:8 * j + 8, :],
                              d[name][0].rearrange("(t p) -> t p", p=P)).then_inc(rows_in, 16)
            mu = d["shift_mu"]
            act.dma_start(rows2[R_SUBLN:R_SUBLN + 1, :], d["da_subln_g"]).then_inc(rows_in, 16)
            act.dma_start(rows2[R_MUW:R_MUW + 1, :], mu[:, 3 * D:3 * D + P]).then_inc(rows_in, 16)
            act.dma_start(rows2[R_MUG:R_MUG + 1, :], mu[:, 3 * D + P:3 * D + 2 * P]).then_inc(rows_in, 16)
            act.dma_start(rows2[R_MUG2:R_MUG2 + 1, 0:32], mu[:, 3 * D + 2 * P:]).then_inc(rows_in, 16)
            for j, name in enumerate(("lambda_q1", "lambda_k1", "lambda_q2", "lambda_k2")):
                act.dma_start(lamv[:, j, :], d[name][0].partition_broadcast(P)).then_inc(lam_in, 16)
            act.dma_start(rel[:, :], d["rel_bias"]).then_inc(rel_in, 16)
            act.dma_start(pick[:, :], d["pick"]).then_inc(rel_in, 16)
            act.dma_start(future[:, :], d["future"]).then_inc(rel_in, 16)
            for t in range(NT):
                n = 2 * t + 1
                act.wait_ge(x_turned, n + 1)
                nc.scalar.copy(xT[:, 4:8, t * P:(t + 1) * P],
                               PS[:, n % 4, :].rearrange("p (k t) -> p k t", k=4)).then_inc(x_out[1], 1)
            act.wait_ge(lam_sum, 1)
            nc.scalar.activation(lexp[:, :], lsum[:, :], ACT.Exp).then_inc(lam_exp, 1)
            act.wait_ge(lora_out, 1)
            nc.scalar.activation(lora[0:LORA, :], lora[0:LORA, :], ACT.Tanh).then_inc(lora_act, 1)
            act.wait_ge(lora_out, 2)
            nc.scalar.activation(gd1[:, :], gd1[:, :], ACT.Sigmoid).then_inc(lora_act, 1)
            act.wait_ge(lora_out, 3)
            nc.scalar.activation(gd2[0:32, :], gd2[0:32, :], ACT.Sigmoid).then_inc(lora_act, 1)
            act.wait_ge(lora_act, 3)

        @block.tensor
        def _(pe):
            pe.wait_ge(const_in, 16)
            for t in range(NT):
                pe.wait_ge(x_in[t % 2], 16 * (t // 2 + 1))
                for half in range(2):
                    n = 2 * t + half
                    if n >= 4:
                        pe.wait_ge(x_out[n % 2], (n - 4) // 2 + 1)
                    for k in range(4):
                        f = 4 * half + k
                        last = nc.tensor.transpose(PS[:, n % 4, k * P:(k + 1) * P],
                                                   xin[:, t % 2, f * P:(f + 1) * P], m.c(C_IDENT))
                    last.then_inc(x_turned, 1)
            pe.wait_ge(rows_in, 16 * (len(PAIR_ROWS) + len(LN_ROWS) + 4))
            nc.tensor.transpose(PS[:, 4, 0:P], rows1[:, :], m.c(C_IDENT))
            nc.tensor.transpose(PS[:, 4, P:2 * P], rows2[:, :], m.c(C_IDENT)).then_inc(tab_turned, 1)
            pe.wait_ge(rel_in, 48)
            nc.tensor.matmul(PS[0:DA_HEADS, 5, 0:WIN], rel[:, :], pick[:, :], start=True,
                             stop=True).then_inc(rel_mm, 1)
            pe.wait_ge(x_out[0], NT)
            pe.wait_ge(x_out[1], NT)
            for j, rows in enumerate((P, P, 32)):
                pe.wait_ge(wl_in[j], 16)
                if j:
                    pe.wait_ge(raw_out, j)
                for h in range(2):
                    for k in range(KT):
                        last = nc.tensor.matmul(PS[0:rows, 6 + h, :], wl[j][:, k, :],
                                                xT[:, k, h * HALF:(h + 1) * HALF],
                                                start=k == 0, stop=k == KT - 1)
                last.then_inc(lora_mm, 1)
            pe.wait_ge(grid_in, 16)
            for h in range(DA_HEADS):
                last = nc.tensor.matmul(PS[:, h // 2, (h % 2) * 2 * P:(h % 2 + 1) * 2 * P], m.c(C_FLIP),
                                        grid[:, h, :], start=True, stop=True)
            last.then_inc(flip_mm, 1)

        @block.vector
        def _(dve):
            v = nc.vector
            steps = [0]

            def link(ins):
                steps[0] += 1
                ins.then_inc(chain, 1)
                dve.wait_ge(chain, steps[0])

            v.memset(rows1[:, :], 0.0).then_inc(rows_zero, 1)
            v.memset(rows2[:, :], 0.0).then_inc(rows_zero, 1)
            v.memset(m.eps[:, 0:1], LN_EPS)
            v.memset(m.eps[:, 1:2], LNX_EPS)
            v.memset(m.eps[:, 2:3], NORM_SHIFT)
            link(v.memset(raw[:, 0:1], 0.0))
            for t in range(NT):
                n = 2 * t
                dve.wait_ge(x_turned, n + 1)
                v.tensor_copy(xT[:, 0:4, t * P:(t + 1) * P],
                              PS[:, n % 4, :].rearrange("p (k t) -> p k t", k=4)).then_inc(x_out[0], 1)
            dve.wait_ge(tab_turned, 1)
            link(v.tensor_copy(m.tab1[:, :], PS[:, 4, 0:P]))
            link(v.tensor_copy(m.tab2[:, :], PS[:, 4, P:2 * P]))
            link(v.tensor_scalar(m.subln[:, :], m.tab2[:, R_SUBLN:R_SUBLN + 1], 1.0 - LAM_INIT, None, ALU.mult))
            dve.wait_ge(rel_mm, 1)
            v.tensor_tensor(frow[:, :], PS[0:DA_HEADS, 5, 0:WIN], future[:, :], ALU.add).then_inc(frow_out, 1)
            dve.wait_ge(lam_in, 64)
            link(v.tensor_tensor(lprod[:, :, :], lamv[:, 0:4:2, :], lamv[:, 1:4:2, :], ALU.mult))
            v.tensor_reduce(lsum[:, :], lprod[:, :, :], AX, ALU.add).then_inc(lam_sum, 1)
            dve.wait_ge(lam_exp, 1)
            link(v.tensor_tensor(m.lam[:, :], lexp[:, 0:1], lexp[:, 1:2], ALU.subtract))
            link(v.tensor_scalar(m.neglam[:, :], m.lam[:, :], LAM_INIT, -1.0, ALU.add, ALU.mult))
            for j, (dst, rows, row) in enumerate(((lora, P, R_MUW), (gd1, P, R_MUG), (gd2, 32, R_MUG2))):
                dve.wait_ge(lora_mm, j + 1)
                v.tensor_copy(raw[0:rows, 1:1 + HALF], PS[0:rows, 6, :])
                last = v.tensor_copy(raw[0:rows, 1 + HALF:1 + S], PS[0:rows, 7, :])
                last.then_inc(raw_out, 1)
                dve.wait_ge(raw_out, j + 1)
                link(v.tensor_tensor(diff[0:rows, :], raw[0:rows, 0:S], raw[0:rows, 1:1 + S], ALU.subtract))
                v.scalar_tensor_tensor(out=dst[0:rows, :], in0=diff[0:rows, :],
                                       scalar=m.tab2[0:rows, row:row + 1], in1=raw[0:rows, 1:1 + S],
                                       op0=ALU.mult, op1=ALU.add).then_inc(lora_out, 1)
                dve.wait_ge(lora_out, j + 1)
            dve.wait_ge(flip_mm, 1)
            for b in range(4):
                last = v.tensor_copy(m.bias[:, 2 * b:2 * b + 2, :],
                                     PS[:, b, :].rearrange("p (h k) -> p h k", h=2))
            link(last)


def attention_phase(nc, m, d):
    PS, big, W = m.PS, m.big, m.wslot
    nxt = [big[:, 8 + j, :] for j in range(3)]
    qT, kT = big[:, 11, :], big[:, 12, :]
    vtok = big[:, 13, :].rearrange("p (t c) -> p t c", c=P)
    prob = big[:, 14:16, :]
    attn = big[:, 16:18, :]
    attnT = big[:, 18:20, :]
    NQ = NT
    ring = []
    for qb in range(NQ):
        ring += [("T", qb, g) for g in range(qb // 4 + 1)]
        if qb:
            ring.append(("O", qb - 1, 0))
        ring.append(("V", qb, 0))
    ring.append(("O", NQ - 1, 0))
    place = {r: n for n, r in enumerate(ring)}
    N_RING = len(ring)
    assert N_RING % 2 == 0
    act_before = [sum(r[0] != "V" for r in ring[:n + 1]) for n in range(N_RING)]
    dve_before = [sum(r[0] == "V" for r in ring[:n + 1]) for n in range(N_RING)]
    PARTS = [(0,), (1,), (2,), (3, 4), (5, 6), (7, 8), (9, 10), (11,)]

    with ExitStack() as ctx:
        sem = semaphores(nc, ctx)

        small = ctx.enter_context(nc.sbuf_tensor("attn_small", [P, 12], F32))
        onorm = ctx.enter_context(nc.sbuf_tensor("onorm", [P, 2, P], F32))
        ojunk = ctx.enter_context(nc.sbuf_tensor("ojunk", [P, P], F32))
        nmax, lsum, rl = small[:, 0:2], small[:, 2:4], small[:, 4:6]
        ssq, lnv, rstd = small[:, 6:7], small[:, 7:8], small[:, 8:9]

        w_in = [sem(f"a_w_in{j}") for j in range(3)]
        proj_done = [sem("a_proj_lo"), sem("a_proj_hi")]
        proj_out = [sem("a_proj_out_dve"), sem("a_proj_out_act")]
        q_cur, k_cur = sem("q_cur"), sem("k_cur")
        v_turned, vtok_out = sem("v_turned"), sem("vtok_out")
        scores = sem("scores_ready")
        maxed = sem("max_ready")
        exped = sem("exp_ready")
        combined = sem("attn_ready")
        ring_full = sem("ring_full")
        ring_act, ring_dve = sem("ring_emptied_act"), sem("ring_emptied_dve")
        rstd_ready = sem("rstd_ready")
        dchain, achain = sem("a_dve_chain"), sem("a_act_chain")

        block = ctx.enter_context(nc.Block())
        wv = tile_cols(d["w_in"][0])

        @block.sync
        def _(sp):
            for j in range(3):
                sp.dma_start(W[:, j, :, :], wv[:, :, j * D:j * D + P]).then_inc(w_in[j], 16)
            with sp.Fori(0, DA_HEADS - 1) as i:
                for j in range(3):
                    sp.wait_ge(proj_done[1], 3 * i + (j + 1))
                    sp.dma_start(W[:, j, :, :],
                                 wv[:, :, bass.ds(i * P + (j * D + P), P)]).then_inc(w_in[j], 16)
            for j in range(3):
                sp.wait_ge(proj_done[1], 3 * (DA_HEADS - 1) + (j + 1))
                sp.dma_start(W[:, j, :, :], wv[:, :, RW0 + j * D:RW0 + j * D + P]).then_inc(w_in[j], 16)

        def project_part(pe, n, part):
            j, half, ks = part // 4, part // 2 % 2, part % 2
            if ks == 0:
                if half == 0:
                    pe.wait_ge(w_in[j], 16 * n + 16)
                pe.wait_ge(proj_out[half], 3 * n + j)
            for k in range(4 * ks, 4 * ks + 4):
                last = nc.tensor.matmul(PS[:, 6 + half, :], W[:, j, k, :],
                                        m.xT[:, k, half * HALF:(half + 1) * HALF],
                                        start=k == 0, stop=k == KT - 1)
            if ks == 1:
                last.then_inc(proj_done[half], 1)

        def copy_projection(eng, copy, n, j, half):
            eng.wait_ge(proj_done[half], 3 * n + j + 1)
            if j < 2:
                eng.wait_ge((q_cur, k_cur)[j], n)
            else:
                eng.wait_ge(v_turned, 2 * n)
            if isinstance(n, int) and n == DA_HEADS:
                out = m.raw[j][:, 1 + half * HALF:1 + (half + 1) * HALF]
            else:
                out = nxt[j][:, half * HALF:(half + 1) * HALF]
            copy(out, PS[:, 6 + half, :]).then_inc(proj_out[half], 1)

        def tensor_turn(pe, i):
            def width(qb):
                return (qb + 1) * P

            def score(qb):
                pe.wait_ge(exped, 16 * i + 2 * qb)
                for c in range(2):
                    for n0 in range(0, width(qb), 512):
                        w = min(512, width(qb) - n0)
                        last = nc.tensor.matmul(PS[:, 2 * c + n0 // 512, 0:w],
                                                qT[64 * c:64 * c + 64, qb * P:(qb + 1) * P],
                                                kT[64 * c:64 * c + 64, n0:n0 + w], start=True, stop=True)
                    last.then_inc(scores, 1)

            def ring_slot(r, act=0, dve=0):
                n = place[r]
                if n >= 2:
                    act, dve = max(act, act_before[n - 2]), max(dve, dve_before[n - 2])
                pe.wait_ge(ring_act, act_before[-1] * i + act)
                pe.wait_ge(ring_dve, dve_before[-1] * i + dve)
                return 4 + n % 2

            def turn_output(qb):
                bank = ring_slot(("O", qb, 0), dve=qb + 1)
                nc.tensor.transpose(PS[:, bank, 0:P], onorm[:, qb % 2, :], m.c(C_IDENT)).then_inc(ring_full, 1)

            pe.wait_ge(proj_out[0], 3 * i + 3)
            pe.wait_ge(proj_out[1], 3 * i + 3)
            for g in range(2):
                if g == 0:
                    pe.wait_ge(ring_act, act_before[-1] * i)
                for t in range(4):
                    last = nc.tensor.transpose(PS[:, 4 + g, t * P:(t + 1) * P],
                                               nxt[2][:, (4 * g + t) * P:(4 * g + t + 1) * P], m.c(C_IDENT))
                last.then_inc(v_turned, 1)
            pe.wait_ge(q_cur, i + 1)
            pe.wait_ge(k_cur, i + 1)
            score(0)
            pe.wait_ge(vtok_out, 2 * i + 2)
            score(1)
            for qb in range(NQ):
                for part in PARTS[qb]:
                    project_part(pe, i + 1, part)
                pe.wait_ge(combined, NQ * i + qb + 1)
                for g in range(qb // 4 + 1):
                    bank = ring_slot(("T", qb, g))
                    for t in range(4 * g, min(4 * g + 4, qb + 1)):
                        last = nc.tensor.transpose(PS[:, bank, (t % 4) * P:(t % 4 + 1) * P],
                                                   attn[:, qb % 2, t * P:(t + 1) * P], m.c(C_IDENT))
                    last.then_inc(ring_full, 1)
                if qb + 2 < NQ:
                    score(qb + 2)
                if qb:
                    turn_output(qb - 1)
                bank = ring_slot(("V", qb, 0), act=act_before[place[("T", qb, qb // 4)]])
                for t in range(qb + 1):
                    last = nc.tensor.matmul(PS[:, bank, 0:P], attnT[:, qb % 2, t * P:(t + 1) * P],
                                            vtok[:, t, :], start=t == 0, stop=t == qb)
                last.then_inc(ring_full, 1)
            turn_output(NQ - 1)

        def scalar_turn(act, i):
            def expo(qb):
                w = (qb + 1) * P
                for c in range(2):
                    act.wait_ge(maxed, 16 * i + 2 * qb + c + 1)
                    act.wait_ge(combined, NQ * i + qb)
                    nc.scalar.activation(prob[:, c, 0:w], PS[:, 2 * c:2 * c + 2, :].rearrange("p b n -> p (b n)")[:, 0:w],
                                         ACT.Exp, bias=nmax[:, c:c + 1],
                                         accum_out=lsum[:, c:c + 1]).then_inc(exped, 1)

            def output_out(qb):
                n = place[("O", qb, 0)]
                act.wait_ge(ring_full, N_RING * i + n + 1)
                nc.scalar.activation(big[:, bass.ds(i, 1), qb * P:(qb + 1) * P], PS[:, 4 + n % 2:5 + n % 2, 0:P],
                                     ACT.Copy, scale=m.subln[:, 0:1]).then_inc(ring_act, 1)

            act.wait_ge(proj_out[0], 3 * i + 3)
            act.wait_ge(proj_out[1], 3 * i + 3)
            nc.scalar.mul(qT[:, :], nxt[0][:, :], DA_HD ** -0.5).then_inc(q_cur, 1)
            for g in range(2):
                act.wait_ge(v_turned, 2 * i + g + 1)
                nc.scalar.copy(vtok[:, 4 * g:4 * g + 4, :].rearrange("p t c -> p (t c)"),
                               PS[:, 4 + g, :]).then_inc(vtok_out, 1)
            expo(0)
            for qb in range(NQ):
                if qb + 1 < NQ:
                    expo(qb + 1)
                for g in range(qb // 4 + 1):
                    n = place[("T", qb, g)]
                    act.wait_ge(ring_full, N_RING * i + n + 1)
                    t1 = min(4 * g + 4, qb + 1)
                    nc.scalar.copy(attnT[:, qb % 2, 4 * g * P:t1 * P],
                                   PS[:, 4 + n % 2, 0:(t1 - 4 * g) * P]).then_inc(ring_act, 1)
                if qb:
                    output_out(qb - 1)
                n = place[("V", qb, 0)]
                act.wait_ge(ring_full, N_RING * i + n + 1)
                act.wait_ge(ring_dve, dve_before[-1] * i + qb)
                nc.scalar.activation(ojunk[:, :], PS[:, 4 + n % 2, 0:P], ACT.Square,
                                     accum_out=ssq).then_inc(achain, 1)
                act.wait_ge(achain, 2 * NQ * i + 2 * qb + 1)
                nc.scalar.activation(lnv, ssq, ACT.Ln, bias=m.eps[:, 0:1], scale=1.0 / P).then_inc(achain, 1)
                act.wait_ge(achain, 2 * NQ * i + 2 * qb + 2)
                nc.scalar.activation(rstd, lnv, ACT.Exp, scale=-0.5).then_inc(rstd_ready, 1)
                for part in PARTS[qb]:
                    if part % 4 == 3:
                        copy_projection(act, nc.scalar.copy, i + 1, part // 4, 1)
            output_out(NQ - 1)

        def vector_turn(dve, i):
            v = nc.vector
            links = 3 * NQ + 2 * NQ
            done = [0]

            def link(ins):
                done[0] += 1
                ins.then_inc(dchain, 1)
                dve.wait_ge(dchain, links * i + done[0])

            def rowmax(qb):
                w = (qb + 1) * P
                wb = min(w, 2 * P)
                for c in range(2):
                    flat = PS[:, 2 * c:2 * c + 2, :].rearrange("p b n -> p (b n)")
                    dve.wait_ge(scores, 16 * i + 2 * qb + c + 1)
                    link(v.tensor_tensor(flat[:, w - wb:w], flat[:, w - wb:w],
                                         m.bias[:, bass.ds(i, 1), 2 * P - wb:2 * P].rearrange("p a n -> p (a n)"),
                                         ALU.add))
                    dve.wait_ge(exped, 16 * i + 2 * qb)
                    v.tensor_reduce(nmax[:, c:c + 1], flat[:, 0:w], AX, ALU.max,
                                    negate=True).then_inc(maxed, 1)

            dve.wait_ge(proj_out[0], 3 * i + 3)
            dve.wait_ge(proj_out[1], 3 * i + 3)
            v.tensor_copy(kT[:, :], nxt[1][:, :]).then_inc(k_cur, 1)
            rowmax(0)
            for qb in range(NQ):
                w = (qb + 1) * P
                dve.wait_ge(exped, 16 * i + 2 * qb + 2)
                link(v.reciprocal(rl, lsum))
                link(v.tensor_tensor(rl[:, 1:2], rl[:, 1:2], m.neglam[:, :], ALU.mult))
                link(v.tensor_scalar(prob[:, 1, 0:w], prob[:, 1, 0:w], rl[:, 1:2], None, ALU.mult))
                if qb >= 2:
                    dve.wait_ge(ring_full, N_RING * i + place[("T", qb - 2, (qb - 2) // 4)] + 1)
                v.scalar_tensor_tensor(out=attn[:, qb % 2, 0:w], in0=prob[:, 0, 0:w], scalar=rl[:, 0:1],
                                       in1=prob[:, 1, 0:w], op0=ALU.mult, op1=ALU.add).then_inc(combined, 1)
                if qb + 1 < NQ:
                    rowmax(qb + 1)
                n = place[("V", qb, 0)]
                dve.wait_ge(rstd_ready, NQ * i + qb + 1)
                if qb >= 2:
                    dve.wait_ge(ring_full, N_RING * i + place[("O", qb - 2, 0)] + 1)
                v.tensor_scalar(onorm[:, qb % 2, :], PS[:, 4 + n % 2, 0:P], rstd, None,
                                ALU.mult).then_inc(ring_dve, 1)
                for part in PARTS[qb]:
                    if part % 4 == 1:
                        copy_projection(dve, v.tensor_copy, i + 1, part // 4, 0)

        @block.tensor
        def _(pe):
            for part in range(12):
                project_part(pe, 0, part)
            with pe.Fori(0, DA_HEADS - 1) as i:
                tensor_turn(pe, i)
            tensor_turn(pe, DA_HEADS - 1)

        @block.scalar
        def _(act):
            nc.scalar.preload_act_table_set("natural_log_exp_and_others")
            for j in range(3):
                copy_projection(act, nc.scalar.copy, 0, j, 1)
            with act.Fori(0, DA_HEADS - 1) as i:
                scalar_turn(act, i)
            scalar_turn(act, DA_HEADS - 1)

        @block.vector
        def _(dve):
            for j in range(3):
                copy_projection(dve, nc.vector.tensor_copy, 0, j, 0)
            with dve.Fori(0, DA_HEADS - 1) as i:
                vector_turn(dve, i)
            vector_turn(dve, DA_HEADS - 1)


def rwkv_phase(nc, m, d):
    PS, big, W = m.PS, m.big, m.wslot
    G = NT // 2
    with ExitStack() as ctx:
        def sb(name, shape):
            return ctx.enter_context(nc.sbuf_tensor(name, shape, F32))

        sem = semaphores(nc, ctx)

        nxt = m.raw
        AR = big[:, 16:18, :].rearrange("p a n -> p (a n)").rearrange("p (t w n) -> p t w n", t=NT, w=2)
        Bt, Kt, V, bon = (big[:, 18 + j, :] for j in range(4))
        work = big[:, 22:24, :].rearrange("p a n -> p (a n)")
        more_work = sb("rw_work", [P, 5, HALF])
        t_r, t_k, t_s = (work[:, j * HALF:(j + 1) * HALF] for j in range(3))
        t_ip, t_q, t_n, t_d, t_a = (more_work[:, j, :] for j in range(5))
        t_p = sb("running_decay", [P, HALF // CHUNK, CHUNK + 1])
        MT = [x.rearrange("p (i n) -> p i n", i=4)
              for x in (work, sb("chunk_maps", [P, 4 * 4 * P])[:, :])]
        X = more_work[:, 2, :].rearrange("p (l n) -> p l n", l=2)
        TB = [x.rearrange("p k n -> p (k n)").rearrange("p (l n) -> p l n", l=2)
              for x in (more_work[:, 0:2, :], W[:, 3, :, :])]
        TT = [x[:, :, 2 * P:4 * P] for x in TB]
        QW = [more_work[:, 3 + j, :].rearrange("p (l n) -> p l n", l=2) for j in range(2)]
        tok2 = sb("tok", [P, 2, 2, 4, P])
        tok = [tok2[:, j] for j in range(2)]
        U = sb("U", [P, 2, RW_HD])
        H = sb("state", [P, 4, RW_HD])
        HP = sb("state_decayed", [P, RW_HD])
        pend = sb("chunk_decay", [P, S // CHUNK])
        reset = sb("reset", [P, HALF])
        cur = sb("cur_params", [P, len(PAIR_ROWS)])
        lnx = sb("lnx_params", [P, 2])
        keep = sb("one_minus_mu", [P, 3])
        negkk = sb("neg_k_k", [P, 1])
        lup = W[:, 3, 0:3, :]
        par = {name: cur[:, j:j + 1] for j, name in enumerate(PAIR_ROWS)}

        w_in = [sem(f"r_w_in{j}") for j in range(3)]
        decay_up_in, gate_up_in = sem("decay_up_in"), sem("gate_up_in")
        proj_done = [sem("r_proj_lo"), sem("r_proj_hi")]
        proj_out = [sem("r_proj_out_dve"), sem("r_proj_out_act")]
        passed, sp_passed = sem("pe_passed_wait"), sem("sp_passed_wait")
        preset, ones_set = sem("preset"), sem("ones_set")
        prev_scaled, cur_copied = sem("prev_scaled"), sem("cur_copied")
        cur_ready, raw_used = sem("cur_ready"), sem("raw_used")
        lora_mm, sig_ready = sem("r_lora_mm"), sem("sig_ready")
        k_mixed, k_squared, ksum_mm = sem("k_mixed"), sem("k_squared"), sem("ksum_mm")
        scanned, decay_ready = sem("scanned"), sem("decay_ready")
        clamped, rinv_ready = sem("clamped"), sem("rinv_ready")
        rk_ready, bonus_mm = sem("rk_ready"), sem("bonus_mm")
        feat_ready = sem("feat_ready")
        chain, achain = sem("r_dve_chain"), sem("r_act_chain")
        tok_turned, tok_out = sem("tok_turned"), sem("tok_out")
        mt_mm, mt_out = sem("mt_mm"), sem("mt_out")
        tt_first, t_turned, t_out = sem("tt_first"), sem("t_turned"), sem("t_out")
        x_mm, x_out = sem("x_mm"), sem("x_out")
        b_mm, b_out = sem("b_mm"), sem("b_out")
        qw_mm, qw_out = sem("qw_mm"), sem("qw_out")
        u_mm, u_out, h_mm, h_out = sem("u_mm"), sem("u_out"), sem("h_mm"), sem("h_out")
        y_mm, y_out = sem("y_mm"), sem("y_out")
        mean_mm, centered, squared = sem("mean_mm"), sem("centered"), sem("squared")
        var_mm, rstd_ready = sem("var_mm"), sem("lnx_rstd")
        gate_mm, pair_done = sem("gate_mm"), sem("pair_done")
        NL, NC = len(LEVELS), S // CHUNK

        block = ctx.enter_context(nc.Block())
        wv = tile_cols(d["w_in"][0])

        @block.sync
        def _(sp):
            def load_decay_up(cols):
                sp.dma_start(lup[0:LORA, 0, :], d["rw_w2"][0, :, cols]).then_inc(decay_up_in, 16)
                sp.dma_start(lup[LORA:P, 0, :], d["rw_a2"][0, :, cols]).then_inc(decay_up_in, 16)

            def load_gate_up(i):
                sp.wait_ge(y_mm, NT * i + NT)
                sp.sem_inc(sp_passed, 1)
                sp.dma_start(lup[:, 1, :], d["rw_g2"][0, 0:P, bass.ds(i * P, P)]).then_inc(gate_up_in, 16)
                sp.dma_start(lup[0:32, 2, :], d["rw_g2"][0, P:GATE_LORA, bass.ds(i * P, P)]).then_inc(gate_up_in, 16)

            load_decay_up(slice(0, P))
            with sp.Fori(0, PAIRS - 1) as i:
                for j in range(3):
                    sp.wait_ge(proj_done[1], 3 * i + (j + 1))
                    sp.dma_start(W[:, j, :, :],
                                 wv[:, :, bass.ds(i * P + (RW0 + j * D + P), P)]).then_inc(w_in[j], 16)
                load_gate_up(i)
                load_decay_up(bass.ds(i * P + P, P))
            load_gate_up(PAIRS - 1)

        def part_bank(j, half):
            return ((0, 1), (6, 0), (0, 0))[j][half]

        def products(pe, n, first, count):
            for p in range(first, first + count):
                j, half, k = p // 16, p // 8 % 2, p % 8
                if k == 0:
                    if half == 0:
                        pe.wait_ge(w_in[j], 16 * n)
                    if (j, half) == (0, 0):
                        pe.wait_ge(proj_out[1], 3 * n)
                    elif (j, half) == (1, 0):
                        pe.wait_ge(pair_done, 2 * n - 2)
                    elif (j, half) == (1, 1):
                        pe.wait_ge(proj_out[0], 3 * n + 1)
                    elif (j, half) == (2, 0):
                        pe.wait_ge(proj_out[1], 3 * n + 2)
                    elif (j, half) == (2, 1):
                        pe.wait_ge(proj_out[0], 3 * n + 3)
                last = nc.tensor.matmul(PS[:, part_bank(j, half), :], W[:, j, k, :],
                                        m.xT[:, k, half * HALF:(half + 1) * HALF],
                                        start=k == 0, stop=k == KT - 1)
                if k == KT - 1:
                    last.then_inc(proj_done[half], 1)

        def copy_projection(eng, copy, n, j, half):
            eng.wait_ge(proj_done[half], 3 * n + j + 1)
            eng.wait_ge(raw_used, n)
            copy(nxt[j][:, 1 + half * HALF:1 + (half + 1) * HALF], PS[:, part_bank(j, half), :]).then_inc(
                proj_out[half], 1)

        def lora_products(pe, n, hh):
            tk = slice(hh * HALF, (hh + 1) * HALF)
            if hh == 0:
                pe.wait_ge(decay_up_in, 32 * n + 32)
                pe.wait_ge(centered, 2 * n)
            else:
                pe.wait_ge(sig_ready, 2 * n + 1)
            nc.tensor.matmul(PS[:, 2, :], lup[0:LORA, 0, :], m.lora[0:LORA, tk], start=True, stop=True)
            nc.tensor.matmul(PS[:, 3, :], lup[LORA:P, 0, :], m.lora[LORA:P, tk], start=True,
                             stop=True).then_inc(lora_mm, 1)

        def tensor_turn(pe, i, more):
            mm = nc.tensor.matmul

            def wait_apart(sem, value):
                pe.wait_ge(sem, value)
                pe.sem_inc(passed, 1)

            def fill(first, count):
                if more:
                    products(pe, i + 1, first, count)

            for hh in range(2):
                if hh:
                    lora_products(pe, i, 1)
                fill(12 * hh, 4)
                pe.wait_ge(k_squared, 2 * i + hh + 1)
                if hh:
                    pe.wait_ge(clamped, 2 * i + 1)
                mm(PS[:, 4, :], m.c(C_HSUM), t_q, start=True, stop=True).then_inc(ksum_mm, 1)
                fill(12 * hh + 4, 4)
                pe.wait_ge(rk_ready, 2 * i + hh + 1)
                if hh:
                    pe.wait_ge(feat_ready, 2 * i + 1)
                mm(PS[:, 5, :], m.c(C_HSUM), t_d, start=True, stop=True).then_inc(bonus_mm, 1)
                fill(12 * hh + 8, 4)
            def state_begin(g, l):
                n, s = G * i + g, g % 2
                if l == 0:
                    pe.wait_ge(qw_out, 2 * n + 2)
                    pe.wait_ge(u_out, 4 * n)
                    if g == 0 and more:
                        pe.wait_ge(proj_out[0], 3 * i + 5)
                else:
                    pe.wait_ge(u_out, 4 * n + 2)
                for h in range(2):
                    mm(PS[:, 6 + h, 0:RW_HD], TT[s][:, l, h * P:(h + 1) * P], QW[s][:, l, h * RW_HD:(h + 1) * RW_HD],
                       start=True, stop=False, skip_group_check=True)

            def state_u(g, l, cc):
                s, c = g % 2, 4 * g + 2 * l + cc
                rows = slice(64 * cc, 64 * cc + 64)
                wait_apart(h_out, NC * i + c)
                for h in range(2):
                    hr = slice(64 * h, 64 * h + 64)
                    last = mm(PS[rows, 6 + h, 0:RW_HD], QW[s][hr, l, P + 64 * cc:P + 64 * cc + 64], H[hr, c % 4, :],
                              start=False, stop=True, skip_group_check=True)
                last.then_inc(u_mm, 1)
                for h in range(2):
                    hr = slice(64 * h, 64 * h + 64)
                    mm(PS[hr, 5, 0:RW_HD], tok[s][rows, l, 2, hr], tok[s][rows, l, 3, hr],
                       start=True, stop=False, skip_group_check=True)

            def state_h(g, l, cc):
                s, c = g % 2, 4 * g + 2 * l + cc
                rows = slice(64 * cc, 64 * cc + 64)
                wait_apart(u_out, NC * i + c + 1)
                for h in range(2):
                    hr = slice(64 * h, 64 * h + 64)
                    last = mm(PS[hr, 5, 0:RW_HD], tok[s][rows, l, 1, hr], U[rows, h, :],
                              start=False, stop=True, skip_group_check=True)
                last.then_inc(h_mm, 1)

            def outputs(g, l):
                s, t = g % 2, 2 * g + l
                if t:
                    pe.wait_ge(y_out, NT * i + t)
                for h in range(2):
                    q = 2 * l + h
                    hr = slice(64 * h, 64 * h + 64)
                    mm(PS[hr, 4, 0:P], U[:, h, :], MT[s][:, q, P:2 * P], start=True, stop=False,
                       skip_group_check=True)
                    mm(PS[hr, 4, 0:P], tok[s][:, l, 3, hr], MT[s][:, q, 3 * P:4 * P], start=False, stop=False,
                       skip_group_check=True)
                    for cc in range(2):
                        last = mm(PS[hr, 4, 64 * cc:64 * cc + 64], H[hr, (2 * t + cc) % 4, :],
                                  AR[hr, t, 1, 64 * cc:64 * cc + 64], start=False, stop=True,
                                  skip_group_check=True)
                last.then_inc(y_mm, 1)

            def state_step(g, step):
                if step == 8:
                    outputs(g, 1)
                    return
                l, cc = step // 4, step // 2 % 2
                if step == 4:
                    outputs(g, 0)
                if step % 4 == 0:
                    state_begin(g, l)
                if step % 2 == 0:
                    state_u(g, l, cc)
                else:
                    state_h(g, l, cc)

            for g in range(G):
                n, s = G * i + g, g % 2
                before = (lambda step: state_step(g - 1, step)) if g else (lambda step: None)
                p, end = [(24, 32, 35, 38)[g]], (32, 35, 38, 40)[g]

                def fill_one():
                    if p[0] < end:
                        fill(p[0], 1)
                        p[0] += 1

                if g == 0:
                    pe.wait_ge(feat_ready, 2 * i + 2)
                else:
                    pe.wait_ge(mt_out, 4 * n)
                for l in range(2):
                    t = 2 * g + l
                    if l:
                        pe.wait_ge(qw_out, 2 * n)
                    for a, src in enumerate((AR[:, t, 0, :], Bt[:, t * P:(t + 1) * P],
                                             Kt[:, t * P:(t + 1) * P], V[:, t * P:(t + 1) * P])):
                        last = nc.tensor.transpose(PS[:, 3 - l, a * P:(a + 1) * P], src, m.c(C_IDENT))
                    last.then_inc(tok_turned, 1)
                before(0)
                for q in range(4):
                    l, h = q // 2, q % 2
                    t = 2 * g + l
                    rows = slice(64 * h, 64 * h + 64)
                    if q == 0:
                        pe.wait_ge(qw_out, 2 * n)
                        if g == 0 and more:
                            pe.wait_ge(proj_out[1], 3 * i + 4)
                    elif q < 3:
                        pe.wait_ge(tok_out, 2 * n + q)
                    else:
                        pe.wait_ge(mt_out, 4 * n + 2)
                    bank = (1, 3, 2, 3)[q]
                    mm(PS[:, bank, 0:2 * P], Bt[rows, t * P:(t + 1) * P], AR[rows, t, :, :],
                       start=True, stop=True)
                    mm(PS[:, bank, 2 * P:4 * P], Kt[rows, t * P:(t + 1) * P], AR[rows, t, :, :],
                       start=True, stop=True).then_inc(mt_mm, 1)
                    if q == 1:
                        before(1)
                before(2)
                fill_one()
                for l in range(2):
                    pe.wait_ge(tt_first, 2 * n + l + 1)
                    for h in range(2):
                        last = nc.tensor.transpose(PS[:, 1 + l, h * P:(h + 1) * P], TT[s][:, l, h * P:(h + 1) * P],
                                                   m.c(C_IDENT))
                    last.then_inc(t_turned, 1)
                before(3)
                fill_one()
                for lv in range(NL):
                    for l in range(2):
                        if lv:
                            pe.wait_ge(b_out, 2 * NL * n + 2 * lv + (l - 1))
                        else:
                            pe.wait_ge(t_out, 2 * n + l + 1)
                        for h in range(2):
                            c = slice(h * P, (h + 1) * P)
                            last = mm(PS[:, 1 + l, c], MT[s][:, 2 * l + h, 0:P], TB[s][:, l, c], start=True, stop=True)
                        last.then_inc(x_mm, 1)
                    if lv in (0, 2):
                        before((4, None, 7)[lv])
                    if g == 0 or lv:
                        fill_one()
                    for l in range(2):
                        pe.wait_ge(x_out, 2 * NL * n + 2 * lv + l + 1)
                        if lv < NL - 1:
                            for h in range(2):
                                c = slice(h * P, (h + 1) * P)
                                mm(PS[:, 1 + l, c], TT[s][:, l, c], X[:, l, c], start=True, stop=True)
                        for h in range(2):
                            c = slice(h * P, (h + 1) * P)
                            last = mm(PS[:, 1 + l, 2 * P + h * P:2 * P + (h + 1) * P], X[:, l, c], TT[s][:, l, c],
                                      start=True, stop=True)
                        last.then_inc(b_mm, 1)
                    if lv < 3:
                        before((5, 6, 8)[lv])
                    if lv == 3:
                        fill_one()
                for l in range(2):
                    pe.wait_ge(b_out, 2 * NL * n + 2 * NL + (l - 1))
                    for h in range(2):
                        mm(PS[:, 1 + l, h * RW_HD:(h + 1) * RW_HD], MT[s][:, 2 * l + h, 2 * P:3 * P],
                           tok[s][:, l, 3, h * 64:h * 64 + 64], start=True, stop=True)
                    for h in range(2):
                        last = mm(PS[64 * h:64 * h + 64, 1 + l, P:2 * P], tok[s][:, l, 0, 64 * h:64 * h + 64],
                                  TT[s][:, l, h * P:(h + 1) * P], start=True, stop=True)
                    last.then_inc(qw_mm, 1)
            for step in range(9):
                if step:
                    fill(39 + step, 1)
                state_step(G - 1, step)
            pe.wait_ge(y_out, NT * i + NT)
            for hh in range(2):
                mm(PS[:, 2 + hh, :], m.c(C_HMEAN), AR[:, 4 * hh:4 * hh + 4, 0, :], start=True,
                   stop=True).then_inc(mean_mm, 1)
            pe.wait_ge(h_out, NC * i + NC)
            for hh in range(2):
                pe.wait_ge(squared, 2 * i + hh + 1)
                mm(PS[:, 4 + hh, :], m.c(C_HMEAN), work[:, (2 + hh) * HALF:(3 + hh) * HALF], start=True,
                   stop=True).then_inc(var_mm, 1)
            pe.wait_ge(gate_up_in, 32 * i + 32)
            for hh in range(2):
                tk = slice(hh * HALF, (hh + 1) * HALF)
                mm(PS[:, 6 + hh, :], lup[:, 1, :], m.gd1[:, tk], start=True, stop=False)
                mm(PS[:, 6 + hh, :], lup[0:32, 2, :], m.gd2[0:32, tk], start=False,
                   stop=True).then_inc(gate_mm, 1)
            if more:
                lora_products(pe, i + 1, 0)

        def scalar_turn(act, i, more):
            a = nc.scalar
            chained = 2 + 2
            for hh in range(2):
                def scaled_prev(j, mu, out):
                    a.activation(out, nxt[j][:, hh * HALF:(hh + 1) * HALF], ACT.Identity, scale=mu).then_inc(prev_scaled, 1)

                a.preload_act_table_set("sigmoid_and_others")
                if hh == 0:
                    act.wait_ge(proj_out[0], 3 * i + 3)
                    act.wait_ge(cur_ready, i + 1)
                scaled_prev(2, par["mu_v"], V[:, hh * HALF:(hh + 1) * HALF])
                act.wait_ge(lora_mm, 2 * i + hh + 1)
                if hh:
                    act.wait_ge(feat_ready, 2 * i + 1)
                a.activation(t_n, PS[:, 2, :], ACT.Sigmoid, bias=par["w0"])
                a.activation(t_a, PS[:, 3, :], ACT.Sigmoid, bias=par["a0"]).then_inc(sig_ready, 1)
                if hh == 0:
                    act.wait_ge(pair_done, 2 * i)
                scaled_prev(1, par["mu_k"], t_k)
                scaled_prev(0, par["mu_r"], t_r)
                act.wait_ge(k_mixed, 2 * i + hh + 1)
                a.activation(t_q, t_k, ACT.Square, scale=par["k_k"]).then_inc(k_squared, 1)
                a.preload_act_table_set("natural_log_exp_and_others")
                act.wait_ge(scanned, 2 * i + hh + 1)
                a.activation(t_p[:, :, 1:1 + CHUNK], t_s.rearrange("p (c n) -> p c n", n=CHUNK), ACT.Exp,
                             scale=-DECAY)
                a.activation(t_ip, t_s, ACT.Exp, scale=DECAY).then_inc(decay_ready, 1)
                act.wait_ge(clamped, 2 * i + hh + 1)
                a.activation(t_n, t_n, ACT.Ln, scale=NORM_SCALE).then_inc(achain, 1)
                act.wait_ge(achain, chained * i + hh + 1)
                a.activation(t_n, t_n, ACT.Exp, scale=-0.5, bias=m.eps[:, 2:3]).then_inc(rinv_ready, 1)
            if more:
                copy_projection(act, a.copy, i + 1, 0, 1)
            def copy_u(g, c):
                cc, t = c % 2, 2 * g + c // 2
                rows = slice(64 * cc, 64 * cc + 64)
                act.wait_ge(u_mm, NC * i + 4 * g + c + 1)
                if cc == 0:
                    act.wait_ge(y_mm, NT * i + t)
                a.copy(U[rows, :, :], PS[rows, 6:8, 0:RW_HD]).then_inc(u_out, 1)

            def copy_y(t):
                act.wait_ge(y_mm, NT * i + t + 1)
                a.copy(AR[:, t, 0, :], PS[:, 4, 0:P]).then_inc(y_out, 1)

            for g in range(G):
                n, s = G * i + g, g % 2
                for l in range(2):
                    act.wait_ge(tok_turned, 2 * n + l + 1)
                    if l == 0 and g >= 2:
                        act.wait_ge(y_mm, 2 * n - 2)
                    a.copy(tok[s][:, l, :, :].rearrange("p a n -> p (a n)"), PS[:, 3 - l, :]).then_inc(tok_out, 1)
                if more and g == 1:
                    copy_projection(act, a.copy, i + 1, 1, 1)
                if g:
                    copy_u(g - 1, 0)
                    copy_u(g - 1, 1)
                for l in range(2):
                    act.wait_ge(t_turned, 2 * n + l + 1)
                    a.copy(TB[s][:, l, 0:2 * P], PS[:, 1 + l, 0:2 * P]).then_inc(t_out, 1)
                if g:
                    copy_y(2 * g - 2)
                    copy_u(g - 1, 2)
                    copy_u(g - 1, 3)
                    copy_y(2 * g - 1)
                for l in range(2):
                    act.wait_ge(qw_mm, 2 * n + l + 1)
                    a.copy(QW[s][:, l, :], PS[:, 1 + l, 0:2 * P]).then_inc(qw_out, 1)
            copy_u(G - 1, 0)
            copy_u(G - 1, 1)
            copy_y(2 * G - 2)
            copy_u(G - 1, 2)
            copy_u(G - 1, 3)
            copy_y(2 * G - 1)
            if more:
                copy_projection(act, a.copy, i + 1, 2, 1)
            for hh in range(2):
                act.wait_ge(centered, 2 * i + hh + 1)
                a.activation(work[:, (2 + hh) * HALF:(3 + hh) * HALF], work[:, hh * HALF:(hh + 1) * HALF],
                             ACT.Square).then_inc(squared, 1)
            for hh in range(2):
                r = work[:, (2 + hh) * HALF:(3 + hh) * HALF]
                act.wait_ge(var_mm, 2 * i + hh + 1)
                a.activation(r, PS[:, 4 + hh, :], ACT.Ln, bias=m.eps[:, 1:2]).then_inc(achain, 1)
                act.wait_ge(achain, chained * i + 2 + hh + 1)
                a.activation(r, r, ACT.Exp, scale=-0.5).then_inc(rstd_ready, 1)

        def take_params(dve, n):
            v = nc.vector
            v.tensor_copy(cur[:, :], m.tab1[:, 0:8 * len(PAIR_ROWS)].rearrange(
                "p (j t) -> p j t", t=8)[:, :, bass.ds(n, 1)].rearrange("p j a -> p (j a)")).then_inc(cur_copied, 1)
            dve.wait_ge(cur_copied, n + 1)
            v.tensor_scalar(keep[:, :], cur[:, 0:3], -1.0, 1.0, ALU.mult, ALU.add)
            v.tensor_scalar(negkk[:, :], par["k_k"], -1.0, None, ALU.mult).then_inc(cur_ready, 1)

        def vector_turn(dve, i, more):
            v = nc.vector
            links = 2 + 21 + 8 + 16 + 4
            done = [0]

            def link(ins):
                done[0] += 1
                ins.then_inc(chain, 1)
                dve.wait_ge(chain, links * i + done[0])

            def tiles(x):
                return x.rearrange("p (t c n) -> p t c n", c=2, n=CHUNK)

            link(v.tensor_copy(lnx[:, :], m.tab1[:, 0:8 * len(PAIR_ROWS)].rearrange(
                "p (j t) -> p j t", t=8)[:, 8:10, bass.ds(i, 1)].rearrange("p j a -> p (j a)")))
            link(v.memset(H[:, 0, :], 0.0))
            dve.wait_ge(cur_ready, i + 1)
            dve.wait_ge(proj_out[1], 3 * i + 3)
            for hh in range(2):
                t0 = hh * HALF
                tk = slice(t0, t0 + HALF)

                def mixed(j, out, place):
                    dve.wait_ge(prev_scaled, 6 * i + 3 * hh + place)
                    return v.scalar_tensor_tensor(out=out, in0=nxt[j][:, t0 + 1:t0 + 1 + HALF],
                                                  scalar=keep[:, j:j + 1], in1=out, op0=ALU.mult, op1=ALU.add)

                link(mixed(2, V[:, tk], 1))
                mixed(1, t_k, 2).then_inc(k_mixed, 1)
                dve.wait_ge(k_mixed, 2 * i + hh + 1)
                if hh == 0:
                    link(mixed(0, t_r, 3))
                else:
                    mixed(0, t_r, 3).then_inc(raw_used, 1)
                    dve.wait_ge(raw_used, i + 1)
                dve.wait_ge(sig_ready, 2 * i + hh + 1)
                v.tensor_tensor_scan(t_s, reset[:, :], t_n, 0.0, ALU.mult, ALU.add).then_inc(scanned, 1)
                dve.wait_ge(scanned, 2 * i + hh + 1)
                dve.wait_ge(ksum_mm, 2 * i + hh + 1)
                v.tensor_scalar(t_n, PS[:, 4, :], 1e-24, None, ALU.max).then_inc(clamped, 1)
                link(v.tensor_scalar(t_d, t_a, -1.0, par["k_a"], ALU.add, ALU.mult))
                dve.wait_ge(rinv_ready, 2 * i + hh + 1)
                link(v.scalar_tensor_tensor(out=t_q, in0=t_k, scalar=negkk[:, 0:1], in1=t_n, op0=ALU.mult,
                                            op1=ALU.mult))
                link(v.scalar_tensor_tensor(out=t_k, in0=t_d, scalar=1.0, in1=t_k, op0=ALU.add, op1=ALU.mult))
                v.scalar_tensor_tensor(out=t_d, in0=t_r, scalar=par["r_k"], in1=t_k, op0=ALU.mult,
                                       op1=ALU.mult).then_inc(rk_ready, 1)
                dve.wait_ge(decay_ready, 2 * i + hh + 1)
                link(v.tensor_tensor(AR[:, 4 * hh:4 * hh + 4, 0, :].rearrange("p t (c n) -> p t c n", n=CHUNK),
                                     tiles(t_q), t_p[:, :, 0:CHUNK].rearrange("p (t c) n -> p t c n", c=2), ALU.mult))
                link(v.tensor_tensor(AR[:, 4 * hh:4 * hh + 4, 1, :].rearrange("p t (c n) -> p t c n", n=CHUNK),
                                     tiles(t_r), t_p[:, :, 1:1 + CHUNK].rearrange("p (t c) n -> p t c n", c=2),
                                     ALU.mult))
                link(v.tensor_copy(pend[:, 8 * hh:8 * hh + 8], t_p[:, :, CHUNK]))
                link(v.tensor_tensor(Kt[:, tk], t_k, t_ip, ALU.mult))
                link(v.scalar_tensor_tensor(out=t_q, in0=t_q, scalar=-1.0, in1=t_a, op0=ALU.mult, op1=ALU.mult))
                link(v.tensor_tensor(Bt[:, tk], t_q, t_ip, ALU.mult))
                dve.wait_ge(bonus_mm, 2 * i + hh + 1)
                v.tensor_tensor(bon[:, tk], PS[:, 5, :], V[:, tk], ALU.mult).then_inc(feat_ready, 1)
                dve.wait_ge(feat_ready, 2 * i + hh + 1)
            if more:
                copy_projection(dve, v.tensor_copy, i + 1, 0, 0)

            def inst(x):
                return x.rearrange("p (q n) -> p q n", n=P)

            def new_state(c):
                link(v.tensor_scalar(HP[:, :], H[:, c % 4, :], pend[:, c:c + 1], None, ALU.mult))
                dve.wait_ge(h_mm, NC * i + c + 1)
                v.scalar_tensor_tensor(out=H[:, (c + 1) % 4, :], in0=PS[:, 5, 0:RW_HD],
                                       scalar=pend[:, c:c + 1], in1=HP[:, :], op0=ALU.mult,
                                       op1=ALU.add).then_inc(h_out, 1)
                dve.wait_ge(h_out, NC * i + c + 1)

            for g in range(G):
                n, s = G * i + g, g % 2
                for q in range(4):
                    dve.wait_ge(mt_mm, 4 * n + q + 1)
                    if q == 0 and g >= 2:
                        dve.wait_ge(y_mm, 2 * n - 2)
                    v.tensor_tensor(MT[s][:, q, :].rearrange("p (a n) -> p a n", a=2),
                                    PS[:, (1, 3, 2, 3)[q], :].rearrange("p (a n) -> p a n", a=2),
                                    m.c(C_STRICT, 2).unsqueeze(1).to_broadcast([P, 2, 2 * P]),
                                    ALU.mult).then_inc(mt_out, 1)
                    if q == 1 and g:
                        new_state(4 * g - 4)
                for l in range(2):
                    dve.wait_ge(mt_out, 4 * n + 2 * l + 2)
                    first = TT[s][:, l, :].rearrange("p (h n) -> p h n", h=2)
                    link(v.tensor_tensor(first, MT[s][:, 2 * l:2 * l + 2, 0:P],
                                         m.c(C_LEVEL1T).unsqueeze(1).to_broadcast([P, 2, P]), ALU.mult))
                    v.tensor_tensor(first, first, m.c(C_IDENT).unsqueeze(1).to_broadcast([P, 2, P]),
                                    ALU.add).then_inc(tt_first, 1)
                    dve.wait_ge(tt_first, 2 * n + l + 1)
                if g:
                    new_state(4 * g - 3)
                elif more:
                    copy_projection(dve, v.tensor_copy, i + 1, 1, 0)
                for lv in range(NL):
                    for l in range(2):
                        dve.wait_ge(x_mm, 2 * NL * n + 2 * lv + l + 1)
                        v.tensor_tensor(X[:, l, :].rearrange("p (h n) -> p h n", h=2),
                                        PS[:, 1 + l, 0:2 * P].rearrange("p (h n) -> p h n", h=2),
                                        m.c(C_LEVEL + lv).unsqueeze(1).to_broadcast([P, 2, P]),
                                        ALU.mult).then_inc(x_out, 1)
                    if g and lv in (1, 3):
                        new_state(4 * g - 2 + lv // 2)
                    for l in range(2):
                        part = slice(0, 4 * P) if lv < NL - 1 else slice(2 * P, 4 * P)
                        dve.wait_ge(b_mm, 2 * NL * n + 2 * lv + l + 1)
                        dve.wait_ge(t_out, 2 * n + l + 1)
                        v.tensor_tensor(TB[s][:, l, part], PS[:, 1 + l, part], TB[s][:, l, part],
                                        ALU.add).then_inc(b_out, 1)
                        dve.wait_ge(b_out, 2 * NL * n + 2 * lv + l + 1)
            if more:
                copy_projection(dve, v.tensor_copy, i + 1, 2, 0)
            for c in range(NC - 4, NC):
                new_state(c)
            if more:
                take_params(dve, i + 1)
            for hh in range(2):
                yc = work[:, hh * HALF:(hh + 1) * HALF]
                dve.wait_ge(mean_mm, 2 * i + hh + 1)
                v.tensor_tensor(inst(yc), AR[:, 4 * hh:4 * hh + 4, 0, :], inst(PS[:, 2 + hh, :]),
                                ALU.subtract).then_inc(centered, 1)
            for hh in range(2):
                yc, r = work[:, hh * HALF:(hh + 1) * HALF], work[:, (2 + hh) * HALF:(3 + hh) * HALF]
                tk = slice(hh * HALF, (hh + 1) * HALF)
                dve.wait_ge(rstd_ready, 2 * i + hh + 1)
                link(v.scalar_tensor_tensor(out=yc, in0=yc, scalar=lnx[:, 0:1], in1=r, op0=ALU.mult, op1=ALU.mult))
                link(v.scalar_tensor_tensor(out=yc, in0=yc, scalar=lnx[:, 1:2], in1=bon[:, tk], op0=ALU.add,
                                            op1=ALU.add))
                dve.wait_ge(gate_mm, 2 * i + hh + 1)
                v.tensor_tensor(big[:, bass.ds(i + PAIRS, 1), tk].rearrange("p a n -> p (a n)"), yc,
                                PS[:, 6 + hh, :], ALU.mult).then_inc(pair_done, 1)
            assert done[0] == links, done

        @block.tensor
        def _(pe):
            for done in proj_done:
                pe.sem_inc(done, 3)
            lora_products(pe, 0, 0)
            with pe.Fori(0, PAIRS - 1) as i:
                tensor_turn(pe, i, True)
            tensor_turn(pe, PAIRS - 1, False)

        @block.scalar
        def _(act):
            act.wait_ge(preset, 3)
            act.sem_inc(proj_out[1], 3)
            with act.Fori(0, PAIRS - 1) as i:
                scalar_turn(act, i, True)
            scalar_turn(act, PAIRS - 1, False)

        @block.vector
        def _(dve):
            dve.wait_ge(preset, 3)
            take_params(dve, 0)
            dve.sem_inc(proj_out[0], 3)
            with dve.Fori(0, PAIRS - 1) as i:
                vector_turn(dve, i, True)
            vector_turn(dve, PAIRS - 1, False)

        @block.gpsimd
        def _(pool):
            for j in range(3):
                last = nc.gpsimd.memset(nxt[j][:, 0:1], 0.0)
            last.then_inc(preset, 1)
            nc.gpsimd.memset(t_p[:, :, 0:1], 1.0).then_inc(preset, 1)
            nc.gpsimd.memset(reset[:, :], 1.0).then_inc(ones_set, 1)
            pool.wait_ge(ones_set, 1)
            nc.gpsimd.memset(reset[:, :].rearrange("p (c n) -> p c n", n=CHUNK)[:, :, 0:1], 0.0).then_inc(preset, 1)


class Split:
    COLS = 4 * P

    def __init__(self, nc, m, ctx, sem, prefix, raw_slots):
        def f32r(name, n):
            return ctx.enter_context(nc.sbuf_tensor(prefix + name, [P, 2, n], mybir.dt.float32r))

        self.nc, self.m, self.R = nc, m, raw_slots
        self.raw = m.wslot[:, :, :, :].rearrange("p a k n -> p (a k n)").rearrange("p (s n) -> p s n", n=self.COLS)
        self.xh, self.xl, self.wh, self.wl = f32r("xh", S), f32r("xl", S), f32r("wh", self.COLS), f32r("wl", self.COLS)
        self.w_in = [sem(f"w_in{j}") for j in range(raw_slots)]
        self.hi_out, self.lo_out, self.used = sem("hi_out"), sem("lo_out"), sem("step_done")
        self.filled = sem("filled")

    def raw_slot(self, s):
        return self.raw[:, s, :]

    def hi(self, act, x, n, slot, raw, turn):
        if not (isinstance(n, int) and n < 2):
            act.wait_ge(self.used, n - 1)
        self.nc.scalar.copy(self.xh[:, slot, :], x).then_inc(self.hi_out, 1)
        act.wait_ge(self.w_in[raw], 16 * turn + 16)
        self.nc.scalar.copy(self.wh[:, slot, :], self.raw_slot(raw)).then_inc(self.hi_out, 1)

    def lo(self, dve, x, n, slot, raw):
        v = self.nc.vector
        dve.wait_ge(self.hi_out, 2 * n + 1)
        v.tensor_tensor(self.xl[:, slot, :], x, self.xh[:, slot, :], ALU.subtract).then_inc(self.lo_out, 1)
        dve.wait_ge(self.hi_out, 2 * n + 2)
        v.tensor_tensor(self.wl[:, slot, :], self.raw_slot(raw), self.wh[:, slot, :],
                        ALU.subtract).then_inc(self.lo_out, 1)

    def step(self, pe, n, slot, first, last, bank_free=None):
        PS, mm = self.m.PS, self.nc.tensor.matmul
        pe.wait_ge(self.lo_out, 2 * n + 2)
        for c in range(4):
            if first and bank_free:
                bank_free(c)
            for half in range(2):
                wh, wl = (w[:, slot, c * P:(c + 1) * P] for w in (self.wh, self.wl))
                xh, xl = (x[:, slot, half * HALF:(half + 1) * HALF] for x in (self.xh, self.xl))
                out = PS[:, 2 * c + half, :]
                mm(out, wh, xh, start=first, stop=False)
                mm(out, wh, xl, start=False, stop=False)
                op = mm(out, wl, xh, start=False, stop=last)
                if last and (c, half) != (3, 1):
                    op.then_inc(self.filled, 1)
        op.then_inc(self.used, 1)

    def wait_filled(self, eng, g, c, nk=KT):
        if c < 3:
            eng.wait_ge(self.filled, 7 * g + (2 * c + 2))
        else:
            eng.wait_ge(self.used, nk * g + nk)


def merge_phase(nc, m, d):
    PS, big, xT = m.PS, m.big, m.xT
    with ExitStack() as ctx:
        sem = semaphores(nc, ctx)
        split = Split(nc, m, ctx, sem, "merge_", 4)
        sig = ctx.enter_context(nc.sbuf_tensor("gates", [P, 4, S], F32))
        sig_out = sem("gates_out")
        product_out, summed = sem("product_out"), sem("summed")
        block = ctx.enter_context(nc.Block())
        rows = lambda w: w.rearrange("(k p) n -> p k n", p=P)
        sources = [(rows(d["w_in"][0]), GATE0, xT, 0), (rows(d["w_da_proj"][0]), 0, big, 0),
                   (rows(d["w_in"][0]), GATE0 + D, xT, 0), (rows(d["w_rw_proj"][0]), 0, big, 8)]
        groups = [(w, c0 + cg * 4 * P, x, k0, j, cg) for cg in range(2) for j, (w, c0, x, k0) in enumerate(sources)]
        STEPS = KT * len(groups)

        @block.sync
        def _(sp):
            for n in range(STEPS):
                w, c0 = groups[n // KT][:2]
                if n >= 4:
                    sp.wait_ge(split.lo_out, 2 * n - 6)
                sp.dma_start(split.raw_slot(n % 4), w[:, n % KT, c0:c0 + 4 * P]).then_inc(split.w_in[n % 4], 16)

        def source(n):
            _, _, x, k0, _, _ = groups[n // KT]
            return x[:, k0 + n % KT, :]

        @block.tensor
        def _(pe):
            for g in range(len(groups)):
                for k in range(KT):
                    def bank_free(c):
                        if g == 0:
                            return
                        if g % 2:
                            pe.wait_ge(sig_out, 4 * (g // 2) + c + 1)
                        else:
                            pe.wait_ge(product_out, 4 * (g // 2 - 1) + c + 1)
                    split.step(pe, KT * g + k, k % 2, k == 0, k == KT - 1, bank_free)

        @block.scalar
        def _(act):
            for n in range(STEPS + 1):
                if n < STEPS:
                    split.hi(act, source(n), n, n % 2, n % 4, n // 4)
                if n and n % KT == 0 and (n // KT - 1) % 2 == 0:
                    g = n // KT - 1
                    for c in range(4):
                        split.wait_filled(act, g, c)
                        if g >= 2:
                            act.wait_ge(product_out, 4 * (g // 2 - 1) + c + 1)
                            act.wait_ge(summed, 4 * (g // 2 - 1) + c + 1)
                        nc.scalar.activation(sig[:, c, :].rearrange("p (h n) -> p h n", h=2),
                                             PS[:, 2 * c:2 * c + 2, :], ACT.Sigmoid).then_inc(sig_out, 1)

        @block.vector
        def _(dve):
            v = nc.vector
            for n in range(STEPS + 1):
                if n < STEPS:
                    split.lo(dve, source(n), n, n % 2, n % 4)
                if n and n % KT == 0 and (n // KT - 1) % 2 == 1:
                    g = n // KT - 1
                    for c in range(4):
                        split.wait_filled(dve, g, c)
                        dve.wait_ge(sig_out, 4 * (g // 2) + c + 1)
                        gate = sig[:, c, :].rearrange("p (h n) -> p h n", h=2)
                        v.tensor_tensor(gate, gate, PS[:, 2 * c:2 * c + 2, :], ALU.mult).then_inc(product_out, 1)
                    for c in range(4):
                        out = big[:, 16 + 4 * groups[g][5] + c, :]
                        dve.wait_ge(product_out, 4 * (g // 2) + c + 1)
                        if g % 4 == 1:
                            v.tensor_copy(out, sig[:, c, :]).then_inc(summed, 1)
                        else:
                            dve.wait_ge(summed, 4 * (g // 2 - 1) + c + 1)
                            v.tensor_tensor(out, out, sig[:, c, :], ALU.add).then_inc(summed, 1)
            dve.wait_ge(summed, 4 * (len(groups) // 2))


def out_norm_phase(nc, m, d, name, w_dram, src, nk, g_row, b_row):
    PS, xT = m.PS, m.xT
    with ExitStack() as ctx:
        sem = semaphores(nc, ctx, name + "_")
        split = Split(nc, m, ctx, sem, name + "_", 2)
        sq = ctx.enter_context(nc.sbuf_tensor(f"{name}_sq", [P, 2, HALF], F32))
        rstd = ctx.enter_context(nc.sbuf_tensor(f"{name}_rstd", [P, 2, HALF], F32))
        colsum = ctx.enter_context(nc.sbuf_tensor(f"{name}_colsum", [P, S], F32))
        added, summed = sem("added"), sem("summed")
        mean_mm, centered, squared, var_mm = sem("mean_mm"), sem("centered"), sem("squared"), sem("var_mm")
        ln_out, rstd_out, scaled, normed = sem("ln_out"), sem("rstd_out"), sem("scaled"), sem("normed")
        block = ctx.enter_context(nc.Block())
        wv = w_dram.rearrange("(k p) n -> p k n", p=P)
        PAIRS_K = nk // 2

        @block.sync
        def _(sp):
            for g in range(2):
                cols = slice(g * 4 * P, (g + 1) * 4 * P)
                if g == 0:
                    for j in range(2):
                        sp.dma_start(split.raw_slot(j), wv[:, j, cols]).then_inc(split.w_in[j], 16)
                with sp.Fori(1 - g, PAIRS_K) as f:
                    for j in range(2):
                        sp.wait_ge(split.lo_out, 4 * f + (2 * (nk * g + j) - 2))
                        sp.dma_start(split.raw_slot(j), wv[:, bass.ds(2 * f + j, 1), cols].rearrange(
                            "p a n -> p (a n)")).then_inc(split.w_in[j], 16)

        def tile(k):
            return src[:, bass.ds(k, 1), :].rearrange("p a n -> p (a n)")

        @block.tensor
        def _(pe):
            for g in range(2):
                def bank_free(c):
                    if g:
                        pe.wait_ge(added, c + 1)
                split.step(pe, nk * g, 0, True, False, bank_free)
                split.step(pe, nk * g + 1, 1, False, False)
                with pe.Fori(1, PAIRS_K - 1) as f:
                    for j in range(2):
                        split.step(pe, 2 * f + (nk * g + j), j, False, False)
                split.step(pe, nk * g + nk - 2, 0, False, False)
                split.step(pe, nk * g + nk - 1, 1, False, True)
            pe.wait_ge(summed, 3)
            for k in range(3, KT):
                pe.wait_ge(added, max(k + 1, 5))
                for hh in range(2):
                    tk = slice(hh * HALF, (hh + 1) * HALF)
                    last = nc.tensor.matmul(PS[:, hh, :], m.c(C_MEAN), colsum[:, tk] if k == 3 else xT[:, k, tk],
                                            start=k == 3, stop=k == KT - 1)
                    if k == KT - 1:
                        last.then_inc(mean_mm, 1)
            for hh in range(2):
                for k in range(KT):
                    n = KT * hh + k
                    pe.wait_ge(squared, n + 1)
                    nc.tensor.matmul(PS[:, 2 + hh, :], m.c(C_MEAN), sq[:, k % 2, :], start=k == 0,
                                     stop=k == KT - 1).then_inc(var_mm, 1)

        @block.vector
        def _(dve):
            v = nc.vector
            split.lo(dve, tile(0), 0, 0, 0)
            for g in range(2):
                n0 = nk * g
                with dve.Fori(0, PAIRS_K - 1) as f:
                    split.lo(dve, tile(2 * f + 1), 2 * f + (n0 + 1), 1, 1)
                    split.lo(dve, tile(2 * f + 2), 2 * f + (n0 + 2), 0, 0)
                split.lo(dve, tile(nk - 1), n0 + nk - 1, 1, 1)
                if g == 0:
                    split.lo(dve, tile(0), nk, 0, 0)
                else:
                    for k in range(3):
                        v.tensor_tensor(colsum[:, :], colsum[:, :] if k else xT[:, 0, :], xT[:, k + 1, :],
                                        ALU.add).then_inc(summed, 1)
                        dve.wait_ge(summed, k + 1)
                for c in range(4):
                    x = xT[:, 4 * g + c, :].rearrange("p (h n) -> p h n", h=2)
                    split.wait_filled(dve, g, c, nk)
                    v.scalar_tensor_tensor(out=x, in0=x, scalar=ALPHA, in1=PS[:, 2 * c:2 * c + 2, :],
                                           op0=ALU.mult, op1=ALU.add).then_inc(added, 1)
            dve.wait_ge(added, KT)
            for hh in range(2):
                x = xT[:, :, hh * HALF:(hh + 1) * HALF]
                dve.wait_ge(mean_mm, hh + 1)
                for k in range(KT):
                    v.tensor_tensor(x[:, k, :], x[:, k, :], PS[:, hh, :], ALU.subtract).then_inc(centered, 1)
            for hh in range(2):
                dve.wait_ge(rstd_out, hh + 1)
                dve.wait_ge(centered, KT * (hh + 1))
                for k in range(KT):
                    x = xT[:, k, hh * HALF:(hh + 1) * HALF]
                    v.scalar_tensor_tensor(out=x, in0=x, scalar=m.tab2[:, g_row * 8 + k:g_row * 8 + k + 1],
                                           in1=rstd[:, hh, :], op0=ALU.mult, op1=ALU.mult).then_inc(scaled, 1)
                if hh == 0:
                    for k in range(KT):
                        dve.wait_ge(scaled, k + 1)
                        v.tensor_scalar(xT[:, k, 0:HALF], xT[:, k, 0:HALF],
                                        m.tab2[:, b_row * 8 + k:b_row * 8 + k + 1], None, ALU.add)

        @block.scalar
        def _(act):
            a = nc.scalar
            a.preload_act_table_set("natural_log_exp_and_others")
            split.hi(act, tile(0), 0, 0, 0, 0)
            for g in range(2):
                n0 = nk * g
                with act.Fori(0, PAIRS_K - 1) as f:
                    split.hi(act, tile(2 * f + 1), 2 * f + (n0 + 1), 1, 1, f + n0 // 2)
                    split.hi(act, tile(2 * f + 2), 2 * f + (n0 + 2), 0, 0, f + (n0 // 2 + 1))
                split.hi(act, tile(nk - 1), n0 + nk - 1, 1, 1, (n0 + nk) // 2 - 1)
                if g == 0:
                    split.hi(act, tile(0), nk, 0, 0, nk // 2)
            for hh in range(2):
                for k in range(KT):
                    n = KT * hh + k
                    act.wait_ge(centered, n + 1)
                    if n >= 2:
                        act.wait_ge(var_mm, n - 1)
                    a.activation(sq[:, k % 2, :], xT[:, k, hh * HALF:(hh + 1) * HALF],
                                 ACT.Square).then_inc(squared, 1)
                act.wait_ge(var_mm, KT * (hh + 1))
                a.activation(rstd[:, hh, :], PS[:, 2 + hh, :], ACT.Ln, bias=m.eps[:, 0:1]).then_inc(ln_out, 1)
                act.wait_ge(ln_out, hh + 1)
                a.activation(rstd[:, hh, :], rstd[:, hh, :], ACT.Exp, scale=-0.5).then_inc(rstd_out, 1)
            for k in range(KT):
                act.wait_ge(scaled, KT + k + 1)
                x = xT[:, k, HALF:S]
                a.activation(x, x, ACT.Identity, bias=m.tab2[:, b_row * 8 + k:b_row * 8 + k + 1]).then_inc(normed, 1)
            act.wait_ge(normed, KT)


def queries_phase(nc, m, d):
    PS, big, xT, memT = m.PS, m.big, m.xT, m.memT
    MT_ = MEM // P
    with ExitStack() as ctx:
        sem = semaphores(nc, ctx, "q_")
        split = Split(nc, m, ctx, sem, "q_", 4)
        scaled = [sem("scaled_act"), sem("scaled_dve")]
        mem = ctx.enter_context(nc.sbuf_tensor("mem_tok", [P, MT_, D], F32))
        squares = ctx.enter_context(nc.sbuf_tensor("mem_squares", [P, D], F32))
        stat = ctx.enter_context(nc.sbuf_tensor("mem_stat", [P, 3, MT_], F32))
        total, ssq, rstd = (stat[:, j, :] for j in range(3))
        mem_in, mem_summed, mem_mean = sem("mem_in"), sem("mem_summed"), sem("mem_mean")
        mem_centered, mem_squared = sem("mem_centered"), sem("mem_squared")
        mem_ln, mem_rstd, mem_scaled = sem("mem_ln"), sem("mem_rstd"), sem("mem_scaled")
        mem_turned, mem_out = sem("mem_turned"), sem("mem_out")
        block = ctx.enter_context(nc.Block())
        wv = d["w_cq"][0].rearrange("(k p) n -> p k n", p=P)
        STEPS = 2 * KT

        @block.sync
        def _(sp):
            for n in range(STEPS):
                g, k = n // KT, n % KT
                if n >= 4:
                    sp.wait_ge(split.lo_out, 2 * n - 6)
                sp.dma_start(split.raw_slot(n % 4), wv[:, k, 4 * P * g:4 * P * (g + 1)]).then_inc(split.w_in[n % 4], 16)
                if n == 1:
                    sp.dma_start(mem[:, :, :], d["mem"][0].rearrange("(t p) n -> p t n", p=P)).then_inc(mem_in, 16)

        @block.tensor
        def _(pe):
            for g in range(2):
                for k in range(KT):
                    def bank_free(c):
                        if g:
                            pe.wait_ge(scaled[c % 2], c // 2 + 1)
                    split.step(pe, KT * g + k, k % 2, k == 0, k == KT - 1, bank_free)
            pe.wait_ge(mem_scaled, MT_)
            for b in range(4):
                if b % 2 == 0:
                    pe.wait_ge(scaled[b // 2], 3)
                for k in (2 * b, 2 * b + 1):
                    for t in range(MT_):
                        last = nc.tensor.transpose(PS[:, b, k % 2 * MEM + t * P:k % 2 * MEM + (t + 1) * P],
                                                   mem[:, t, k * P:(k + 1) * P], m.c(C_IDENT))
                last.then_inc(mem_turned, 1)

        def scale_out(eng, which, scale):
            for c in range(which, 4, 2):
                split.wait_filled(eng, g_of[which], c)
                scale(big[:, 8 + 4 * g_of[which] + c, :].rearrange("p (h n) -> p h n", h=2),
                      PS[:, 2 * c:2 * c + 2, :]).then_inc(scaled[which], 1)
            g_of[which] += 1

        g_of = [0, 0]

        @block.scalar
        def _(act):
            for n in range(STEPS + 1):
                if n < STEPS:
                    split.hi(act, xT[:, n % KT, :], n, n % 2, n % 4, n // 4)
                if n in (5, 6):
                    t = n - 5
                    act.wait_ge(mem_centered, t + 1)
                    if t:
                        act.wait_ge(mem_squared, 1)
                    nc.scalar.activation(squares[:, :], mem[:, t, :], ACT.Square,
                                         accum_out=ssq[:, t:t + 1]).then_inc(mem_squared, 1)
                if n == 7:
                    act.wait_ge(mem_squared, MT_)
                    nc.scalar.activation(rstd, ssq, ACT.Ln, bias=m.eps[:, 0:1], scale=1.0 / D).then_inc(mem_ln, 1)
                    act.wait_ge(mem_ln, 1)
                    nc.scalar.activation(rstd, rstd, ACT.Exp, scale=-0.5).then_inc(mem_rstd, 1)
                if n and n % KT == 0:
                    scale_out(act, 0, lambda out, x: nc.scalar.mul(out, x, CA_HD ** -0.5))
            for k in range(KT):
                act.wait_ge(mem_turned, k // 2 + 1)
                nc.scalar.activation(memT[:, k, :], PS[:, k // 2, k % 2 * MEM:(k % 2 + 1) * MEM], ACT.Identity,
                                     scale=m.tab2[:, 48 + k:49 + k],
                                     bias=m.tab2[:, 56 + k:57 + k]).then_inc(mem_out, 1)
            act.wait_ge(mem_out, KT)

        @block.vector
        def _(dve):
            v = nc.vector
            for n in range(STEPS + 1):
                if n < STEPS:
                    split.lo(dve, xT[:, n % KT, :], n, n % 2, n % 4)
                if n == 2:
                    dve.wait_ge(mem_in, 16)
                    v.tensor_reduce(total, mem[:, :, :], AX, ALU.add).then_inc(mem_summed, 1)
                if n == 3:
                    dve.wait_ge(mem_summed, 1)
                    v.tensor_scalar(total, total, -1.0 / D, None, ALU.mult).then_inc(mem_mean, 1)
                    dve.wait_ge(mem_mean, 1)
                if n in (3, 4):
                    t = n - 3
                    v.tensor_scalar(mem[:, t, :], mem[:, t, :], total[:, t:t + 1], None,
                                    ALU.add).then_inc(mem_centered, 1)
                if n in (9, 10):
                    t = n - 9
                    dve.wait_ge(mem_rstd, 1)
                    dve.wait_ge(mem_centered, MT_)
                    v.tensor_scalar(mem[:, t, :], mem[:, t, :], rstd[:, t:t + 1], None,
                                    ALU.mult).then_inc(mem_scaled, 1)
                if n and n % KT == 0:
                    scale_out(dve, 1, lambda out, x: nc.vector.tensor_scalar(out, x, CA_HD ** -0.5, None, ALU.mult))


def cross_phase(nc, m, d):
    PS, big, xT, memT = m.PS, m.big, m.xT, m.memT
    HT = CA_HD // P
    MT_ = MEM // P
    with ExitStack() as ctx:
        sem = semaphores(nc, ctx, "x_")

        W = [m.wslot[:, 2 * j:2 * j + 2, :, :].rearrange("p a k n -> p (a k n)").rearrange(
            "p (k n) -> p k n", n=CA_HD) for j in range(2)]
        queries = big[:, 8:16, :]
        ck = big[:, 16, 0:HT * MEM].rearrange("p (t n) -> p t n", n=MEM)
        cv = big[:, 16, HT * MEM:2 * HT * MEM].rearrange("p (t n) -> p t n", n=CA_HD)
        prob = big[:, 17:19, :].rearrange("p a n -> p (a n)").rearrange("p (t n) -> p t n", n=MEM)
        probT = big[:, 19:21, :]
        stat = ctx.enter_context(nc.sbuf_tensor("x_stat", [P, 3, NT], F32))
        cq = ctx.enter_context(nc.sbuf_tensor("x_queries", [P, HT, S], F32))
        w_in = [sem(f"w_in{j}") for j in range(2)]
        k_mm, k_out, v_mm, v_out = sem("k_mm"), sem("k_out"), sem("v_mm"), sem("v_out")
        q_out = sem("q_out")
        s_mm, maxed, exped, normed = sem("s_mm"), sem("maxed"), sem("exped"), sem("normed")
        rec = sem("reciprocal")
        p_turned, p_out = sem("p_turned"), sem("p_out")
        o_mm, o_out = sem("o_mm"), sem("o_out")
        block = ctx.enter_context(nc.Block())
        wv = tile_cols(d["w_ckv"][0])

        @block.sync
        def _(sp):
            for j in range(2):
                sp.dma_start(W[j], wv[:, :, j * D:j * D + CA_HD]).then_inc(w_in[j], 16)
            with sp.Fori(1, CA_HEADS) as h:
                for j, sm in enumerate((k_mm, v_mm)):
                    sp.wait_ge(sm, h)
                    sp.dma_start(W[j], wv[:, :, bass.ds(h * CA_HD + j * D, CA_HD)]).then_inc(w_in[j], 16)

        def tensor_turn(pe, h, more):
            mm = nc.tensor.matmul
            pe.wait_ge(k_out, h + 1)
            pe.wait_ge(q_out, h + 1)
            for t in range(NT):
                bank = (6, 7, 4, 5)[t // 2]
                if t == 4:
                    pe.wait_ge(o_out, 4 * h)
                for ft in range(HT):
                    last = mm(PS[:, bank, t % 2 * MEM:(t % 2 + 1) * MEM], cq[:, ft, t * P:(t + 1) * P],
                              ck[:, ft, :], start=ft == 0, stop=ft == HT - 1)
                last.then_inc(s_mm, 1)
            if more:
                keys_values(pe, h + 1)
            pe.wait_ge(exped, NT * h + NT)
            for half in range(2):
                pe.wait_ge(normed, NT * h + 4 * half + 4)
                for mt in range(MT_):
                    for t in range(4):
                        last = nc.tensor.transpose(PS[:, 4 + 2 * half + mt, t * P:(t + 1) * P],
                                                   prob[:, 4 * half + t, mt * P:(mt + 1) * P], m.c(C_IDENT))
                    last.then_inc(p_turned, 1)
            pe.wait_ge(p_out, 4 * h + 4)
            pe.wait_ge(o_out, 4 * h)
            pe.wait_ge(v_out, h + 1)
            for n in range(4):
                ft, half = n // 2, n % 2
                for mt in range(MT_):
                    last = mm(PS[:, 2 + n, :], cv[:, mt, ft * P:(ft + 1) * P],
                              probT[:, mt, half * HALF:(half + 1) * HALF], start=mt == 0, stop=mt == MT_ - 1)
                last.then_inc(o_mm, 1)

        def keys_values(pe, h):
            mm = nc.tensor.matmul
            pe.wait_ge(w_in[0], 16 * h + 16)
            pe.wait_ge(k_out, h)
            for ft in range(HT):
                for k in range(KT):
                    last = mm(PS[:, 0, ft * MEM:(ft + 1) * MEM], W[0][:, k, ft * P:(ft + 1) * P],
                              memT[:, k, :], start=k == 0, stop=k == KT - 1)
            last.then_inc(k_mm, 1)
            pe.wait_ge(w_in[1], 16 * h + 16)
            pe.wait_ge(v_out, h)
            for mt in range(MT_):
                for k in range(KT):
                    last = mm(PS[:, 1, mt * CA_HD:(mt + 1) * CA_HD], memT[:, k, mt * P:(mt + 1) * P],
                              W[1][:, k, :], start=k == 0, stop=k == KT - 1)
            last.then_inc(v_mm, 1)

        @block.tensor
        def _(pe):
            keys_values(pe, 0)
            with pe.Fori(0, CA_HEADS - 1) as h:
                tensor_turn(pe, h, True)
            tensor_turn(pe, CA_HEADS - 1, False)

        def take_queries(act, h):
            act.wait_ge(s_mm, NT * h)
            nc.scalar.copy(cq[:, :, :], queries[:, bass.ds(HT * h, HT), :]).then_inc(q_out, 1)

        def scalar_turn(act, h, more):
            a = nc.scalar
            for t in range(NT):
                bank = (6, 7, 4, 5)[t // 2]
                act.wait_ge(maxed, NT // 2 * h + t // 2 + 1)
                act.wait_ge(p_turned, 4 * h)
                a.activation(prob[:, t, :], PS[:, bank, t % 2 * MEM:(t % 2 + 1) * MEM], ACT.Exp,
                             bias=stat[:, 0, t:t + 1], accum_out=stat[:, 1, t:t + 1]).then_inc(exped, 1)
            for n in range(4):
                half, mt = n // 2, n % 2
                act.wait_ge(p_turned, 4 * h + n + 1)
                act.wait_ge(o_mm, 4 * h)
                a.copy(probT[:, mt, half * HALF:(half + 1) * HALF], PS[:, 4 + n, :]).then_inc(p_out, 1)
            if more:
                take_queries(act, h + 1)

        @block.scalar
        def _(act):
            nc.scalar.preload_act_table_set("natural_log_exp_and_others")
            take_queries(act, 0)
            with act.Fori(0, CA_HEADS - 1) as h:
                scalar_turn(act, h, True)
            scalar_turn(act, CA_HEADS - 1, False)

        def take_keys(dve, h):
            dve.wait_ge(k_mm, h + 1)
            dve.wait_ge(s_mm, NT * h)
            nc.vector.tensor_copy(ck.rearrange("p t n -> p (t n)"), PS[:, 0, :]).then_inc(k_out, 1)

        def vector_turn(dve, h, more):
            v = nc.vector
            dve.wait_ge(v_mm, h + 1)
            dve.wait_ge(o_mm, 4 * h)
            v.tensor_copy(cv.rearrange("p t n -> p (t n)"), PS[:, 1, :]).then_inc(v_out, 1)
            for b in range(NT // 2):
                dve.wait_ge(s_mm, NT * h + 2 * b + 2)
                dve.wait_ge(exped, NT * h)
                v.tensor_reduce(stat[:, 0, 2 * b:2 * b + 2],
                                PS[:, (6, 7, 4, 5)[b], :].rearrange("p (t n) -> p t n", n=MEM), AX, ALU.max,
                                negate=True).then_inc(maxed, 1)
            for t in range(NT):
                dve.wait_ge(exped, NT * h + t + 1)
                v.reciprocal(stat[:, 2, t:t + 1], stat[:, 1, t:t + 1]).then_inc(rec, 1)
                dve.wait_ge(rec, NT * h + t + 1)
                v.tensor_scalar(prob[:, t, :], prob[:, t, :], stat[:, 2, t:t + 1], None,
                                ALU.mult).then_inc(normed, 1)
            if more:
                take_keys(dve, h + 1)
            for n in range(4):
                ft, half = n // 2, n % 2
                dve.wait_ge(o_mm, 4 * h + n + 1)
                v.tensor_copy(big[:, bass.ds(HT * h + ft, 1), half * HALF:(half + 1) * HALF],
                              PS[:, 2 + n:3 + n, :]).then_inc(o_out, 1)

        @block.vector
        def _(dve):
            take_keys(dve, 0)
            with dve.Fori(0, CA_HEADS - 1) as h:
                vector_turn(dve, h, True)
            vector_turn(dve, CA_HEADS - 1, False)


def hidden_phase(nc, m, d):
    PS, big, xT = m.PS, m.big, m.xT
    GROUPS = FT // 2
    with ExitStack() as ctx:
        sem = semaphores(nc, ctx, "h_")
        split = Split(nc, m, ctx, sem, "hidden_", 4)
        act_buf = ctx.enter_context(nc.sbuf_tensor("silu", [P, 2, S], F32))
        silu_out, up_used = sem("silu_out"), sem("up_used")
        block = ctx.enter_context(nc.Block())
        wv = d["w_ffn_in"][0].rearrange("(k p) (u n) -> p k u n", p=P, u=2)

        @block.sync
        def _(sp):
            def load(g, k):
                c0 = g * (2 * P)
                cols = slice(c0, c0 + 2 * P) if isinstance(g, int) else bass.ds(c0, 2 * P)
                sp.dma_start(split.raw_slot(k % 4).rearrange("p (u n) -> p u n", u=2),
                             wv[:, k, :, cols]).then_inc(split.w_in[k % 4], 16)
            for k in range(4):
                load(0, k)
            for k in range(4, KT):
                sp.wait_ge(split.lo_out, 2 * k - 6)
                load(0, k)
            with sp.Fori(1, GROUPS) as g:
                for k in range(KT):
                    sp.wait_ge(split.lo_out, 2 * KT * g + (2 * k - 6))
                    load(g, k)

        @block.tensor
        def _(pe):
            with pe.Fori(0, GROUPS) as g:
                for k in range(KT):
                    def bank_free(c):
                        if c == 0:
                            pe.wait_ge(silu_out, 2 * g)
                        if c == 2:
                            pe.wait_ge(up_used, 2 * g)
                    split.step(pe, KT * g + k, k % 2, k == 0, k == KT - 1, bank_free)

        def for_groups(eng, halve, evacuate):
            halve(0, 0)
            with eng.Fori(0, GROUPS - 1) as g:
                for k in range(1, KT + 1):
                    halve(g, k)
                evacuate(g)
            for k in range(1, KT):
                halve(GROUPS - 1, k)
            evacuate(GROUPS - 1)

        @block.scalar
        def _(act):
            def halve(g, k):
                split.hi(act, xT[:, k % KT, :], KT * g + k, k % 2, k % 4, 2 * g + k // 4)

            def silu(g):
                for c in range(2):
                    split.wait_filled(act, g, c)
                    act.wait_ge(up_used, 2 * g + c)
                    nc.scalar.activation(act_buf[:, c, :].rearrange("p (h n) -> p h n", h=2),
                                         PS[:, 2 * c:2 * c + 2, :], ACT.Silu).then_inc(silu_out, 1)
            for_groups(act, halve, silu)

        @block.vector
        def _(dve):
            def halve(g, k):
                split.lo(dve, xT[:, k % KT, :], KT * g + k, k % 2, k % 4)

            def times_up(g):
                for c in range(2):
                    split.wait_filled(dve, g, c + 2)
                    dve.wait_ge(silu_out, 2 * g + c + 1)
                    nc.vector.tensor_tensor(big[:, bass.ds(2 * g + c, 1), :].rearrange("p a (h n) -> p (a h) n", h=2),
                                            act_buf[:, c, :].rearrange("p (h n) -> p h n", h=2),
                                            PS[:, 2 * c + 4:2 * c + 6, :], ALU.mult).then_inc(up_used, 1)
            for_groups(dve, halve, times_up)


def store_phase(nc, m, d):
    PS = m.PS
    with ExitStack() as ctx:
        sem = semaphores(nc, ctx, "o_")

        rows = m.big[:, 0:4, :]
        turned = sem("turned")
        copied = [sem("copied_dve"), sem("copied_act")]
        stored = [sem(f"stored{j}") for j in range(4)]
        block = ctx.enter_context(nc.Block())

        @block.tensor
        def _(pe):
            for t in range(NT):
                for half in range(2):
                    n = 2 * t + half
                    if n >= 8:
                        pe.wait_ge(copied[half], (n - 8) // 2 + 1)
                    for k in range(4):
                        last = nc.tensor.transpose(PS[:, n % 8, k * P:(k + 1) * P],
                                                   m.xT[:, 4 * half + k, t * P:(t + 1) * P], m.c(C_IDENT))
                    last.then_inc(turned, 1)

        def copy_out(eng, copy, half):
            for t in range(NT):
                n = 2 * t + half
                eng.wait_ge(turned, n + 1)
                if t >= 4:
                    eng.wait_ge(stored[t % 4], 16)
                copy(rows[:, t % 4, half * HALF:(half + 1) * HALF], PS[:, n % 8, :]).then_inc(copied[half], 1)

        @block.vector
        def _(dve):
            copy_out(dve, nc.vector.tensor_copy, 0)

        @block.scalar
        def _(act):
            copy_out(act, nc.scalar.copy, 1)

        @block.sync
        def _(sp):
            for t in range(NT):
                sp.wait_ge(copied[0], t + 1)
                sp.wait_ge(copied[1], t + 1)
                sp.dma_start(d["out"][0, t * P:(t + 1) * P, :], rows[:, t % 4, :]).then_inc(stored[t % 4], 16)
            for j in range(4):
                sp.wait_ge(stored[j], 32)


def layer(nc, d):
    with ExitStack() as ctx:
        m = Memory(nc, ctx)
        big = m.big
        setup_phase(nc, m, d)
        with ExitStack() as mixers:
            m.take_raw(nc, mixers)
            attention_phase(nc, m, d)
            rwkv_phase(nc, m, d)
        merge_phase(nc, m, d)
        out_norm_phase(nc, m, d, "mix", d["w_mix_out"][0], big[:, 16:24, :], KT, 0, 1)
        queries_phase(nc, m, d)
        cross_phase(nc, m, d)
        out_norm_phase(nc, m, d, "co", d["w_co"][0], big[:, 0:8, :], KT, 2, 3)
        hidden_phase(nc, m, d)
        out_norm_phase(nc, m, d, "ffn", d["w_ffn_out"][0], big[:, 0:FT, :], FT, 4, 5)
        store_phase(nc, m, d)


_INS = ['x', 'mem', 'rel_bias', 'w_in', 'shift_mu', 'lambda_q1', 'lambda_k1', 'lambda_q2', 'lambda_k2',
        'da_subln_g', 'w_da_proj', 'rw_w0', 'rw_w2', 'rw_a0', 'rw_a2', 'rw_g2', 'rw_k_k', 'rw_k_a', 'rw_r_k',
        'rw_lnx_g', 'rw_lnx_b', 'w_rw_proj', 'w_mix_out', 'ln1_g', 'ln1_b', 'mem_ln_g', 'mem_ln_b', 'w_cq',
        'w_ckv', 'w_co', 'ln2_g', 'ln2_b', 'w_ffn_in', 'w_ffn_out', 'ln3_g', 'ln3_b']


def kernel(**inputs):
    import numpy as _np
    import concourse.bacc as _bacc
    from concourse import mybir as _mybir
    from concourse.bass_utils import run_bass_kernel_spmd as _run

    nc = _bacc.Bacc("TRN2", target_bir_lowering=False, num_devices=1)
    arrays, d = {}, {}
    const, pick, future = shape_constants()
    for name, a in [(n, inputs[n]) for n in _INS] + [("const", const), ("pick", pick), ("future", future)]:
        a = _np.ascontiguousarray(a)
        arrays[f"in_{name}_dram"] = a
        d[name] = nc.dram_tensor(f"in_{name}_dram", a.shape, _mybir.dt.from_np(a.dtype), kind="ExternalInput").ap()
    d["out"] = nc.dram_tensor("out_0_dram", (1, S, D), F32, kind="ExternalOutput").ap()
    layer(nc, d)
    r = _run(nc, [arrays], core_ids=[0])
    return r.results[0]["out_0_dram"]
```
